# Optimizing a Trainium2 kernel written in Bass

```python
import math
import jax, jax.numpy as jnp
from jax import lax
import numpy as np

D_MODEL = 1024
BATCH = 1
SEQ = 512
DEPTH = 1

HEAD_DIM = 64
N_BRANCHES = 4
BRANCH_WIDTH = D_MODEL // 4

A_HEADS = BRANCH_WIDTH // HEAD_DIM
A_PATTERNS = ((128, 1), (512, 4), (2048, 16))
A_BLOCK = 128
B_HEADS = BRANCH_WIDTH // HEAD_DIM
B_LATENT = D_MODEL // 16
IDX_HEADS = 8
IDX_DIM = 32
TOPK_MAX = 256
TOPK_DIV = 4
Q_BLOCK = 128
C_HEADS = 4
C_KEY_DIM = 32
C_VAL_DIM = BRANCH_WIDTH // C_HEADS
C_GATE_RANK = 16
C_GATE_TAU = 16.0
C_CHUNK = 64
D_HEADS = 4
D_HEAD_SIZE = BRANCH_WIDTH // D_HEADS
D_DECAY_RANK = 16
D_ICLR_RANK = 16
D_GATE_RANK = 32
D_GN_EPS = 64e-5
D_IN_WIDTH = 3 * BRANCH_WIDTH + D_DECAY_RANK + D_ICLR_RANK + D_GATE_RANK
RPB_BUCKETS = 32
RPB_MAX_DIST = 2048
RPB_HEADS = A_HEADS + B_HEADS
MOE_GROUPS = 4
MOE_PER_GROUP = 8
MOE_EXPERTS = MOE_GROUPS * MOE_PER_GROUP
MOE_TOPK = 2
MOE_HIDDEN = 256
DN_ALPHA = (2 * DEPTH) ** 0.25
DN_BETA = (8 * DEPTH) ** -0.25
LN_EPS = 1e-5

IN_SPLITS = (
    ("a_q", A_HEADS * HEAD_DIM), ("a_k", A_HEADS * HEAD_DIM), ("a_v", A_HEADS * HEAD_DIM),
    ("b_q", B_HEADS * B_LATENT), ("b_ckv", B_LATENT), ("b_iq", IDX_HEADS * IDX_DIM),
    ("b_ik", IDX_DIM), ("b_iw", IDX_HEADS),
    ("c_q", C_HEADS * C_KEY_DIM), ("c_k", C_HEADS * C_KEY_DIM), ("c_v", C_HEADS * C_VAL_DIM),
    ("c_a", C_GATE_RANK), ("c_g", BRANCH_WIDTH),
    ("d", D_IN_WIDTH),
    ("gate", N_BRANCHES * D_MODEL),
)
IN_WIDTH = sum(w for _, w in IN_SPLITS)


def _split_in(h):
    out = {}
    off = 0
    for name, w in IN_SPLITS:
        out[name] = h[..., off:off + w]
        off += w
    return out

def _layer_norm(x, g, b):
    xf = x.astype(jnp.float32)
    mu = jnp.mean(xf, -1, keepdims=True)
    var = jnp.mean(jnp.square(xf - mu), -1, keepdims=True)
    return ((xf - mu) * lax.rsqrt(var + LN_EPS) * g + b).astype(x.dtype)

def _rms_norm(x, g, eps=1e-6):
    xf = x.astype(jnp.float32)
    return (xf * lax.rsqrt(jnp.mean(xf * xf, -1, keepdims=True) + eps) * g).astype(x.dtype)

def _t5_bucket(dist):
    exact = RPB_BUCKETS // 2
    d = jnp.maximum(dist, 0)
    df = jnp.maximum(d, 1).astype(jnp.float32)
    large = exact + (jnp.log(df / exact) / math.log(RPB_MAX_DIST / exact)
                     * (RPB_BUCKETS - exact)).astype(jnp.int32)
    large = jnp.minimum(large, RPB_BUCKETS - 1)
    return jnp.where(d < exact, d, large)

def _dilated_pattern(q, k, v, bias_tab, window, dilation):
    bsz, seq, nh, dh = q.shape
    lr = seq // dilation
    span = window // dilation
    nb = -(-lr // A_BLOCK)
    lp = nb * A_BLOCK
    bd = bsz * dilation

    def regroup(z):
        z = z.reshape(bsz, lr, dilation, nh, dh).transpose(0, 2, 1, 3, 4)
        return z.reshape(bd, lr, nh, dh)

    qr, kr, vr = regroup(q), regroup(k), regroup(v)
    qb = jnp.pad(qr, ((0, 0), (0, lp - lr), (0, 0), (0, 0))).reshape(bd, nb, A_BLOCK, nh, dh)

    def band(z):
        zp = jnp.pad(z, ((0, 0), (A_BLOCK, lp - lr), (0, 0), (0, 0)))
        prev = zp[:, :lp].reshape(bd, nb, A_BLOCK, nh, dh)
        cur = zp[:, A_BLOCK:].reshape(bd, nb, A_BLOCK, nh, dh)
        return jnp.concatenate([prev, cur], axis=2)

    kb, vb = band(kr), band(vr)
    qi = jnp.arange(A_BLOCK)[:, None]
    kj = jnp.arange(2 * A_BLOCK)[None, :]
    rdist = qi + A_BLOCK - kj
    in_band = (rdist >= 0) & (rdist <= span)
    bias = jnp.transpose(bias_tab[_t5_bucket(rdist * dilation)], (2, 0, 1))
    kpos = jnp.arange(nb)[:, None] * A_BLOCK - A_BLOCK + kj
    mask = in_band[None] & (kpos >= 0)[:, None, :]

    s = jnp.einsum('bnqhd,bnkhd->bnhqk', qb, kb).astype(jnp.float32) * dh ** -0.5 + bias
    s = jnp.where(mask[None, :, None], s, -jnp.inf)
    m = jnp.max(s, -1, keepdims=True)
    p = jnp.exp(s - m)
    den = jnp.sum(p, -1)
    o = jnp.einsum('bnhqk,bnkhd->bnqhd', p, vb.astype(jnp.float32))
    o = o / jnp.swapaxes(den, 2, 3)[..., None]
    lse = jnp.swapaxes(m[..., 0] + jnp.log(den), 2, 3)
    o = o.reshape(bd, lp, nh, dh)
    lse = lse.reshape(bd, lp, nh)

    def ungroup(z):
        z = z[:, :lr].reshape((bsz, dilation, lr) + z.shape[2:])
        z = jnp.moveaxis(z, 1, 2)
        return z.reshape((bsz, seq) + z.shape[3:])

    return ungroup(o), ungroup(lse)

def _mixer_a(q, k, v, bias_tab):
    bsz, seq, _ = q.shape
    shp = (bsz, seq, A_HEADS, HEAD_DIM)
    q, k, v = q.reshape(shp), k.reshape(shp), v.reshape(shp)
    outs, lses = [], []
    for window, dilation in A_PATTERNS:
        o, lse = _dilated_pattern(q, k, v, bias_tab, window, dilation)
        outs.append(o)
        lses.append(lse)
    wts = jax.nn.softmax(jnp.stack(lses), axis=0)
    o = jnp.sum(jnp.stack(outs) * wts[..., None], axis=0)
    return o.reshape(bsz, seq, A_HEADS * HEAD_DIM).astype(q.dtype)

def _mixer_b(q, ckv, iq, ik, iw, kv_gain, w_uv, bias_tab):
    bsz, seq, _ = q.shape
    keep = min(TOPK_MAX, seq // TOPK_DIV)
    nblk = seq // Q_BLOCK
    q = q.reshape(bsz, seq, B_HEADS, B_LATENT)
    ckv = _rms_norm(ckv, kv_gain)
    iq = iq.reshape(bsz, seq, IDX_HEADS, IDX_DIM)

    def to_blocks(z):
        return jnp.moveaxis(z.reshape((bsz, nblk, Q_BLOCK) + z.shape[2:]), 1, 0)

    def one_block(args):
        bi, qb, iqb, iwb = args
        tpos = bi * Q_BLOCK + jnp.arange(Q_BLOCK)
        rel = jax.nn.relu(jnp.einsum('bqhd,bsd->bqhs', iqb, ik).astype(jnp.float32) * IDX_DIM ** -0.5)
        score = jnp.einsum('bqhs,bqh->bqs', rel, iwb.astype(jnp.float32)) * IDX_HEADS ** -0.5
        admissible = jnp.arange(seq)[None, :] <= tpos[:, None]
        score = jnp.where(admissible[None], score, -jnp.inf)
        _, idx = lax.top_k(score, keep)
        sel = jax.vmap(lambda c, i: c[i])(ckv, idx)
        logits = jnp.einsum('bqhc,bqkc->bqhk', qb, sel).astype(jnp.float32) * B_LATENT ** -0.5
        dist = tpos[None, :, None] - idx
        bias = jnp.moveaxis(bias_tab[_t5_bucket(dist)], -1, 2)
        logits = jnp.where((dist >= 0)[:, :, None, :], logits + bias, -jnp.inf)
        p = jax.nn.softmax(logits, axis=-1)
        return jnp.einsum('bqhk,bqkc->bqhc', p.astype(sel.dtype), sel)

    ob = lax.map(one_block, (jnp.arange(nblk), to_blocks(q), to_blocks(iq), to_blocks(iw)))
    o = jnp.moveaxis(ob, 0, 1).reshape(bsz, seq, B_HEADS, B_LATENT)
    o = jnp.einsum('bshc,hcd->bshd', o, w_uv)
    return o.reshape(bsz, seq, B_HEADS * HEAD_DIM).astype(q.dtype)

def _mixer_c(q, k, v, a_low, og, a_up, a_bias, norm_gain):
    f32 = jnp.float32
    bsz, seq, _ = q.shape
    nc = seq // C_CHUNK
    log_a = jax.nn.log_sigmoid((a_low @ a_up + a_bias).astype(f32)) / C_GATE_TAU

    def chunks(z, dim):
        return z.astype(f32).reshape(bsz, nc, C_CHUNK, C_HEADS, dim)

    qc = chunks(q, C_KEY_DIM) * C_KEY_DIM ** -0.5
    kc = chunks(k, C_KEY_DIM)
    vc = chunks(v, C_VAL_DIM)
    cum = jnp.cumsum(chunks(log_a, C_KEY_DIM), axis=2)
    last = cum[:, :, -1]
    q_dec = qc * jnp.exp(cum)
    k_inv = kc * jnp.exp(-cum)
    causal = jnp.tril(jnp.ones((C_CHUNK, C_CHUNK), bool))
    att = jnp.where(causal, jnp.einsum('bnihd,bnjhd->bnhij', q_dec, k_inv), 0.0)
    o_intra = jnp.einsum('bnhij,bnjhv->bnihv', att, vc)
    upd = jnp.einsum('bnjhd,bnjhv->bnhdv', kc * jnp.exp(last[:, :, None] - cum), vc)
    dec = jnp.exp(last)

    def step(state, inp):
        d, u = inp
        return d[..., None] * state + u, state

    init = jnp.zeros((bsz, C_HEADS, C_KEY_DIM, C_VAL_DIM), f32)
    _, before = lax.scan(step, init, (jnp.moveaxis(dec, 1, 0), jnp.moveaxis(upd, 1, 0)))
    before = jnp.moveaxis(before, 0, 1)
    o = o_intra + jnp.einsum('bnihd,bnhdv->bnihv', q_dec, before)
    o = o.reshape(bsz, seq, C_HEADS, C_VAL_DIM)
    o = o * lax.rsqrt(jnp.mean(o * o, -1, keepdims=True) + 1e-6)
    o = o.reshape(bsz, seq, BRANCH_WIDTH) * norm_gain
    return (jax.nn.silu(og.astype(f32)) * o).astype(q.dtype)

def _token_shift(z, mu):
    prev = jnp.pad(z, ((0, 0), (1, 0), (0, 0)))[:, :-1]
    return z + (prev - z) * mu

def _mixer_d(seg, mu, w0, w2, a0, a2, g2, k_k, k_a, r_k, gn_w, gn_b):
    f32 = jnp.float32
    out_dtype = seg.dtype
    bsz, seq, _ = seg.shape
    bw = BRANCH_WIDTH
    seg = _token_shift(seg, mu).astype(f32)
    r, k, v = seg[..., :bw], seg[..., bw:2 * bw], seg[..., 2 * bw:3 * bw]
    o1 = 3 * bw
    o2 = o1 + D_DECAY_RANK
    o3 = o2 + D_ICLR_RANK
    wl, al, gl = seg[..., o1:o2], seg[..., o2:o3], seg[..., o3:o3 + D_GATE_RANK]
    w_raw = -jax.nn.softplus(-(w0 + jnp.tanh(wl) @ w2)) - 0.5
    w = jnp.exp(-jnp.exp(w_raw))
    a = jax.nn.sigmoid(a0 + al @ a2)
    g = jax.nn.sigmoid(gl) @ g2

    def heads(z):
        return z.astype(f32).reshape(bsz, seq, D_HEADS, D_HEAD_SIZE)

    kk = heads(k * k_k)
    kk = kk / jnp.maximum(jnp.sqrt(jnp.sum(kk * kk, -1, keepdims=True)), 1e-12)
    k = k * (1.0 + (a - 1.0) * k_a)
    rh, kh, vh, wh, ah = heads(r), heads(k), heads(v), heads(w), heads(a)
    a_vec = -kk
    b_vec = kk * ah

    def step(state, inp):
        rt, wt, kt, vt, at, bt = inp
        sa = jnp.einsum('bhvk,bhk->bhv', state, at)
        state = (state * wt[:, :, None, :] + sa[..., None] * bt[:, :, None, :]
                 + vt[..., None] * kt[:, :, None, :])
        return state, jnp.einsum('bhvk,bhk->bhv', state, rt)

    init = jnp.zeros((bsz, D_HEADS, D_HEAD_SIZE, D_HEAD_SIZE), f32)
    xs = tuple(jnp.moveaxis(z, 1, 0) for z in (rh, wh, kh, vh, a_vec, b_vec))
    _, y = lax.scan(step, init, xs)
    y = jnp.moveaxis(y, 0, 1)
    mu_y = jnp.mean(y, -1, keepdims=True)
    var_y = jnp.mean(jnp.square(y - mu_y), -1, keepdims=True)
    y = ((y - mu_y) * lax.rsqrt(var_y + D_GN_EPS)).reshape(bsz, seq, bw) * gn_w + gn_b
    bonus = jnp.sum(rh * kh * r_k.reshape(D_HEADS, D_HEAD_SIZE), -1, keepdims=True) * vh
    y = (y + bonus.reshape(bsz, seq, bw)) * g
    return y.astype(out_dtype)

def _moe(x, wr_g, br_g, wr_e, br_e, w_gate, w_up, w_down):
    f32 = jnp.float32

    def one_seq(xs):
        lg = (xs @ wr_g).astype(f32) + br_g
        pg = jax.nn.softmax(lg, axis=-1)
        ptop, gsel = lax.top_k(pg, 1)
        le = ((xs @ wr_e).astype(f32) + br_e).reshape(-1, MOE_GROUPS, MOE_PER_GROUP)
        le = jnp.take_along_axis(le, gsel[:, :, None], axis=1)[:, 0]
        lv, esel = lax.top_k(le, MOE_TOPK)
        we = jax.nn.softmax(lv, axis=-1) * ptop
        local = jnp.einsum('sk,ske->se', we, jax.nn.one_hot(esel, MOE_PER_GROUP, dtype=f32))
        gate = (jax.nn.one_hot(gsel[:, 0], MOE_GROUPS, dtype=f32)[:, :, None]
                * local[:, None, :]).reshape(-1, MOE_EXPERTS)
        hg = jnp.einsum('sd,edh->seh', xs, w_gate)
        hu = jnp.einsum('sd,edh->seh', xs, w_up)
        h = jax.nn.silu(hg) * hu * gate[..., None].astype(xs.dtype)
        return jnp.einsum('seh,ehd->sd', h, w_down)

    return lax.map(one_seq, x).astype(x.dtype)

def first_inputs(seed: int = 0) -> dict:
    key = jax.random.key(seed)
    ks = jax.random.split(key, 32)
    f32 = jnp.float32

    def nrm(k, shape, scale):
        return jax.random.normal(k, shape, f32) * scale

    L = DEPTH
    bw = BRANCH_WIDTH
    return {
        "x": nrm(ks[0], (BATCH, SEQ, D_MODEL), 1.0),
        "rpb_table": nrm(ks[1], (RPB_BUCKETS, RPB_HEADS), 0.5),
        "w_in": nrm(ks[2], (L, D_MODEL, IN_WIDTH), D_MODEL ** -0.5),
        "b_kv_gain": 1.0 + nrm(ks[3], (L, B_LATENT), 0.05),
        "b_w_uv": nrm(ks[4], (L, B_HEADS, B_LATENT, HEAD_DIM), B_LATENT ** -0.5),
        "c_a_up": nrm(ks[5], (L, C_GATE_RANK, C_HEADS * C_KEY_DIM), C_GATE_RANK ** -0.5),
        "c_a_bias": nrm(ks[6], (L, C_HEADS * C_KEY_DIM), 0.5),
        "c_norm_gain": 1.0 + nrm(ks[7], (L, bw), 0.05),
        "d_mu": jax.random.uniform(ks[8], (L, D_IN_WIDTH), f32),
        "d_w0": nrm(ks[9], (L, bw), 0.5),
        "d_w2": nrm(ks[10], (L, D_DECAY_RANK, bw), 0.5 * D_DECAY_RANK ** -0.5),
        "d_a0": nrm(ks[11], (L, bw), 0.1),
        "d_a2": nrm(ks[12], (L, D_ICLR_RANK, bw), 0.5 * D_ICLR_RANK ** -0.5),
        "d_g2": nrm(ks[13], (L, D_GATE_RANK, bw), D_GATE_RANK ** -0.5),
        "d_k_k": 0.85 + nrm(ks[14], (L, bw), 0.05),
        "d_k_a": 1.0 + nrm(ks[15], (L, bw), 0.05),
        "d_r_k": nrm(ks[16], (L, bw), 0.1),
        "d_gn_w": 1.0 + nrm(ks[17], (L, bw), 0.05),
        "d_gn_b": nrm(ks[18], (L, bw), 0.01),
        "w_branch": nrm(ks[19], (L, N_BRANCHES, bw, D_MODEL), bw ** -0.5),
        "w_out": nrm(ks[20], (L, D_MODEL, D_MODEL), D_MODEL ** -0.5 * DN_BETA),
        "ln_g": 1.0 + nrm(ks[21], (L, 2, D_MODEL), 0.05),
        "ln_b": nrm(ks[22], (L, 2, D_MODEL), 0.01),
        "router_g": nrm(ks[23], (L, D_MODEL, MOE_GROUPS), D_MODEL ** -0.5),
        "router_g_bias": nrm(ks[24], (L, MOE_GROUPS), 0.01),
        "router_e": nrm(ks[25], (L, D_MODEL, MOE_EXPERTS), D_MODEL ** -0.5),
        "router_e_bias": nrm(ks[26], (L, MOE_EXPERTS), 0.01),
        "moe_w_gate": nrm(ks[27], (L, MOE_EXPERTS, D_MODEL, MOE_HIDDEN), D_MODEL ** -0.5),
        "moe_w_up": nrm(ks[28], (L, MOE_EXPERTS, D_MODEL, MOE_HIDDEN), D_MODEL ** -0.5),
        "moe_w_down": nrm(ks[29], (L, MOE_EXPERTS, MOE_HIDDEN, D_MODEL), MOE_HIDDEN ** -0.5 * DN_BETA),
    }

def first_block(x, rpb_table, w_in, b_kv_gain, b_w_uv, c_a_up, c_a_bias, c_norm_gain,
              d_mu, d_w0, d_w2, d_a0, d_a2, d_g2, d_k_k, d_k_a, d_r_k, d_gn_w, d_gn_b,
              w_branch, w_out, ln_g, ln_b, router_g, router_g_bias, router_e, router_e_bias,
              moe_w_gate, moe_w_up, moe_w_down):
    bsz, seq, _ = x.shape
    for l in range(DEPTH):
        p = _split_in(x @ w_in[l])
        ya = _mixer_a(p["a_q"], p["a_k"], p["a_v"], rpb_table[:, :A_HEADS])
        yb = _mixer_b(p["b_q"], p["b_ckv"], p["b_iq"], p["b_ik"], p["b_iw"],
                      b_kv_gain[l], b_w_uv[l], rpb_table[:, A_HEADS:])
        yc = _mixer_c(p["c_q"], p["c_k"], p["c_v"], p["c_a"], p["c_g"],
                      c_a_up[l], c_a_bias[l], c_norm_gain[l])
        yd = _mixer_d(p["d"], d_mu[l], d_w0[l], d_w2[l], d_a0[l], d_a2[l], d_g2[l],
                      d_k_k[l], d_k_a[l], d_r_k[l], d_gn_w[l], d_gn_b[l])
        ys = jnp.stack([ya.astype(x.dtype), yb.astype(x.dtype), yc.astype(x.dtype), yd.astype(x.dtype)], axis=2)
        gates = jax.nn.sigmoid(p["gate"].reshape(bsz, seq, N_BRANCHES, D_MODEL))
        merged = jnp.sum(gates * jnp.einsum('bsnc,ncd->bsnd', ys, w_branch[l]), axis=2)
        x = _layer_norm(DN_ALPHA * x + merged @ w_out[l], ln_g[l, 0], ln_b[l, 0])
        y = _moe(x, router_g[l], router_g_bias[l], router_e[l], router_e_bias[l],
                 moe_w_gate[l], moe_w_up[l], moe_w_down[l])
        x = _layer_norm(DN_ALPHA * x + y, ln_g[l, 1], ln_b[l, 1])
    return x


DEPTH_2 = 2

GRID_W = 64
N_MEM = 256
N_BRANCH = 4
BRANCH_WIDTH_2 = D_MODEL // N_BRANCH
IN_WIDTH_2 = 9 * BRANCH_WIDTH_2
RET_HEADS = BRANCH_WIDTH_2 // HEAD_DIM
RET_CHUNK = 128
ROPE_THETA = 10000.0
POOL_WINDOWS = (2, 4, 8, 16)
POOL_GROUPS = len(POOL_WINDOWS)
POOL_GROUP_DIM = BRANCH_WIDTH_2 // POOL_GROUPS
NA_HEADS = BRANCH_WIDTH_2 // HEAD_DIM
NA_WIN_ROWS = 8
NA_WIN_COLS = 16
NA_QBLOCK_COLS = 16
NA_KBLOCK_COLS = 2 * NA_QBLOCK_COLS
MEM_HEADS = BRANCH_WIDTH_2 // HEAD_DIM
FF_HIDDEN = -(-8 * D_MODEL // (3 * 256)) * 256
NEG_INF = -1e30
EPS = 1e-6


def rms_norm(x, g):
    xf = x.astype(jnp.float32)
    y = xf * lax.rsqrt(jnp.mean(xf * xf, axis=-1, keepdims=True) + EPS)
    return (y * g.astype(jnp.float32)).astype(x.dtype)

def split_heads(t, n_heads):
    b, s, _ = t.shape
    return t.reshape(b, s, n_heads, -1).transpose(0, 2, 1, 3)

def merge_heads(t):
    b, h, s, d = t.shape
    return t.transpose(0, 2, 1, 3).reshape(b, s, h * d)

def rotary(t, pos):
    half = t.shape[-1] // 2
    inv = ROPE_THETA ** (-jnp.arange(half, dtype=jnp.float32) / half)
    ang = pos[:, None] * inv[None, :]
    cos, sin = jnp.cos(ang), jnp.sin(ang)
    tf = t.astype(jnp.float32)
    t1, t2 = tf[..., :half], tf[..., half:]
    return jnp.concatenate([t1 * cos - t2 * sin, t1 * sin + t2 * cos], axis=-1).astype(t.dtype)

def retention_dir(q, k, v, log_gamma, include_diag):
    b, h, s, d = q.shape
    c = RET_CHUNK
    n = s // c
    dt = q.dtype
    qc, kc, vc = (t.reshape(b, h, n, c, d) for t in (q, k, v))
    idx = jnp.arange(c, dtype=jnp.float32)
    diff = idx[:, None] - idx[None, :]
    mask = (diff >= 0) if include_diag else (diff > 0)
    lg = log_gamma.astype(jnp.float32)[:, None]
    d_intra = jnp.where(mask[None], jnp.exp(jnp.where(mask, diff, 0.0)[None] * lg[:, :, None]), 0.0)
    scores = jnp.einsum('bhncd,bhnmd->bhncm', qc, kc) * d_intra[None, :, None].astype(dt)
    intra = jnp.einsum('bhncm,bhnme->bhnce', scores, vc)
    k_decay = jnp.exp((c - 1 - idx)[None, :] * lg).astype(dt)
    kv = jnp.einsum('bhncd,bhnce->nbhde', kc * k_decay[None, :, None, :, None], vc)
    chunk_decay = jnp.exp(c * lg[:, 0]).astype(dt)[None, :, None, None]

    def step(state, kv_n):
        return chunk_decay * state + kv_n, state

    _, states = lax.scan(step, jnp.zeros_like(kv[0]), kv)
    q_decay = jnp.exp((idx + 1)[None, :] * lg).astype(dt)
    cross = jnp.einsum('bhncd,nbhde->bhnce', qc * q_decay[None, :, None, :, None], states)
    return (intra + cross).reshape(b, h, s, d)

def bidirectional_retention(q, k, v, log_gamma_fwd, log_gamma_bwd):
    fwd = retention_dir(q, k, v, log_gamma_fwd, True)
    flip = lambda t: jnp.flip(t, axis=2)
    bwd = flip(retention_dir(flip(q), flip(k), flip(v), log_gamma_bwd, False))
    return fwd + bwd

def multiscale_pool(v, w_group, scale):
    b, s, cw = v.shape
    vg = v.reshape(b, s, POOL_GROUPS, POOL_GROUP_DIM)
    cs = jnp.cumsum(vg.astype(jnp.float32), axis=1)
    cs = jnp.concatenate([jnp.zeros_like(cs[:, :1]), cs], axis=1)
    t = np.arange(s)[:, None]
    half = np.array(POOL_WINDOWS)[None, :] // 2
    lo = np.clip(t - half, 0, s)
    hi = np.clip(t + half, 0, s)
    g_idx = np.arange(POOL_GROUPS)[None, :]
    win_sum = cs[:, hi, g_idx] - cs[:, lo, g_idx]
    count = jnp.asarray((hi - lo)[None, :, :, None], dtype=jnp.float32)
    pooled = (win_sum / count).astype(v.dtype) - vg
    mixed = jnp.einsum('bsgc,gce->bsge', pooled, w_group)
    return mixed.reshape(b, s, cw) * scale

def neighbourhood_attention(q, k, v, rpb):
    b, h, s, d = q.shape
    rows = s // GRID_W
    wr = min(NA_WIN_ROWS, rows)
    n_cb = GRID_W // NA_QBLOCK_COLS
    r = np.arange(rows)
    row_idx = np.clip(r - wr // 2, 0, rows - wr)[:, None] + np.arange(wr)[None, :]
    cb = np.arange(n_cb)
    kcol_idx = np.clip(cb * NA_QBLOCK_COLS - NA_WIN_COLS // 2, 0, GRID_W - NA_KBLOCK_COLS)[:, None] \
        + np.arange(NA_KBLOCK_COLS)[None, :]
    qcol = cb[:, None] * NA_QBLOCK_COLS + np.arange(NA_QBLOCK_COLS)[None, :]
    qwin = np.clip(qcol - NA_WIN_COLS // 2, 0, GRID_W - NA_WIN_COLS)
    col_mask = (kcol_idx[:, None, :] >= qwin[:, :, None]) & (kcol_idx[:, None, :] < qwin[:, :, None] + NA_WIN_COLS)
    row_off = row_idx - r[:, None]
    col_off = np.clip(kcol_idx[:, None, :] - qcol[:, :, None], -(NA_WIN_COLS - 1), NA_WIN_COLS - 1)
    bias = rpb[:, row_off[:, None, None, :, None] + NA_WIN_ROWS - 1,
               col_off[None, :, :, None, :] + NA_WIN_COLS - 1]
    bias = jnp.where(col_mask[None, None, :, :, None, :], bias.astype(jnp.float32), NEG_INF)

    qg = q.reshape(b, h, rows, n_cb, NA_QBLOCK_COLS, d)
    k_grid = k.reshape(b, h, rows, GRID_W, d)
    v_grid = v.reshape(b, h, rows, GRID_W, d)
    ri = row_idx[:, None, :, None]
    ci = kcol_idx[None, :, None, :]
    kg = k_grid[:, :, ri, ci]
    vg = v_grid[:, :, ri, ci]
    sc = jnp.einsum('bhrnqd,bhrnwkd->bhrnqwk', qg, kg).astype(jnp.float32) * (d ** -0.5) + bias[None]
    p = jax.nn.softmax(sc, axis=(-2, -1))
    o = jnp.einsum('bhrnqwk,bhrnwkd->bhrnqd', p.astype(v.dtype), vg)
    return o.reshape(b, h, s, d)

def memory_attention(q, mk, mv):
    sc = jnp.einsum('bhsd,bhmd->bhsm', q, mk).astype(jnp.float32) * (q.shape[-1] ** -0.5)
    p = jax.nn.softmax(sc, axis=-1)
    return jnp.einsum('bhsm,bhmd->bhsd', p.astype(mv.dtype), mv)

def hybrid_layer(x, mem, norm_mix_g, norm_mem_g, w_in, w_gate, ret_decay_fwd, ret_decay_bwd,
                 ret_norm_g, pool_w, pool_scale, na_q_norm_g, na_k_norm_g, na_rpb,
                 mem_q_norm_g, mem_k_norm_g, w_mem_kv, w_branch, w_out, norm_ffn_g,
                 w_ffn_in, w_ffn_out):
    b, s, dm = x.shape
    h = rms_norm(x, norm_mix_g)
    proj = h @ w_in
    rq, rk, rv, rg, pv, nq, nk, nv, mq = jnp.split(proj, 9, axis=-1)

    pos = jnp.arange(s, dtype=jnp.float32)
    rq_h = rotary(split_heads(rq, RET_HEADS), pos) * (HEAD_DIM ** -0.5)
    rk_h = rotary(split_heads(rk, RET_HEADS), pos)
    ret = bidirectional_retention(rq_h, rk_h, split_heads(rv, RET_HEADS),
                                  jax.nn.log_sigmoid(ret_decay_fwd.astype(jnp.float32)),
                                  jax.nn.log_sigmoid(ret_decay_bwd.astype(jnp.float32)))
    ret = merge_heads(rms_norm(ret, ret_norm_g.reshape(RET_HEADS, 1, HEAD_DIM))) * jax.nn.silu(rg)

    pool = multiscale_pool(pv, pool_w, pool_scale)

    na = merge_heads(neighbourhood_attention(rms_norm(split_heads(nq, NA_HEADS), na_q_norm_g),
                                             rms_norm(split_heads(nk, NA_HEADS), na_k_norm_g),
                                             split_heads(nv, NA_HEADS), na_rpb))

    mk, mv = jnp.split(rms_norm(mem, norm_mem_g) @ w_mem_kv, 2, axis=-1)
    mo = merge_heads(memory_attention(rms_norm(split_heads(mq, MEM_HEADS), mem_q_norm_g),
                                      rms_norm(split_heads(mk, MEM_HEADS), mem_k_norm_g),
                                      split_heads(mv, MEM_HEADS)))

    branches = jnp.stack([ret, pool, na, mo], axis=2)
    up = jnp.einsum('bsnc,ncd->bsnd', branches, w_branch)
    gates = jax.nn.sigmoid(h @ w_gate).reshape(b, s, N_BRANCH, dm)
    merged = jnp.einsum('bsnd,bsnd->bsd', gates, up)
    x = x + merged @ w_out

    a, g = jnp.split(rms_norm(x, norm_ffn_g) @ w_ffn_in, 2, axis=-1)
    return x + (jax.nn.silu(a) * g) @ w_ffn_out

def second_inputs(seed: int = 0) -> dict:
    key = jax.random.key(seed)
    ks = jax.random.split(key, 22)
    f32 = jnp.float32
    L, D, BW = DEPTH_2, D_MODEL, BRANCH_WIDTH_2

    def nrm(k, shape, scale):
        return jax.random.normal(k, shape, f32) * scale

    base_logit = jnp.log(2.0 ** (5.0 + jnp.arange(RET_HEADS, dtype=f32)) - 1.0)
    return {
        "x": nrm(ks[0], (BATCH, SEQ, D), 1.0),
        "mem": nrm(ks[1], (BATCH, N_MEM, D), 1.0),
        "norm_mix_g": 1.0 + nrm(ks[2], (L, D), 0.02),
        "norm_mem_g": 1.0 + nrm(ks[3], (L, D), 0.02),
        "w_in": nrm(ks[4], (L, D, IN_WIDTH_2), D ** -0.5),
        "w_gate": nrm(ks[5], (L, D, N_BRANCH * D), D ** -0.5),
        "ret_decay_fwd": base_logit[None, :] + nrm(ks[6], (L, RET_HEADS), 0.1),
        "ret_decay_bwd": base_logit[None, :] + nrm(ks[7], (L, RET_HEADS), 0.1),
        "ret_norm_g": 1.0 + nrm(ks[8], (L, BW), 0.02),
        "pool_w": nrm(ks[9], (L, POOL_GROUPS, POOL_GROUP_DIM, POOL_GROUP_DIM), POOL_GROUP_DIM ** -0.5),
        "pool_scale": 1.0 + nrm(ks[10], (L, BW), 0.02),
        "na_q_norm_g": 1.0 + nrm(ks[11], (L, HEAD_DIM), 0.02),
        "na_k_norm_g": 1.0 + nrm(ks[12], (L, HEAD_DIM), 0.02),
        "na_rpb": nrm(ks[13], (L, NA_HEADS, 2 * NA_WIN_ROWS - 1, 2 * NA_WIN_COLS - 1), 0.02),
        "mem_q_norm_g": 1.0 + nrm(ks[14], (L, HEAD_DIM), 0.02),
        "mem_k_norm_g": 1.0 + nrm(ks[15], (L, HEAD_DIM), 0.02),
        "w_mem_kv": nrm(ks[16], (L, D, 2 * BW), D ** -0.5),
        "w_branch": nrm(ks[17], (L, N_BRANCH, BW, D), BW ** -0.5),
        "w_out": nrm(ks[18], (L, D, D), D ** -0.5),
        "norm_ffn_g": 1.0 + nrm(ks[19], (L, D), 0.02),
        "w_ffn_in": nrm(ks[20], (L, D, 2 * FF_HIDDEN), D ** -0.5),
        "w_ffn_out": nrm(ks[21], (L, FF_HIDDEN, D), FF_HIDDEN ** -0.5),
    }

def second_block(x, mem, norm_mix_g, norm_mem_g, w_in, w_gate, ret_decay_fwd, ret_decay_bwd,
              ret_norm_g, pool_w, pool_scale, na_q_norm_g, na_k_norm_g, na_rpb,
              mem_q_norm_g, mem_k_norm_g, w_mem_kv, w_branch, w_out, norm_ffn_g,
              w_ffn_in, w_ffn_out):
    for l in range(DEPTH_2):
        x = hybrid_layer(x, mem, norm_mix_g[l], norm_mem_g[l], w_in[l], w_gate[l],
                         ret_decay_fwd[l], ret_decay_bwd[l], ret_norm_g[l], pool_w[l],
                         pool_scale[l], na_q_norm_g[l], na_k_norm_g[l], na_rpb[l],
                         mem_q_norm_g[l], mem_k_norm_g[l], w_mem_kv[l], w_branch[l],
                         w_out[l], norm_ffn_g[l], w_ffn_in[l], w_ffn_out[l])
    return x


def setup_inputs(seed=0):
    out = dict(first_inputs(seed))
    for name, value in second_inputs(seed + 1).items():
        if name != "x":
            out[name + "_2"] = value
    return out


def reference(
    x, rpb_table, w_in, b_kv_gain, b_w_uv, c_a_up, c_a_bias, c_norm_gain, d_mu, d_w0, d_w2,
    d_a0, d_a2, d_g2, d_k_k, d_k_a, d_r_k, d_gn_w, d_gn_b, w_branch, w_out, ln_g, ln_b,
    router_g, router_g_bias, router_e, router_e_bias, moe_w_gate, moe_w_up, moe_w_down, mem_2,
    norm_mix_g_2, norm_mem_g_2, w_in_2, w_gate_2, ret_decay_fwd_2, ret_decay_bwd_2,
    ret_norm_g_2, pool_w_2, pool_scale_2, na_q_norm_g_2, na_k_norm_g_2, na_rpb_2,
    mem_q_norm_g_2, mem_k_norm_g_2, w_mem_kv_2, w_branch_2, w_out_2, norm_ffn_g_2, w_ffn_in_2,
    w_ffn_out_2,
):
    x = first_block(
        x, rpb_table, w_in, b_kv_gain, b_w_uv, c_a_up, c_a_bias, c_norm_gain, d_mu, d_w0, d_w2,
        d_a0, d_a2, d_g2, d_k_k, d_k_a, d_r_k, d_gn_w, d_gn_b, w_branch, w_out, ln_g, ln_b,
        router_g, router_g_bias, router_e, router_e_bias, moe_w_gate, moe_w_up, moe_w_down,
    )
    return second_block(
        x, mem_2, norm_mix_g_2, norm_mem_g_2, w_in_2, w_gate_2, ret_decay_fwd_2,
        ret_decay_bwd_2, ret_norm_g_2, pool_w_2, pool_scale_2, na_q_norm_g_2, na_k_norm_g_2,
        na_rpb_2, mem_q_norm_g_2, mem_k_norm_g_2, w_mem_kv_2, w_branch_2, w_out_2, norm_ffn_g_2,
        w_ffn_in_2, w_ffn_out_2,
    )


_drawn_inputs = setup_inputs


def setup_inputs(seed=0):
    import zlib

    import numpy as np

    out = dict(_drawn_inputs(seed))
    spreads = {}
    factors = {'b_kv_gain': 3.473,
     'c_norm_gain': 3.212,
     'd_w2': 3.517,
     'd_a0': 3.596,
     'd_k_k': 8.0,
     'd_k_a': 3.297,
     'd_gn_w': 4.162,
     'd_gn_b': 8.0,
     'router_g_bias': 6.278,
     'router_e_bias': 6.493,
     'norm_mem_g_2': 8.0,
     'ret_norm_g_2': 6.73,
     'pool_scale_2': 4.256,
     'na_q_norm_g_2': 8.0,
     'na_k_norm_g_2': 8.0,
     'na_rpb_2': 56.615,
     'mem_q_norm_g_2': 8.0,
     'mem_k_norm_g_2': 8.0,
     'norm_ffn_g_2': 2.965}
    for name, (base, spread) in spreads.items():
        noise = np.random.default_rng([zlib.crc32(name.encode()), seed]).standard_normal(out[name].shape)
        drawn = base * np.exp(spread * noise) if base else spread * noise
        out[name] = __import__('jax').numpy.asarray(drawn.astype(out[name].dtype))
    for name, factor in factors.items():
        out[name] = (out[name] * factor).astype(out[name].dtype)
    return out
```

```python
import math
from contextlib import ExitStack, contextmanager

import numpy as np

import concourse.bass as bass
from concourse import mybir

F32 = mybir.dt.float32
F32R = mybir.dt.float32r
ALU = mybir.AluOpType
ACT = mybir.ActivationFunctionType
AX = mybir.AxisListType

SEQ, D, FF, LAYERS, EXPERTS = 512, 1024, 2816, 2, 32
KT = D // 128
CHUNK = 2048
SLOTS = 2
ALPHA = 2.0 ** 0.25
MASKED = -1e30
TAKEN = -3e38
STRIP = 896
POOL_WINDOWS = (2, 4, 8, 16)
FIRST_CHUNKS = 37
MOE_CHUNKS = 12
LAYER_CHUNKS = 68
CHUNKS = FIRST_CHUNKS + 8 * MOE_CHUNKS + LAYERS * LAYER_CHUNKS
SPARE = 4

_widths = dict(ident=128, ones=128, blk64=128, gla_mask=128, up_same=128, up_other=128, low_same=128, up=128,
               up_diag=128, future=128, gla_heads=256, reset64=512, reset128=512, rotate=128, rank8=32)
CONST = {}
CONSTS = 0
for _n, _w in _widths.items():
    CONST[_n] = CONSTS
    CONSTS += _w

P1 = dict(ln_g=0, ln_b=16, kv_gain=32, a_bias=33, c_norm=34, mu=36, w0=43, a0=45, k_k=47, k_a=49, r_k=51, gn_w=53,
          gn_b=55)
P1_COLS = 57
P2 = dict(mix=0, mem=8, ffn=16, ret=24, pool=26, naq=28, nak=29, memq=30, memk=31, decay=32)
P2_COLS = 40
T1 = dict(aq=0, ak=2, bq=4, iq=6, ckv=8, ik=9, low=10, cq=11, ck=12, cg=13, dr=15, dk=17, dv=19)
T1_TILES = 21
T2 = dict(rq=0, rk=2, rg=4, pv=6, nq=8, nk=10, mq=12)
T2_TILES = 14


class Kernel:

    def __init__(self, nc, dram):
        self.nc, self.dram, self.tensors = nc, dram, 0


class Order:

    def __init__(self, engine, sem):
        self.engine, self.sem, self.n = engine, sem, 0

    def __call__(self, instruction):
        instruction.then_inc(self.sem, 1)
        self.n += 1
        self.engine.wait_ge(self.sem, self.n)


class Stream:

    def __init__(self, nc, ctx, dram):
        self.dram = dram
        self.raw = ctx.enter_context(nc.sbuf_tensor("w_raw", [128, SLOTS, CHUNK], F32))
        self.hi = ctx.enter_context(nc.sbuf_tensor("w_hi", [128, SLOTS, CHUNK], F32R))
        self.lo = ctx.enter_context(nc.sbuf_tensor("w_lo", [128, SLOTS, CHUNK], F32R))
        self.zero = ctx.enter_context(nc.sbuf_tensor("w_zero", [128, 1], F32))
        self.loaded = [ctx.enter_context(nc.semaphore(f"w_loaded{s}")) for s in range(SLOTS)]
        self.rounded = ctx.enter_context(nc.semaphore("w_rounded"))
        self.split = ctx.enter_context(nc.semaphore("w_split"))
        self.used = ctx.enter_context(nc.semaphore("w_used"))
        self.blocks = 0
        self.n_loaded = 0
        self.n_split = 0
        self.turn = 0
        self.want = 0

    def plan(self, n_blocks):
        self.want = self.blocks + n_blocks
        started = -(-self.want // 16)
        self.to_split = started + 1
        self.to_load = started + 3

    def load(self, sp, upto=None):
        for c in range(self.n_loaded, self.to_load if upto is None else upto):
            if c >= SLOTS:
                sp.wait_ge(self.split, self.turn + (c - SLOTS + 1))
            sp.dma_start(self.raw[:, c % SLOTS, :], self.dram[self.turn + c, :, :]).then_inc(
                self.loaded[c % SLOTS], 16)
        self.n_loaded = max(self.n_loaded, self.to_load)

    def divide(self, pool):
        for c in range(self.n_split, self.to_split):
            s = c % SLOTS
            pool.wait_ge(self.loaded[s], self.turn * (16 // SLOTS) + 16 * (c // SLOTS + 1))
            if c >= SLOTS:
                pool.wait_ge(self.used, self.turn + (c - SLOTS + 1))
            pool.tensor_tensor(self.hi[:, s, :], self.raw[:, s, :], self.zero[:, 0:1].to_broadcast([128, CHUNK]),
                               ALU.add).then_inc(self.rounded, 1)
            pool.wait_ge(self.rounded, self.turn + (c + 1))
            pool.tensor_tensor(self.lo[:, s, :], self.raw[:, s, :], self.hi[:, s, :].bitcast(F32),
                               ALU.subtract).then_inc(self.split, 1)
        self.n_split = self.to_split

    def take(self, pe, n=1):
        c, b = divmod(self.blocks, 16)
        assert b + n <= 16
        if b == 0:
            pe.wait_ge(self.split, self.turn + (c + 1))
            self.release = c > 0
        self.blocks += n
        cols = slice(128 * b, 128 * (b + n))
        return self.hi[:, c % SLOTS, cols], self.lo[:, c % SLOTS, cols]

    def released(self, matmul):
        if self.release:
            matmul.then_inc(self.used, 1)
            self.release = False

    def product(self, pe, out, moving, start, stop):
        hi, lo = self.take(pe)
        self.released(pe.matmul(out, hi, moving[0], start=start, stop=False))
        pe.matmul(out, hi, moving[1], start=False, stop=False)
        return pe.matmul(out, lo, moving[0], start=False, stop=stop)

    def product_tm(self, pe, outs, still, n, start, stop):
        hi, lo = self.take(pe, n)
        for out, (sh, sl) in zip(outs, still):
            self.released(pe.matmul(out, sh, hi, start=start, stop=False))
            pe.matmul(out, sh, lo, start=False, stop=False)
            last = pe.matmul(out, sl, hi, start=False, stop=stop)
        return last


@contextmanager
def stage(k, *names):
    nc = k.nc
    with ExitStack() as ctx:
        sems = [ctx.enter_context(nc.semaphore(n)) for n in names]
        with nc.Block(no_gpsimd_drain=True) as block:
            yield (block, *sems)
        for s in sems:
            nc.sync.sem_clear(s)
        nc.all_engine_barrier()


@contextmanager
def memory(k, **shapes):
    with ExitStack() as ctx:
        out = []
        for name, shape in shapes.items():
            dt = F32
            if shape[0] == "r":
                dt, shape = F32R, shape[1:]
            k.tensors += 1
            out.append(ctx.enter_context(k.nc.sbuf_tensor(f"{name}_{k.tensors}", [128, *shape], dt)))
        yield out[0] if len(out) == 1 else out


def const(k, name, rows=slice(0, 128)):
    return k.consts[rows, CONST[name]:CONST[name] + _widths[name]]




def load_start(k):
    with stage(k, "zeroed", "loaded_in", "rounded_x") as (block, zeroed, loaded_in, rounded_x):
        @block.sync
        def _(sp):
            sp.dma_start(k.consts[:, :], k.dram["consts"]).then_inc(loaded_in, 16)
            sp.dma_start(k.res[:, :, :], k.dram["xT"]).then_inc(loaded_in, 16)
            sp.dma_start(k.par1[:, :], k.dram["params1"]).then_inc(loaded_in, 16)
            sp.dma_start(k.mats1[:, :], k.dram["mats1"]).then_inc(loaded_in, 16)

        @block.vector
        def _(dve):
            dve.memset(k.ws.zero[:, :], 0.0).then_inc(zeroed, 1)
            dve.memset(k.eps[:, 0:1], 1e-5).then_inc(zeroed, 1)
            dve.memset(k.eps[:, 1:2], 1e-6).then_inc(zeroed, 1)
            dve.memset(k.eps[:, 2:3], 64e-5).then_inc(zeroed, 1)
            dve.memset(k.eps[:, 3:4], 1.0).then_inc(zeroed, 1)
            dve.wait_ge(loaded_in, 64)
            for t in range(KT):
                dve.tensor_copy(k.xh[:, t, :], k.res[:, t, :]).then_inc(rounded_x, 1)
                dve.wait_ge(rounded_x, t + 1)
                last = dve.tensor_tensor(k.xl[:, t, :], k.res[:, t, :], k.xh[:, t, :].bitcast(F32), ALU.subtract)
            last.then_inc(zeroed, 1)


def project(k, tiles, out, token_major, moving=None, n_moving=SEQ):
    ws = k.ws
    moving = moving or (k.xh, k.xl)
    nt = n_moving // 128
    ws.plan(tiles * KT + sum(KT * w // 128 for _, w in token_major))
    with stage(k, "product_ready", "product_copied", "rows_ready", "rows_copied") as (
            block, product_ready, product_copied, rows_ready, rows_copied):
        @block.sync
        def _(sp):
            ws.load(sp)

        @block.gpsimd
        def _(pool):
            ws.divide(pool)

        @block.tensor
        def _(pe):
            for j in range(tiles):
                if j >= 2:
                    pe.wait_ge(product_copied, j - 1)
                for t in range(KT):
                    last = ws.product(pe, k.bank[j % 2][:, 0:n_moving],
                                      (moving[0][:, t, 0:n_moving], moving[1][:, t, 0:n_moving]), t == 0, t == KT - 1)
                last.then_inc(product_ready, 1)
            for m, (_, width) in enumerate(token_major):
                if m:
                    pe.wait_ge(rows_copied, m)
                for t in range(KT):
                    still = [(moving[0][:, t, 128 * q:128 * q + 128], moving[1][:, t, 128 * q:128 * q + 128])
                             for q in range(nt)]
                    last = ws.product_tm(pe, [k.bank[4 + q][:, 0:width] for q in range(nt)], still, width // 128,
                                         t == 0, t == KT - 1)
                last.then_inc(rows_ready, 1)

        @block.vector
        def _(dve):
            for j in range(tiles):
                dve.wait_ge(product_ready, j + 1)
                dve.tensor_copy(out[:, j, 0:n_moving], k.bank[j % 2][:, 0:n_moving]).then_inc(product_copied, 1)
            for m, (rows, width) in enumerate(token_major):
                dve.wait_ge(rows_ready, m + 1)
                for q in range(nt):
                    last = dve.tensor_copy(rows[:, q, :], k.bank[4 + q][:, 0:width])
                last.then_inc(rows_copied, 1)


def normalise(k, src, gain, bias, eps, mean, hi=None, lo=None, out=None, n=SEQ):
    ones = const(k, "ones")
    with memory(k, nrm_sq=(2, n), nrm_mean=(n,), nrm_rstd=(n,), nrm_c=(KT, n) if mean else (1, 1),
                nrm_y=(2, n)) as (sq, mu, rstd, cent, y), \
            stage(k, "summed", "mean_ready", "centred", "squared", "square_used", "var_ready", "log_ready",
                  "rstd_ready", "vector_order") as (
                block, summed, mean_ready, centred, squared, square_used, var_ready, log_ready, rstd_ready, order):
        x = cent if mean else src

        @block.tensor
        def _(pe):
            if mean:
                for t in range(KT):
                    last = pe.matmul(k.bank[0][:, 0:n], ones, src[:, t, :], start=t == 0, stop=t == KT - 1)
                last.then_inc(summed, 1)
            for t in range(KT):
                pe.wait_ge(squared, t + 1)
                pe.matmul(k.bank[1][:, 0:n], ones, sq[:, t % 2, :], start=t == 0, stop=t == KT - 1).then_inc(
                    square_used, 1)

        @block.scalar
        def _(act):
            for t in range(KT):
                if mean:
                    act.wait_ge(centred, t + 1)
                if t >= 2:
                    act.wait_ge(square_used, t - 1)
                act.activation(sq[:, t % 2, :], x[:, t, :], ACT.Square).then_inc(squared, 1)
            act.wait_ge(square_used, KT)
            act.activation(rstd[:, :], k.bank[1][:, 0:n], ACT.Ln, scale=1.0 / D, bias=eps).then_inc(log_ready, 1)
            act.wait_ge(log_ready, 1)
            act.activation(rstd[:, :], rstd[:, :], ACT.Exp, scale=-0.5).then_inc(rstd_ready, 1)

        @block.vector
        def _(dve):
            step = Order(dve, order)
            if mean:
                dve.wait_ge(summed, 1)
                step(dve.tensor_scalar(mu[:, :], k.bank[0][:, 0:n], 1.0 / D, None, ALU.mult))
                for t in range(KT):
                    dve.tensor_tensor(cent[:, t, :], src[:, t, :], mu[:, :], ALU.subtract).then_inc(centred, 1)
            dve.wait_ge(rstd_ready, 1)
            for t in range(KT):
                dst = y[:, t % 2, :] if out is None else out[:, t, :]
                step(dve.tensor_tensor(y[:, t % 2, :], x[:, t, :], rstd[:, :], ALU.mult))
                if bias is None:
                    step(dve.tensor_scalar(dst, y[:, t % 2, :], gain(t), None, ALU.mult))
                else:
                    step(dve.tensor_scalar(dst, y[:, t % 2, :], gain(t), bias(t), ALU.mult, ALU.add))
                if hi is not None:
                    step(dve.tensor_copy(hi[:, t, :], dst))
                    step(dve.tensor_tensor(lo[:, t, :], dst, hi[:, t, :].bitcast(F32), ALU.subtract))


def merge(k, scale_residual):
    ws = k.ws
    with memory(k, yh=("r", KT, SEQ), yl=("r", KT, SEQ), mh=("r", KT, SEQ), ml=("r", KT, SEQ), sig=(2, SEQ),
                part=(2, SEQ)) as (yh, yl, mh, ml, sig, part):
        ws.plan(KT * 40)
        with stage(k, "gate_ready", "sigmoid_ready", "branch_ready", "banks_free", "branch_rounded", "merge_order",
                   "branch_split") as (block, gate_ready, sigmoid_ready, branch_ready, banks_free, rounded, order,
                                       branch_split):
            @block.sync
            def _(sp):
                ws.load(sp)

            @block.gpsimd
            def _(pool):
                ws.divide(pool)

            @block.tensor
            def _(pe):
                for dt in range(KT):
                    for n in range(4):
                        u = 4 * dt + n
                        if u >= 2:
                            pe.wait_ge(banks_free, u - 1)
                        g, b = k.bank[2 * (u % 2)], k.bank[2 * (u % 2) + 1]
                        for t in range(KT):
                            last = ws.product(pe, g[:, :], (k.xh[:, t, :], k.xl[:, t, :]), t == 0, t == KT - 1)
                        last.then_inc(gate_ready, 1)
                        if u == 0:
                            pe.wait_ge(branch_split, KT)
                        for c in range(2):
                            last = ws.product(pe, b[:, :], (yh[:, 2 * n + c, :], yl[:, 2 * n + c, :]), c == 0, c == 1)
                        last.then_inc(branch_ready, 1)

            @block.scalar
            def _(act):
                for u in range(4 * KT):
                    act.wait_ge(gate_ready, u + 1)
                    if u >= 2:
                        act.wait_ge(banks_free, u - 1)
                    act.activation(sig[:, u % 2, :], k.bank[2 * (u % 2)][:, :], ACT.Sigmoid).then_inc(
                        sigmoid_ready, 1)

            @block.vector
            def _(dve):
                step = Order(dve, order)
                for t in range(KT):
                    step(dve.tensor_copy(yh[:, t, :], k.yb[:, t, :]))
                    dve.tensor_tensor(yl[:, t, :], k.yb[:, t, :], yh[:, t, :].bitcast(F32), ALU.subtract).then_inc(
                        branch_split, 1)
                for dt in range(KT):
                    for n in range(4):
                        u = 4 * dt + n
                        dve.wait_ge(sigmoid_ready, u + 1)
                        dve.wait_ge(branch_ready, u + 1)
                        dve.tensor_tensor(part[:, 0 if n == 0 else 1, :], sig[:, u % 2, :],
                                          k.bank[2 * (u % 2) + 1][:, :], ALU.mult).then_inc(banks_free, 1)
                        dve.wait_ge(banks_free, u + 1)
                        if n:
                            step(dve.tensor_tensor(part[:, 0, :], part[:, 0, :], part[:, 1, :], ALU.add))
                    step(dve.tensor_copy(mh[:, dt, :], part[:, 0, :]))
                    step(dve.tensor_tensor(ml[:, dt, :], part[:, 0, :], mh[:, dt, :].bitcast(F32), ALU.subtract))
        add_product(k, KT, mh, ml, scale_residual)


def add_product(k, tiles_in, hi, lo, scale_residual):
    ws = k.ws
    ws.plan(KT * tiles_in)
    with stage(k, "product_ready", "product_added") as (block, product_ready, product_added):
        @block.sync
        def _(sp):
            ws.load(sp)

        @block.gpsimd
        def _(pool):
            ws.divide(pool)

        @block.tensor
        def _(pe):
            for dt in range(KT):
                if dt >= 2:
                    pe.wait_ge(product_added, dt - 1)
                for t in range(tiles_in):
                    last = ws.product(pe, k.bank[dt % 2][:, :], (hi[:, t, :], lo[:, t, :]), t == 0,
                                      t == tiles_in - 1)
                last.then_inc(product_ready, 1)

        @block.vector
        def _(dve):
            for dt in range(KT):
                dve.wait_ge(product_ready, dt + 1)
                dve.scalar_tensor_tensor(k.res[:, dt, :], k.res[:, dt, :], scale_residual, k.bank[dt % 2][:, :],
                                         ALU.mult, ALU.add).then_inc(product_added, 1)


def attention(k, units, outs, strip_loads=(), strips_per=1):
    n_units = len(units)
    last_of_pair = {}
    last_of_strip = {}
    for i, u in enumerate(units):
        last_of_pair[u["pair"]] = i
        if u["strip"] is not None:
            last_of_strip[u["strip"]] = i
    with memory(k, att_p=(2, SEQ), att_t=(2, SEQ), att_s=(2, 4)) as (prob, probt, small), \
            stage(k, "scores_ready", "biased", "exp_ready", "probs_ready", "turned", "turned_copied", "unit_done",
                  "pair_copied", "vector_order", "strip_even", "strip_odd") as (
                block, scores_ready, biased, exp_ready, probs_ready, turned, turned_copied, unit_done, pair_copied,
                order, strip_even, strip_odd):
        strip_sem = (strip_even, strip_odd)

        @block.sync
        def _(sp):
            for s, (dst, src) in enumerate(strip_loads):
                if s >= 2:
                    sp.wait_ge(biased, last_of_strip[s - 2] + 1)
                sp.dma_start(dst, src).then_inc(strip_sem[s % 2], 16)

        @block.tensor
        def _(pe):
            for i in range(n_units + 2):
                if i < n_units:
                    u = units[i]
                    if i >= 2:
                        pe.wait_ge(biased, i - 1)
                    pe.matmul(k.bank[i % 2][:, 0:u["n"]], u["q"], u["keys"], start=True, stop=True).then_inc(
                        scores_ready, 1)
                if 1 <= i <= n_units:
                    u = units[i - 1]
                    pe.wait_ge(probs_ready, i)
                    if i >= 3:
                        pe.wait_ge(turned_copied, i - 2)
                    for j in range(u["n"] // 128):
                        last = pe.transpose(k.bank[2 + (i - 1) % 2][:, 128 * j:128 * j + 128],
                                            prob[:, (i - 1) % 2, 128 * j:128 * j + 128], const(k, "ident"))
                    last.then_inc(turned, 1)
                if i >= 2:
                    u = units[i - 2]
                    pe.wait_ge(turned_copied, i - 1)
                    if u["pair"] >= 2:
                        pe.wait_ge(pair_copied, u["pair"] - 1)
                    nj = u["n"] // 128
                    for j in range(nj):
                        last = pe.matmul(k.bank[4 + u["pair"] % 2][u["rows"], u["cols"]], u["values"][j],
                                         probt[:, (i - 2) % 2, 128 * j:128 * j + 128], start=j == 0, stop=j == nj - 1)
                    last.then_inc(unit_done, 1)

        @block.scalar
        def _(act):
            for i in range(n_units + 1):
                if i < n_units:
                    u = units[i]
                    act.wait_ge(biased, i + 1)
                    act.activation(prob[:, i % 2, 0:u["n"]], prob[:, i % 2, 0:u["n"]], ACT.Exp,
                                   bias=small[:, i % 2, 0:1], accum_out=small[:, i % 2, 1:2]).then_inc(exp_ready, 1)
                if i >= 1:
                    u = units[i - 1]
                    act.wait_ge(turned, i)
                    if i >= 3:
                        act.wait_ge(unit_done, i - 2)
                    act.activation(probt[:, (i - 1) % 2, 0:u["n"]], k.bank[2 + (i - 1) % 2][:, 0:u["n"]],
                                   ACT.Copy).then_inc(turned_copied, 1)

        @block.vector
        def _(dve):
            step = Order(dve, order)
            waited = -1
            for i in range(n_units + 1):
                if i < n_units:
                    u = units[i]
                    p = prob[:, i % 2, 0:u["n"]]
                    dve.wait_ge(scores_ready, i + 1)
                    if i >= 2:
                        dve.wait_ge(turned, i - 1)
                    if u["strip"] is not None and u["strip"] != waited:
                        waited = u["strip"]
                        dve.wait_ge(strip_sem[waited % 2], 16 * (waited // 2 + 1))
                    s = k.bank[i % 2][:, 0:u["n"]]
                    if u["bias"] is None:
                        step(dve.tensor_scalar(p, s, u["scale"], None, ALU.mult))
                    else:
                        step(dve.scalar_tensor_tensor(p, s, u["scale"], u["bias"], ALU.mult, ALU.add))
                    if u["select"] is not None:
                        step(dve.tensor_tensor(p, p, u["select"], ALU.add))
                    dve.tensor_reduce(small[:, i % 2, 0:1], p, AX.X, ALU.max, negate=True).then_inc(biased, 1)
                if i >= 1:
                    u = units[i - 1]
                    b = (i - 1) % 2
                    dve.wait_ge(exp_ready, i)
                    step(dve.reciprocal(small[:, b, 2:3], small[:, b, 1:2]))
                    dve.tensor_scalar(prob[:, b, 0:u["n"]], prob[:, b, 0:u["n"]], small[:, b, 2:3], None,
                                      ALU.mult).then_inc(probs_ready, 1)
                    if last_of_pair[u["pair"]] == i - 1:
                        pair = u["pair"]
                        if pair >= 1:
                            dve.wait_ge(unit_done, last_of_pair[pair - 1] + 1)
                            dve.tensor_copy(outs[pair - 1], k.bank[4 + (pair - 1) % 2][:, :]).then_inc(pair_copied, 1)
            pair = units[-1]["pair"]
            dve.wait_ge(unit_done, n_units)
            dve.tensor_copy(outs[pair], k.bank[4 + pair % 2][:, :]).then_inc(pair_copied, 1)




def distance_bias(k, bias_dram):
    with memory(k, rows=(1024,), tab=(8,), bias_rows=(1024,)) as (rows, tab, out), \
            stage(k, "rows_in", "bias_ready", "bias_copied", "bias_stored") as (
                block, rows_in, bias_ready, bias_copied, bias_stored):
        @block.sync
        def _(sp):
            sp.dma_start(rows[0:34, :], k.dram["dist_rows"]).then_inc(rows_in, 16)
            sp.dma_start(tab[0:34, :], k.dram["rpb"]).then_inc(rows_in, 16)
            sp.wait_ge(bias_copied, 2)
            for h in range(8):
                row = out[h:h + 1, :].rearrange("p (a x) -> p a x", a=1).to_broadcast([1, 128, 1024])
                sp.dma_start(bias_dram[h:h + 1, :, :], row).then_inc(bias_stored, 16)
            sp.wait_ge(bias_stored, 128)

        @block.tensor
        def _(pe):
            pe.wait_ge(rows_in, 32)
            for j in range(2):
                pe.matmul(k.bank[j][0:8, :], tab[0:34, :], rows[0:34, 512 * j:512 * j + 512], start=True,
                          stop=True).then_inc(bias_ready, 1)

        @block.vector
        def _(dve):
            for j in range(2):
                dve.wait_ge(bias_ready, j + 1)
                dve.tensor_copy(out[0:8, 512 * j:512 * j + 512], k.bank[j][0:8, :]).then_inc(bias_copied, 1)


def head_norm(k, jobs, n=SEQ):
    blk = const(k, "blk64")
    with memory(k, hn_sq=(2, n), hn_r=(2, n)) as (sq, r), \
            stage(k, "squared", "summed", "log_ready", "rstd_ready", "finished", "vector_order") as (
                block, squared, summed, log_ready, rstd_ready, finished, order):
        @block.tensor
        def _(pe):
            for i, job in enumerate(jobs):
                pe.wait_ge(squared, i + 1)
                if i >= 2:
                    pe.wait_ge(log_ready, i - 1)
                pe.matmul(k.bank[i % 2][:, 0:n], blk, sq[:, i % 2, :], start=True, stop=True).then_inc(summed, 1)

        @block.scalar
        def _(act):
            for i in range(len(jobs) + 1):
                if i < len(jobs):
                    if i >= 2:
                        act.wait_ge(summed, i - 1)
                    act.activation(sq[:, i % 2, :], jobs[i]["src"], ACT.Square).then_inc(squared, 1)
                if i >= 1:
                    b = (i - 1) % 2
                    act.wait_ge(summed, i)
                    if i >= 3:
                        act.wait_ge(finished, i - 2)
                    act.activation(r[:, b, :], k.bank[b][:, 0:n], ACT.Ln, scale=jobs[i - 1]["scale"],
                                   bias=jobs[i - 1]["eps"]).then_inc(log_ready, 1)
                    act.wait_ge(log_ready, i)
                    act.activation(r[:, b, :], r[:, b, :], ACT.Exp, scale=-0.5).then_inc(rstd_ready, 1)

        @block.vector
        def _(dve):
            step = Order(dve, order)
            for i, job in enumerate(jobs):
                dve.wait_ge(rstd_ready, i + 1)
                job["finish"](dve, step, r[:, i % 2, :]).then_inc(finished, 1)
                dve.wait_ge(finished, i + 1)


def gained(src, gain):
    def finish(dve, step, rstd):
        step(dve.tensor_tensor(src, src, rstd, ALU.mult))
        return dve.tensor_scalar(src, src, gain, None, ALU.mult)
    return finish


def turn(k, jobs):
    with stage(k, "turned", "turned_copied") as (block, turned, turned_copied):
        @block.tensor
        def _(pe):
            for i, (_, srcs) in enumerate(jobs):
                if i >= 2:
                    pe.wait_ge(turned_copied, i - 1)
                for j, s in enumerate(srcs):
                    last = pe.transpose(k.bank[i % 2][:, 128 * j:128 * j + 128], s, const(k, "ident"))
                last.then_inc(turned, 1)

        @block.vector
        def _(dve):
            for i, (out, srcs) in enumerate(jobs):
                dve.wait_ge(turned, i + 1)
                dve.tensor_copy(out, k.bank[i % 2][:, 0:128 * len(srcs)]).then_inc(turned_copied, 1)


def select_keys(k, pj, lowt, select):
    heads, keep = 8, 128
    with memory(k, ix_rel=(2, SEQ), ix_score=(SEQ,), ix_top=(8,)) as (rel, score, top), \
            stage(k, "score_ready", "rel_ready", "rel_used", "bank_read", "vector_order") as (
                block, score_ready, rel_ready, rel_used, bank_read, order):
        units = [(i, h) for i in (1, 2, 3) for h in range(heads)]

        @block.tensor
        def _(pe):
            for u, (i, h) in enumerate(units):
                if u >= 2:
                    pe.wait_ge(rel_ready, u - 1)
                rows = slice(32 * (h % 4), 32 * (h % 4) + 32)
                pe.matmul(k.bank[u % 2][:, 0:128 * i + 128],
                          pj[rows, T1["iq"] + h // 4, 128 * i:128 * i + 128],
                          pj[rows, T1["ik"], 0:128 * i + 128], start=True, stop=True).then_inc(score_ready, 1)

        @block.scalar
        def _(act):
            for u, (i, h) in enumerate(units):
                act.wait_ge(score_ready, u + 1)
                if u >= 2:
                    act.wait_ge(rel_used, u - 1)
                n = 128 * i + 128
                act.activation(rel[:, u % 2, 0:n], k.bank[u % 2][:, 0:n], ACT.Relu, scale=32 ** -0.5).then_inc(
                    rel_ready, 1)

        @block.vector
        def _(dve):
            step = Order(dve, order)
            for u, (i, h) in enumerate(units):
                n = 128 * i + 128
                s = score[:, 0:n]
                dve.wait_ge(rel_ready, u + 1)
                weight = lowt[:, i, 112 + h:113 + h]
                if h == 0:
                    dve.tensor_scalar(s, rel[:, u % 2, 0:n], weight, None, ALU.mult).then_inc(rel_used, 1)
                else:
                    dve.scalar_tensor_tensor(s, rel[:, u % 2, 0:n], weight, s, ALU.mult, ALU.add).then_inc(
                        rel_used, 1)
                dve.wait_ge(rel_used, u + 1)
                if h < heads - 1:
                    continue
                step(dve.tensor_scalar(s, s, heads ** -0.5, None, ALU.mult))
                step(dve.tensor_tensor(score[:, n - 128:n], score[:, n - 128:n], const(k, "future"), ALU.add))
                for _ in range(keep // 8):
                    step(dve.max(top[:, :], s))
                    step(dve.match_replace(s, top[:, :], s, TAKEN))
                step(dve.tensor_scalar(select[:, i - 1, 0:n], s, TAKEN / 2, MASKED, ALU.is_gt, ALU.mult))


def mixers_ab(k, pj, av, bias_dram):
    yb = k.yb
    kv = pj[:, T1["ckv"], :]
    g = k.par1[:, P1["kv_gain"]:P1["kv_gain"] + 1]
    head_norm(k, [dict(src=kv, scale=1.0 / 64, eps=k.eps[:, 1:2], finish=gained(kv, g))])
    with memory(k, low_t=(4, 128), kv_t=(4, 128), strips=(2, STRIP)) as (lowt, kvt, strips):
        tiles = [slice(128 * t, 128 * t + 128) for t in range(4)]
        turn(k, [(lowt[:, :, :], [pj[:, T1["low"], t] for t in tiles]),
                 (kvt[:, :, :], [pj[:, T1["ckv"], t] for t in tiles])])
        select = k.res[:, 0:3, :]
        select_keys(k, pj, lowt, select)
        distance_bias(k, bias_dram)
        units, loads = [], []
        for head in range(8):
            b, h = divmod(head, 4)
            rows = slice(64 * (h % 2), 64 * (h % 2) + 64)
            loads.append((strips[:, head % 2, :],
                          bass.AP(tensor=bias_dram.tensor, offset=128 * 1024 * head + 127,
                                  ap=[[1023, 128], [1, STRIP]])))
            for i in range(4):
                n = 128 * i + 128
                q = pj[rows, (T1["aq"], T1["bq"])[b] + h // 2, tiles[i]]
                if b == 0:
                    keys = pj[rows, T1["ak"] + h // 2, 0:n]
                    values = [av[:, j, 64 * h:64 * h + 64] for j in range(i + 1)]
                else:
                    keys = pj[rows, T1["ckv"], 0:n]
                    values = [kvt[:, j, 0:64] for j in range(i + 1)]
                units.append(dict(q=q, keys=keys, n=n, scale=0.125, strip=head, values=values, pair=2 * b + h // 2,
                                  bias=strips[:, head % 2, 384 - 128 * i:384 - 128 * i + n],
                                  select=select[:, i - 1, 0:n] if b and i else None, rows=rows, cols=tiles[i]))
        attention(k, units, [yb[:, 0, :], yb[:, 1, :], yb[:, 2, :], yb[:, 3, :]], strip_loads=loads)
    small_products(k, [(yb[:, 2 + p, :], k.mats1[:, 256 + 128 * p:384 + 128 * p], yb[:, 2 + p, :], None)
                       for p in range(2)])


def small_products(k, jobs):
    with stage(k, "product_ready", "product_copied") as (block, product_ready, product_copied):
        @block.tensor
        def _(pe):
            for i, (_, lhs, rhs, _) in enumerate(jobs):
                if i >= 2:
                    pe.wait_ge(product_copied, i - 1)
                pe.matmul(k.bank[i % 2][:, 0:rhs.shape[-1]], lhs, rhs, start=True, stop=True).then_inc(
                    product_ready, 1)

        @block.vector
        def _(dve):
            for i, (out, _, rhs, scale) in enumerate(jobs):
                dve.wait_ge(product_ready, i + 1)
                b = k.bank[i % 2][:, 0:rhs.shape[-1]]
                if scale is None:
                    dve.tensor_copy(out, b).then_inc(product_copied, 1)
                else:
                    dve.tensor_scalar(out, b, scale, None, ALU.mult).then_inc(product_copied, 1)


def mixer_c(k, pj, cv):
    p1 = lambda n, j=0: k.par1[:, P1[n] + j:P1[n] + j + 1]
    q, key = pj[:, T1["cq"], :], pj[:, T1["ck"], :]
    chunked = lambda ap: ap.rearrange("p (c t) -> p c t", t=64)
    with memory(k, cum=(SEQ,), dec=(8,), e_tmp=(SEQ,), qd=(SEQ,), ki=(SEQ,), ku=(SEQ,), kut=(4, 128), att=(4, 4, 128),
                st=(8, 256)) as (cum, dec, tmp, qd, ki, ku, kut, att, st):
        with stage(k, "gate_ready", "abs_ready", "exp_ready", "log_ready", "cum_ready", "decays_ready",
                   "vector_order") as (block, gate_ready, abs_ready, exp_ready, log_ready, cum_ready, decays_ready,
                                       order):
            @block.tensor
            def _(pe):
                pe.matmul(k.bank[0][:, :], k.mats1[96:112, 0:128], pj[96:112, T1["low"], :], start=True,
                          stop=True).then_inc(gate_ready, 1)

            @block.scalar
            def _(act):
                act.wait_ge(abs_ready, 1)
                act.activation(tmp[:, :], tmp[:, :], ACT.Exp, scale=-1.0).then_inc(exp_ready, 1)
                act.wait_ge(exp_ready, 1)
                act.activation(tmp[:, :], tmp[:, :], ACT.Ln, bias=k.eps[:, 3:4]).then_inc(log_ready, 1)
                act.wait_ge(cum_ready, 1)
                act.activation(qd[:, :], cum[:, :], ACT.Exp).then_inc(decays_ready, 1)
                act.activation(ki[:, :], cum[:, :], ACT.Exp, scale=-1.0).then_inc(decays_ready, 1)
                act.activation(dec[:, :], chunked(cum[:, :])[:, :, 63], ACT.Exp).then_inc(decays_ready, 1)
                act.wait_ge(cum_ready, 2)
                act.activation(ku[:, :], tmp[:, :], ACT.Exp).then_inc(decays_ready, 1)

            @block.vector
            def _(dve):
                step = Order(dve, order)
                dve.wait_ge(gate_ready, 1)
                step(dve.tensor_scalar(cum[:, :], k.bank[0][:, :], p1("a_bias"), None, ALU.add))
                step(dve.tensor_scalar(ku[:, :], cum[:, :], -1.0, None, ALU.mult))
                dve.tensor_tensor(tmp[:, :], cum[:, :], ku[:, :], ALU.max).then_inc(abs_ready, 1)
                dve.wait_ge(abs_ready, 1)
                step(dve.tensor_scalar(ku[:, :], cum[:, :], 0.0, 1.0 / 16, ALU.min, ALU.mult))
                dve.wait_ge(log_ready, 1)
                step(dve.scalar_tensor_tensor(ku[:, :], tmp[:, :], -1.0 / 16, ku[:, :], ALU.mult, ALU.add))
                dve.tensor_tensor_scan(cum[:, :], const(k, "reset64"), ku[:, :], 0.0, ALU.mult, ALU.add).then_inc(
                    cum_ready, 1)
                dve.wait_ge(cum_ready, 1)
                last = chunked(cum[:, :])[:, :, 63:64].to_broadcast([128, 8, 64])
                dve.tensor_tensor(chunked(tmp[:, :]), last, chunked(cum[:, :]), ALU.subtract).then_inc(cum_ready, 1)
                dve.wait_ge(decays_ready, 4)
                step(dve.scalar_tensor_tensor(qd[:, :], q, 32 ** -0.5, qd[:, :], ALU.mult, ALU.mult))
                step(dve.tensor_tensor(ki[:, :], key, ki[:, :], ALU.mult))
                step(dve.tensor_tensor(ku[:, :], key, ku[:, :], ALU.mult))
                step(dve.memset(st[:, 0, :], 0.0))
        update_bank = lambda n: 2 * (n % 2) + n // 4
        update_cols = lambda n: slice(256 * (n // 2 % 2), 256 * (n // 2 % 2) + 256)
        turn(k, [(kut[:, :, :], [ku[:, 128 * t:128 * t + 128] for t in range(4)])])
        with stage(k, "att_ready", "att_masked", "update_ready", "update_masked", "states_ready", "out_ready",
                   "out_copied", "vector_order") as (block, att_ready, att_masked, update_ready, update_masked,
                                                     states_ready, out_ready, out_copied, order):
            @block.tensor
            def _(pe):
                for n in range(8):
                    rows = slice(64 * (n % 2), 64 * (n % 2) + 64)
                    pe.matmul(k.bank[update_bank(n)][:, update_cols(n)], kut[rows, n // 2, :], cv[rows, n // 2, :],
                              start=True, stop=True).then_inc(update_ready, 1)
                for h in range(4):
                    rows = slice(32 * h, 32 * h + 32)
                    for t in range(4):
                        c = slice(128 * t, 128 * t + 128)
                        last = pe.matmul(k.bank[4 + h][:, c], ki[rows, c], qd[rows, c], start=True, stop=True)
                    last.then_inc(att_ready, 1)
                pe.wait_ge(states_ready, 1)
                pe.wait_ge(att_masked, 4)
                for p in range(2):
                    out = k.bank[p]
                    for n in range(8):
                        pe.matmul(out[:, 64 * n:64 * n + 64], st[:, n, 128 * p:128 * p + 128],
                                  qd[:, 64 * n:64 * n + 64], start=n == 0, stop=False, skip_group_check=True)
                    for h in (2 * p, 2 * p + 1):
                        rows = slice(64 * (h % 2), 64 * (h % 2) + 64)
                        for t in range(4):
                            last = pe.matmul(out[rows, 128 * t:128 * t + 128], cv[:, t, 64 * h:64 * h + 64],
                                             att[:, h, t, :], start=False, stop=(h % 2 == 1 and t == 3),
                                             skip_group_check=True)
                    last.then_inc(out_ready, 1)

            @block.vector
            def _(dve):
                step = Order(dve, order)
                heads = const(k, "gla_heads")
                for n in range(8):
                    dve.wait_ge(update_ready, 8)
                    upd = k.bank[update_bank(n)][:, update_cols(n)]
                    if n < 7:
                        step(dve.tensor_tensor(st[:, n + 1, :], upd, heads, ALU.mult))
                        step(dve.scalar_tensor_tensor(st[:, n + 1, :], st[:, n, :], dec[:, n:n + 1], st[:, n + 1, :],
                                                      ALU.mult, ALU.add))
                dve.tensor_copy(tmp[:, 0:8], dec[:, :]).then_inc(states_ready, 1)
                mask = const(k, "gla_mask").rearrange("p (a t) -> p a t", a=1).to_broadcast([128, 4, 128])
                for h in range(4):
                    dve.wait_ge(att_ready, h + 1)
                    dve.tensor_tensor(att[:, h, :, :], k.bank[4 + h][:, :].rearrange("p (a t) -> p a t", a=4), mask,
                                      ALU.mult).then_inc(att_masked, 1)
                for p in range(2):
                    dve.wait_ge(out_ready, p + 1)
                    dve.tensor_copy(k.yb[:, 4 + p, :], k.bank[p][:, :]).then_inc(out_copied, 1)
    with stage(k, "silu_ready") as (block, silu_ready):
        @block.scalar
        def _(act):
            for p in range(2):
                g = pj[:, T1["cg"] + p, :]
                act.activation(g, g, ACT.Silu).then_inc(silu_ready, 1)

    def finish(p):
        y = k.yb[:, 4 + p, :]

        def run(dve, step, rstd):
            step(dve.tensor_tensor(y, y, rstd, ALU.mult))
            return dve.scalar_tensor_tensor(y, y, p1("c_norm", p), pj[:, T1["cg"] + p, :], ALU.mult, ALU.mult)
        return run

    head_norm(k, [dict(src=k.yb[:, 4 + p, :], scale=1.0 / 64, eps=k.eps[:, 1:2], finish=finish(p))
                  for p in range(2)])


def mixer_d(k, pj):
    p1 = lambda n, j=0: k.par1[:, P1[n] + j:P1[n] + j + 1]
    low = pj[:, T1["low"], :]
    tiled = lambda ap: ap.rearrange("p (c t) -> p c t", t=128)
    R, K_, V = T1["dr"], T1["dk"], T1["dv"]
    wk = [pj[:, n, :] for n in range(T1["low"])]
    rs = [k.res[:, n, :] for n in range(KT)]
    lg, cw, ic, ga = wk[0:2], wk[2:4], wk[4:6], wk[6:8]
    kk, bonus = rs[0:2], rs[2:4]
    at, bt = rs[4:6], rs[6:8]
    tmp, tmp2 = wk[8], wk[9]
    rt, kt = pj[:, R:R + 2, :], pj[:, K_:K_ + 2, :]
    cg = [pj[:, n, :] for n in range(T1["cq"], T1["cq"] + 4)]
    sh = cg[0]
    e_dn, e_up, e_a = cg[1], cg[2], cg[3]
    with memory(k, tl=(SEQ,), zs=(2, 4)) as (tl, zs):
        with stage(k, "vector_order") as (block, order):
            @block.vector
            def _(dve):
                step = Order(dve, order)
                for j, t in enumerate([R, R + 1, K_, K_ + 1, V, V + 1, T1["low"]]):
                    z = pj[:, t, :]
                    step(dve.tensor_tensor(sh[:, 1:SEQ], z[:, 0:SEQ - 1], z[:, 1:SEQ], ALU.subtract))
                    step(dve.tensor_scalar(sh[:, 0:1], z[:, 0:1], -1.0, None, ALU.mult))
                    step(dve.scalar_tensor_tensor(z, sh, p1("mu", j), z, ALU.mult, ALU.add))
        with stage(k, "inner_ready", "low_ready", "sigmoids_ready", "gates_copied", "vector_order") as (
                block, inner_ready, low_ready, sigmoids_ready, gates_copied, order):
            @block.scalar
            def _(act):
                act.activation(tl[0:16, :], low[0:16, :], ACT.Tanh).then_inc(inner_ready, 1)
                act.activation(tl[32:48, :], low[32:48, :], ACT.Copy).then_inc(inner_ready, 1)
                act.activation(tl[64:96, :], low[64:96, :], ACT.Sigmoid).then_inc(inner_ready, 1)
                act.wait_ge(low_ready, 6)
                for p in range(2):
                    act.activation(lg[p], k.bank[p][:, :], ACT.Sigmoid, bias=p1("w0", p)).then_inc(sigmoids_ready, 1)
                    act.activation(ic[p], k.bank[2 + p][:, :], ACT.Sigmoid, bias=p1("a0", p)).then_inc(
                        sigmoids_ready, 1)

            @block.tensor
            def _(pe):
                pe.wait_ge(inner_ready, 3)
                for m, rows in enumerate((slice(0, 16), slice(32, 48), slice(64, 96))):
                    for p in range(2):
                        pe.matmul(k.bank[2 * m + p][:, :], k.mats1[rows, 128 * p:128 * p + 128], tl[rows, :],
                                  start=True, stop=True).then_inc(low_ready, 1)

            @block.vector
            def _(dve):
                step = Order(dve, order)
                dve.wait_ge(low_ready, 6)
                for p in range(2):
                    step(dve.tensor_copy(ga[p], k.bank[4 + p][:, :]))
                dve.wait_ge(sigmoids_ready, 4)
                for p in range(2):
                    step(dve.tensor_scalar(lg[p], lg[p], -math.exp(-0.5), None, ALU.mult))
                    step(dve.tensor_tensor_scan(cw[p], const(k, "reset128"), lg[p], 0.0, ALU.mult, ALU.add))
                    step(dve.tensor_scalar(kk[p], pj[:, K_ + p, :], p1("k_k", p), None, ALU.mult))
                    step(dve.tensor_scalar(tmp, ic[p], 1.0, p1("k_a", p), ALU.subtract, ALU.mult))
                    step(dve.scalar_tensor_tensor(pj[:, K_ + p, :], tmp, 1.0, pj[:, K_ + p, :], ALU.add, ALU.mult))
                    step(dve.scalar_tensor_tensor(bonus[p], pj[:, R + p, :], p1("r_k", p), pj[:, K_ + p, :],
                                                  ALU.mult, ALU.mult))
        with stage(k, "squared", "summed", "norm_ready", "exponent_ready", "exps_ready", "exps_used",
                   "scales_ready", "vector_order") as (block, squared, summed, norm_ready, exponent_ready,
                                                       exps_ready, exps_used, scales_ready, order):
            @block.tensor
            def _(pe):
                for p in range(2):
                    pe.matmul(k.bank[2 + p][:, :], const(k, "blk64"), bonus[p], start=True, stop=True)
                for p in range(2):
                    pe.wait_ge(squared, p + 1)
                    pe.matmul(k.bank[p][:, :], const(k, "blk64"), (tl[:, :], sh)[p], start=True, stop=True).then_inc(
                        summed, 1)

            @block.scalar
            def _(act):
                for p in range(2):
                    act.activation((tl[:, :], sh)[p], kk[p], ACT.Square).then_inc(squared, 1)
                for p in range(2):
                    act.wait_ge(summed, p + 1)
                    act.activation((tl[:, :], sh)[p], k.bank[p][:, :], ACT.Sqrt).then_inc(norm_ready, 1)
                for p in range(2):
                    act.wait_ge(exponent_ready, 3 * p + 3)
                    act.activation(e_dn, cw[p], ACT.Exp).then_inc(exps_ready, 1)
                    act.activation(e_up, cw[p], ACT.Exp, scale=-1.0).then_inc(exps_ready, 1)
                    act.activation(e_a, lg[p], ACT.Exp).then_inc(exps_ready, 1)
                    act.activation(zs[:, p, :], zs[:, p, :], ACT.Exp).then_inc(exps_ready, 1)
                    act.wait_ge(exps_used, p + 1)

            @block.vector
            def _(dve):
                step = Order(dve, order)
                dve.wait_ge(summed, 2)
                for p in range(2):
                    nrm = (tl[:, :], sh)[p]
                    step(dve.tensor_tensor(bonus[p], k.bank[2 + p][:, :], pj[:, V + p, :], ALU.mult))
                    dve.wait_ge(norm_ready, p + 1)
                    step(dve.tensor_scalar(nrm, nrm, 1e-12, None, ALU.max))
                    step(dve.reciprocal(nrm, nrm))
                    step(dve.tensor_tensor(kk[p], kk[p], nrm, ALU.mult))
                for p in range(2):
                    c = tiled(cw[p])
                    step(dve.tensor_tensor(zs[:, p, :], c[:, :, 127], c[:, :, 63], ALU.subtract))
                    dve.tensor_tensor(zs[:, p, 0:3], zs[:, p, 0:3], c[:, 1:4, 63], ALU.add).then_inc(
                        exponent_ready, 1)
                    step(dve.tensor_copy(tmp2[:, 0:4], c[:, :, 63]))
                    mid = tmp2[:, 0:4].rearrange("p (c t) -> p c t", t=1).to_broadcast([128, 4, 128])
                    dve.tensor_tensor(c, c, mid, ALU.subtract).then_inc(exponent_ready, 1)
                    dve.wait_ge(exponent_ready, 3 * p + 2)
                    dve.tensor_tensor(lg[p], cw[p], lg[p], ALU.subtract).then_inc(exponent_ready, 1)
                    dve.wait_ge(exps_ready, 4 * p + 4)
                    step(dve.scalar_tensor_tensor(at[p], kk[p], -1.0, e_a, ALU.mult, ALU.mult))
                    step(dve.tensor_tensor(bt[p], kk[p], ic[p], ALU.mult))
                    step(dve.tensor_tensor(bt[p], bt[p], e_up, ALU.mult))
                    step(dve.tensor_tensor(kt[:, p, :], kt[:, p, :], e_up, ALU.mult))
                    dve.tensor_tensor(rt[:, p, :], rt[:, p, :], e_dn, ALU.mult).then_inc(exps_used, 1)
                    dve.wait_ge(exps_used, p + 1)
        vt = pj[:, 0:2, :].rearrange("p a (c n) -> p (a c) n", c=2)
        btt = pj[:, 2:4, :].rearrange("p a (c n) -> p (a c) n", c=2)
        ktt = pj[:, 4:6, :].rearrange("p a (c n) -> p (a c) n", c=2)
        tiles = [slice(128 * t, 128 * t + 128) for t in range(4)]
        jobs = []
        for dst, src in ((vt, [pj[:, V + p, :] for p in range(2)]), (btt, bt), (ktt, [kt[:, 0, :], kt[:, 1, :]])):
            for c in range(0, 4, 2):
                jobs.append((dst[:, c:c + 2, :].rearrange("p c n -> p (c n)"),
                             [src[p][:, tiles[c + e]] for e in range(2) for p in range(2)]))
        turn(k, jobs)
        delta_chunks(k, at, bt, kt, rt, vt, btt, ktt, zs, cg, [wk[8], wk[9], rs[0], rs[1]])
        y = [k.yb[:, 6, :], k.yb[:, 7, :]]
        with stage(k, "mean_ready", "vector_order") as (block, mean_ready, order):
            @block.tensor
            def _(pe):
                for p in range(2):
                    pe.matmul(k.bank[p][:, :], const(k, "blk64"), y[p], start=True, stop=True).then_inc(
                        mean_ready, 1)

            @block.vector
            def _(dve):
                step = Order(dve, order)
                for p in range(2):
                    dve.wait_ge(mean_ready, p + 1)
                    step(dve.scalar_tensor_tensor(y[p], k.bank[p][:, :], -1.0 / 64, y[p], ALU.mult, ALU.add))

        def finish(p):
            def run(dve, step, rstd):
                step(dve.tensor_tensor(y[p], y[p], rstd, ALU.mult))
                step(dve.tensor_scalar(y[p], y[p], p1("gn_w", p), p1("gn_b", p), ALU.mult, ALU.add))
                step(dve.tensor_tensor(y[p], y[p], bonus[p], ALU.add))
                return dve.tensor_tensor(y[p], y[p], ga[p], ALU.mult)
            return run

        head_norm(k, [dict(src=y[p], scale=1.0 / 64, eps=k.eps[:, 2:3], finish=finish(p)) for p in range(2)])


def delta_chunks(k, at, bt, kt, rt, vt, btt, ktt, zs, free_a, free_b):
    four = lambda ap: ap.rearrange("p (h t) -> p h t", h=4)
    wide = lambda name, n: const(k, name).rearrange("p (a t) -> p a t", a=1).to_broadcast([128, n, 128])
    rows = [slice(64 * (h % 2), 64 * (h % 2) + 64) for h in range(4)]
    quarter = [slice(128 * h, 128 * h + 128) for h in range(4)]
    ed, el, md, nt = (four(x) for x in free_a)
    bi, ki, s1, s2 = (four(x) for x in free_b)
    bank = k.bank
    with memory(k, d_s3=(4, 128), d_s4=(4, 128), d_s5=(4, 128), d_pq=(4, 256), d_pq2=(4, 256), d_r=(256,),
                d_u=(256,), d_z=(2, 64)) as (s3, s4, s5, pq, pq2, rr, uu, z), \
            stage(k, "products_done", "evacuated", "vector_order") as (block, products_done, evacuated, order):
        x, q = pq2[:, :, 0:128], pq2[:, :, 128:256]

        @block.tensor
        def _(pe):
            sets = [0]

            def done(last):
                last.then_inc(products_done, 1)
                sets[0] += 1
                pe.wait_ge(evacuated, sets[0])

            def by_head(b, left, right):
                for h in range(4):
                    last = pe.matmul(bank[b][:, quarter[h]], left[:, h, :], right[:, h, :], start=True, stop=True)
                return last

            def by_head_wide(left, right):
                for h in range(4):
                    last = pe.matmul(bank[3 + h // 2][:, 256 * (h % 2):256 * (h % 2) + 256], left[:, h, :],
                                     right[:, h, :], start=True, stop=True)
                return last

            for c in range(4):
                cols = quarter[c]
                for h in range(4):
                    p, r = h // 2, rows[h]
                    for m, left in enumerate((bt[p], kt[:, p, :])):
                        b = bank[2 * m + h % 2]
                        pe.matmul(b[:, 256 * p:256 * p + 128], left[r, cols], at[p][r, cols], start=True, stop=True)
                        pe.matmul(b[:, 256 * p + 128:256 * p + 256], left[r, cols], rt[r, p, cols], start=True,
                                  stop=True)
                    last = pe.matmul(bank[4 + h % 2][:, 128 * p:128 * p + 128], at[p][r, cols], bt[p][r, cols],
                                     start=True, stop=True)
                done(last)
                by_head(0, md, el)
                by_head(1, md, ed)
                done(by_head(2, ed, md))
                by_head(0, s2, s1)
                by_head(1, s1, s2)
                done(by_head_wide(s2, pq))
                by_head(1, s3, s4)
                done(by_head_wide(s4, pq2))
                done(by_head_wide(s2, pq))
                for h in range(4):
                    last = pe.transpose(bank[0][:, quarter[h]], pq2[:, h, 128:256], const(k, "ident"))
                done(last)
                by_head(1, s5, q)
                done(by_head(2, q, s5))
                done(by_head(1, s1, s2))
                for left in (s3, s2, s5):
                    done(by_head(0, left, x))
                for h in range(4):
                    p, r = h // 2, rows[h]
                    o = bank[1 + h % 2][:, 64 * p:64 * p + 64]
                    if c:
                        pe.matmul(o, at[p][r, cols], z[r, p, :], start=True, stop=False)
                    last = pe.matmul(o, nt[:, h, :], vt[:, c, 64 * h:64 * h + 64], start=not c, stop=True)
                done(last)
                for h in range(4):
                    hs = slice(64 * h, 64 * h + 64)
                    last = pe.matmul(bank[3][:, hs], x[:, h, :], rr[:, hs], start=True, stop=True)
                done(last)
                for h in range(4):
                    p, r = h // 2, rows[h]
                    us, vs = uu[:, 64 * h:64 * h + 64], vt[:, c, 64 * h:64 * h + 64]
                    o = bank[5 + h % 2][r, 128 * p:128 * p + 128]
                    if c:
                        pe.matmul(o, z[r, p, :], rt[r, p, cols], start=True, stop=False)
                    pe.matmul(o, us, bi[:, h, :], start=not c, stop=False)
                    last = pe.matmul(o, vs, ki[:, h, :], start=False, stop=True)
                    if c < 3:
                        o = bank[7][r, 64 * p:64 * p + 64]
                        pe.matmul(o, btt[:, c, 64 * h:64 * h + 64], us, start=True, stop=False)
                        last = pe.matmul(o, ktt[:, c, 64 * h:64 * h + 64], vs, start=False, stop=True)
                done(last)

        @block.vector
        def _(dve):
            step = Order(dve, order)
            sets = [0]

            def products():
                sets[0] += 1
                dve.wait_ge(products_done, sets[0])

            def done(last):
                last.then_inc(evacuated, 1)
                dve.wait_ge(evacuated, sets[0])

            def grow(dst, src):
                for p in range(2):
                    a = slice(2 * p, 2 * p + 2)
                    last = dve.tensor_tensor(dst[:, a, :].rearrange("p h t -> p (h t)"),
                                             src[:, a, :].rearrange("p h t -> p (h t)"), bank[3 + p][:, :], ALU.add)
                    if p == 0:
                        step(last)
                return last

            for c in range(4):
                products()
                for p in range(2):
                    b = bank[p][:, :].rearrange("p (h g t) -> p h g t", h=2, g=2)
                    n = bank[2 + p][:, :].rearrange("p (h g t) -> p h g t", h=2, g=2)
                    hs = slice(p, 4, 2)
                    step(dve.tensor_tensor(ed[:, hs, :], b[:, :, 0, :], wide("up_same", 2), ALU.mult))
                    step(dve.tensor_tensor(el[:, hs, :], b[:, :, 0, :], wide("up_other", 2), ALU.mult))
                    step(dve.tensor_tensor(bi[:, hs, :], b[:, :, 1, :], wide("up_diag", 2), ALU.mult))
                    step(dve.tensor_tensor(nt[:, hs, :], n[:, :, 0, :], wide("up", 2), ALU.mult))
                    step(dve.tensor_tensor(ki[:, hs, :], n[:, :, 1, :], wide("up_diag", 2), ALU.mult))
                    step(dve.tensor_tensor(md[:, hs, :], bank[4 + p][:, 0:256].rearrange("p (h t) -> p h t", h=2),
                                           wide("low_same", 2), ALU.mult))
                done(dve.tensor_tensor(pq[:, :, 0:128], ed[:, :, :], wide("ident", 4), ALU.add))
                products()
                step(dve.tensor_tensor(pq[:, :, 128:256], el[:, :, :], four(bank[0][:, :]), ALU.add))
                step(dve.tensor_copy(s1[:, :, :], four(bank[1][:, :])))
                done(dve.tensor_copy(s2[:, :, :], four(bank[2][:, :])))
                products()
                step(dve.tensor_copy(s3[:, :, :], four(bank[0][:, :])))
                step(dve.tensor_copy(s4[:, :, :], four(bank[1][:, :])))
                done(grow(pq2, pq))
                products()
                step(dve.tensor_copy(s2[:, :, :], four(bank[1][:, :])))
                done(grow(pq, pq2))
                products()
                done(grow(pq2, pq))
                products()
                done(dve.tensor_copy(s5[:, :, :], four(bank[0][:, :])))
                products()
                step(dve.tensor_copy(s1[:, :, :], four(bank[1][:, :])))
                done(dve.tensor_copy(s2[:, :, :], four(bank[2][:, :])))
                products()
                done(dve.tensor_copy(s3[:, :, :], four(bank[1][:, :])))
                for _ in range(3):
                    products()
                    done(dve.tensor_tensor(x, x, four(bank[0][:, :]), ALU.add))
                products()
                for p in range(2):
                    out = dve.tensor_copy(rr[:, :].rearrange("p (h v) -> p h v", h=4)[:, p:4:2, :],
                                          bank[1 + p][:, 0:128].rearrange("p (h v) -> p h v", h=2))
                    if p == 0:
                        step(out)
                done(out)
                products()
                done(dve.tensor_copy(uu[:, :], bank[3][:, 0:256]))
                products()
                for p in range(2):
                    r = rows[p]
                    out = dve.tensor_copy(k.yb[r, 6:8, quarter[c]],
                                          bank[5 + p][r, 0:256].rearrange("p (a t) -> p a t", a=2))
                    if p == 0:
                        step(out)
                if c < 3:
                    step(out)
                    b = bank[7][:, 0:128].rearrange("p (a t) -> p a t", a=2)
                    if c:
                        step(dve.tensor_tensor(z[:, :, :], z[:, :, :], b, ALU.add))
                    else:
                        step(dve.tensor_copy(z[:, :, :], b))
                    step(dve.tensor_scalar(z[:, 0, :], z[:, 0, :], zs[:, 0, c:c + 1], None, ALU.mult))
                    out = dve.tensor_scalar(z[:, 1, :], z[:, 1, :], zs[:, 1, c:c + 1], None, ALU.mult)
                done(out)




def route(k, gate_dram):
    ws = k.ws
    ws.plan(8)
    bias = k.mats1[:, 512:548]
    four = lambda name: const(k, name).rearrange("p (q e) -> p q e", q=4)
    with memory(k, lg=(4, 128), pick=(4, 4), m=(4, 8), le=(4, 32), hot=(4, 32), hot2=(4, 32), gate=(4, 32),
                wide=(4, 32), gate_t=(512,)) as (lg, pick, m, le, hot, hot2, gate, wide, gate_t), \
            stage(k, "logits_ready", "exp_ready", "best_ready", "gates_ready", "turned", "turned_copied", "stored",
                  "vector_order") as (block, logits_ready, exp_ready, best_ready, gates_ready, turned,
                                      turned_copied, stored, order):
        bc = lambda ap, n: ap.to_broadcast([128, 4, n])

        @block.sync
        def _(sp):
            ws.load(sp)
            sp.wait_ge(turned_copied, 1)
            sp.dma_start(gate_dram, gate_t[0:32, :]).then_inc(stored, 16)
            sp.wait_ge(stored, 16)

        @block.gpsimd
        def _(pool):
            ws.divide(pool)

        @block.tensor
        def _(pe):
            for t in range(KT):
                still = [(k.xh[:, t, 128 * q:128 * q + 128], k.xl[:, t, 128 * q:128 * q + 128]) for q in range(4)]
                last = ws.product_tm(pe, [k.bank[q][:, 0:128] for q in range(4)], still, 1, t == 0, t == KT - 1)
            last.then_inc(logits_ready, 1)
            pe.wait_ge(gates_ready, 1)
            for q in range(4):
                last = pe.transpose(k.bank[4][0:32, 128 * q:128 * q + 128], gate[:, q, :], const(k, "ident"))
            last.then_inc(turned, 1)

        @block.scalar
        def _(act):
            act.wait_ge(best_ready, 1)
            act.activation(m[:, :, 4:8], lg[:, :, 0:4], ACT.Exp).then_inc(exp_ready, 1)
            act.wait_ge(best_ready, 2)
            act.activation(m[:, :, 3:4], m[:, :, 3:4], ACT.Exp).then_inc(exp_ready, 1)

        @block.vector
        def _(dve):
            step = Order(dve, order)
            dve.wait_ge(logits_ready, 1)
            for q in range(4):
                step(dve.tensor_tensor(lg[:, q, 0:36], k.bank[q][:, 0:36], bias, ALU.add))
            step(dve.tensor_reduce(m[:, :, 0:1], lg[:, :, 0:4], AX.X, ALU.max))
            step(dve.tensor_tensor(pick[:, :, :], lg[:, :, 0:4], bc(m[:, :, 0:1], 4), ALU.is_equal))
            dve.tensor_tensor(lg[:, :, 0:4], lg[:, :, 0:4], bc(m[:, :, 0:1], 4), ALU.subtract).then_inc(best_ready, 1)
            step(dve.tensor_tensor(pick[:, :, :], pick[:, :, :], four("rank8")[:, :, 0:4], ALU.mult))
            step(dve.tensor_reduce(m[:, :, 1:2], pick[:, :, :], AX.X, ALU.max))
            step(dve.tensor_tensor(pick[:, :, :], pick[:, :, :], bc(m[:, :, 1:2], 4), ALU.is_equal))
            dve.wait_ge(exp_ready, 1)
            step(dve.tensor_reduce(m[:, :, 2:3], m[:, :, 4:8], AX.X, ALU.add))
            step(dve.reciprocal(m[:, :, 2:3], m[:, :, 2:3]))
            spread = pick[:, :, :].rearrange("p q (g a) -> p (q g) a", a=1).to_broadcast([128, 16, 8])
            groups = lambda ap: ap.rearrange("p q (g e) -> p (q g) e", e=8)
            step(dve.tensor_copy(groups(wide[:, :, :]), spread))
            step(dve.tensor_tensor(le[:, :, :], lg[:, :, 4:36], wide[:, :, :], ALU.mult))
            step(dve.tensor_scalar(wide[:, :, :], wide[:, :, :], 1.0, -MASKED, ALU.subtract, ALU.mult))
            step(dve.tensor_tensor(le[:, :, :], le[:, :, :], wide[:, :, :], ALU.add))
            for hots, at in ((hot, 0), (hot2, 1)):
                step(dve.tensor_reduce(m[:, :, at:at + 1], le[:, :, :], AX.X, ALU.max))
                step(dve.tensor_tensor(hots[:, :, :], le[:, :, :], bc(m[:, :, at:at + 1], 32), ALU.is_equal))
                step(dve.tensor_tensor(hots[:, :, :], hots[:, :, :],
                                       const(k, "rank8").rearrange("p (a e) -> p a e", a=1).to_broadcast([128, 4, 32]),
                                       ALU.mult))
                step(dve.tensor_reduce(m[:, :, 4:5], hots[:, :, :], AX.X, ALU.max))
                step(dve.tensor_tensor(hots[:, :, :], hots[:, :, :], bc(m[:, :, 4:5], 32), ALU.is_equal))
                if at == 0:
                    step(dve.scalar_tensor_tensor(le[:, :, :], hots[:, :, :], 2 * MASKED, le[:, :, :], ALU.mult,
                                                  ALU.add))
            dve.tensor_tensor(m[:, :, 3:4], m[:, :, 1:2], m[:, :, 0:1], ALU.subtract).then_inc(best_ready, 1)
            dve.wait_ge(exp_ready, 2)
            step(dve.tensor_scalar(m[:, :, 5:6], m[:, :, 3:4], 1.0, None, ALU.add))
            step(dve.reciprocal(m[:, :, 5:6], m[:, :, 5:6]))
            step(dve.tensor_tensor(m[:, :, 5:6], m[:, :, 5:6], m[:, :, 2:3], ALU.mult))
            step(dve.tensor_tensor(m[:, :, 6:7], m[:, :, 5:6], m[:, :, 3:4], ALU.mult))
            step(dve.tensor_tensor(gate[:, :, :], hot[:, :, :], bc(m[:, :, 5:6], 32), ALU.mult))
            step(dve.tensor_tensor(hot2[:, :, :], hot2[:, :, :], bc(m[:, :, 6:7], 32), ALU.mult))
            dve.tensor_tensor(gate[:, :, :], gate[:, :, :], hot2[:, :, :], ALU.add).then_inc(gates_ready, 1)
            dve.wait_ge(turned, 1)
            dve.tensor_copy(gate_t[0:32, :], k.bank[4][0:32, :]).then_inc(turned_copied, 1)


def experts(k, gate_dram):
    ws = k.ws
    turns, per = EXPERTS // 4, MOE_CHUNKS
    c0 = ws.blocks // 16
    assert ws.blocks % 16 == 0 and ws.n_loaded == c0 + 3 and ws.n_split == c0 + 1
    with memory(k, hh=("r", 8, SEQ), hl=("r", 8, SEQ), gates=(4, SEQ), silu=(2, SEQ), mid=(2, SEQ)) as (
            hh, hl, gates, silu, mid), \
            stage(k, "gates_in", "gate_ready", "up_ready", "silu_ready", "pair_read", "hidden_ready", "down_ready",
                  "down_added", "vector_order") as (
                block, gates_in, gate_ready, up_ready, silu_ready, pair_read, hidden_ready, down_ready, down_added,
                order):

        @block.sync
        def _(sp):
            with sp.Fori(0, turns) as i:
                row = gate_dram[i, :].partition_broadcast(128).rearrange("p (e t) -> p e t", e=4)
                sp.wait_ge(order, i * 16 + 1)
                sp.dma_start(gates[:, :, :], row).then_inc(gates_in, 16)
                for c in range(c0 + 3, c0 + 3 + per):
                    sp.wait_ge(ws.split, i * per + (c - SLOTS + 1))
                    sp.dma_start(ws.raw[:, c % SLOTS, :], ws.dram[i * per + c, :, :]).then_inc(
                        ws.loaded[c % SLOTS], 16)

        @block.gpsimd
        def _(pool):
            with pool.Fori(0, turns) as i:
                ws.turn = i * per
                ws.n_split, ws.to_split = c0 + 1, c0 + 1 + per
                ws.divide(pool)

        @block.tensor
        def _(pe):
            with pe.Fori(0, turns) as i:
                ws.turn = i * per
                ws.blocks = 16 * c0
                for u in range(8):
                    a, b = k.bank[2 * (u % 2)], k.bank[2 * (u % 2) + 1]
                    pe.wait_ge(pair_read, i * 8 + (u + 1))
                    for t in range(KT):
                        last = ws.product(pe, a[:, :], (k.xh[:, t, :], k.xl[:, t, :]), t == 0, t == KT - 1)
                    last.then_inc(gate_ready, 1)
                    for t in range(KT):
                        last = ws.product(pe, b[:, :], (k.xh[:, t, :], k.xl[:, t, :]), t == 0, t == KT - 1)
                    last.then_inc(up_ready, 1)
                for dt in range(KT):
                    pe.wait_ge(down_added, i * 8 + (dt + 1))
                    for u in range(8):
                        if dt == 0:
                            pe.wait_ge(hidden_ready, i * 8 + (u + 1))
                        last = ws.product(pe, k.bank[4 + dt % 2][:, :], (hh[:, u, :], hl[:, u, :]), u == 0, u == 7)
                    last.then_inc(down_ready, 1)

        @block.scalar
        def _(act):
            with act.Fori(0, turns) as i:
                for u in range(8):
                    act.wait_ge(gate_ready, i * 8 + (u + 1))
                    act.activation(silu[:, u % 2, :], k.bank[2 * (u % 2)][:, :], ACT.Silu).then_inc(silu_ready, 1)

        @block.vector
        def _(dve):
            for s in range(2):
                dve.memset(mid[:, s, 0:1], 0.0).then_inc(pair_read, 1)
                dve.memset(mid[:, s, 1:2], 0.0).then_inc(down_added, 1)
            dve.memset(mid[:, 0, 2:3], 0.0).then_inc(order, 1)
            dve.wait_ge(pair_read, 2)
            dve.wait_ge(down_added, 2)
            dve.wait_ge(order, 1)
            with dve.Fori(0, turns) as i:
                n = 1
                for u in range(8):
                    m = mid[:, u % 2, :]
                    dve.wait_ge(silu_ready, i * 8 + (u + 1))
                    dve.wait_ge(up_ready, i * 8 + (u + 1))
                    if u == 0:
                        dve.wait_ge(gates_in, i * 16 + 16)
                    dve.tensor_tensor(m, silu[:, u % 2, :], k.bank[2 * (u % 2) + 1][:, :], ALU.mult).then_inc(
                        pair_read, 1)
                    dve.wait_ge(pair_read, i * 8 + (u + 3))
                    dve.tensor_tensor(m, m, gates[:, u // 2, :], ALU.mult).then_inc(order, 1)
                    n += 1
                    dve.wait_ge(order, i * 16 + n)
                    dve.tensor_copy(hh[:, u, :], m).then_inc(order, 1)
                    n += 1
                    dve.wait_ge(order, i * 16 + n)
                    dve.tensor_tensor(hl[:, u, :], m, hh[:, u, :].bitcast(F32), ALU.subtract).then_inc(
                        hidden_ready, 1)
                for dt in range(KT):
                    dve.wait_ge(down_ready, i * 8 + (dt + 1))
                    dve.tensor_tensor(k.res[:, dt, :], k.res[:, dt, :], k.bank[4 + dt % 2][:, :], ALU.add).then_inc(
                        down_added, 1)
    total = turns * per
    ws.turn = 0
    ws.blocks = 16 * (c0 + total)
    ws.n_loaded, ws.n_split = c0 + total + 3, c0 + total + 1




def retention(k, pj, rv):
    par = lambda n, j=0: k.par2[:, P2[n] + j:P2[n] + j + 1]
    rotate = const(k, "rotate")
    with memory(k, decays=(4, STRIP)) as decays:
        with memory(k, tabs=(2 * SEQ + 2 * STRIP,), rot_t=(SEQ,), lgam=(3, 8)) as (tabs, tmp, lgam):
            cos, sin = tabs[:, 0:SEQ], tabs[:, SEQ:2 * SEQ]
            ahead, behind = tabs[:, 2 * SEQ:2 * SEQ + STRIP], tabs[:, 2 * SEQ + STRIP:2 * SEQ + 2 * STRIP]
            with stage(k, "tables_in", "rotated", "rotated_read", "abs_ready", "exp_ready", "log_ready", "powers_ready",
                       "strips_ready", "vector_order") as (block, tables_in, rotated, rotated_read, abs_ready, exp_ready,
                                                           log_ready, powers_ready, strips_ready, order):
                @block.sync
                def _(sp):
                    sp.dma_start(tabs[:, :], k.dram["tables"][:, 0:2 * SEQ + 2 * STRIP]).then_inc(tables_in, 16)

                @block.tensor
                def _(pe):
                    for j in range(4):
                        if j >= 2:
                            pe.wait_ge(rotated_read, j - 1)
                        pe.matmul(k.bank[j % 2][:, :], rotate, pj[:, T2["rq"] + j, :], start=True, stop=True).then_inc(
                            rotated, 1)

                @block.scalar
                def _(act):
                    act.wait_ge(abs_ready, 1)
                    act.activation(lgam[:, 1, :], lgam[:, 1, :], ACT.Exp, scale=-1.0).then_inc(exp_ready, 1)
                    act.wait_ge(exp_ready, 1)
                    act.activation(lgam[:, 1, :], lgam[:, 1, :], ACT.Ln, bias=k.eps[:, 3:4]).then_inc(log_ready, 1)
                    for h in range(4):
                        act.wait_ge(powers_ready, h + 1)
                        act.activation(decays[:, h, :], decays[:, h, :], ACT.Exp).then_inc(strips_ready, 1)

                @block.vector
                def _(dve):
                    step = Order(dve, order)
                    g = k.par2[:, P2["decay"]:P2["decay"] + 8]
                    step(dve.tensor_scalar(lgam[:, 0, :], g, -1.0, None, ALU.mult))
                    dve.tensor_tensor(lgam[:, 1, :], lgam[:, 0, :], g, ALU.max).then_inc(abs_ready, 1)
                    step(dve.tensor_scalar(lgam[:, 2, :], g, 0.0, None, ALU.min))
                    dve.wait_ge(log_ready, 1)
                    step(dve.tensor_tensor(lgam[:, 2, :], lgam[:, 2, :], lgam[:, 1, :], ALU.subtract))
                    dve.wait_ge(tables_in, 16)
                    for h in range(4):
                        d = decays[:, h, :]
                        step(dve.tensor_scalar(d, behind, lgam[:, 2, 4 + h:5 + h], None, ALU.mult))
                        dve.scalar_tensor_tensor(d, ahead, lgam[:, 2, h:h + 1], d, ALU.mult, ALU.add).then_inc(
                            powers_ready, 1)
                    for j in range(4):
                        z = pj[:, T2["rq"] + j, :]
                        dve.wait_ge(rotated, j + 1)
                        dve.tensor_tensor(tmp[:, :], k.bank[j % 2][:, :], sin, ALU.mult).then_inc(rotated_read, 1)
                        dve.wait_ge(rotated_read, j + 1)
                        step(dve.tensor_tensor(z, z, cos, ALU.mult))
                        step(dve.tensor_tensor(z, z, tmp[:, :], ALU.add))
        with memory(k, wsc=(2, 4, SEQ)) as wsc:
            with stage(k, "scores_ready", "scores_used", "out_ready", "out_copied") as (
                    block, scores_ready, scores_used, out_ready, out_copied):
                @block.tensor
                def _(pe):
                    for h in range(5):
                        if h < 4:
                            rows = slice(64 * (h % 2), 64 * (h % 2) + 64)
                            for j in range(4):
                                u = 4 * h + j
                                if u >= 4:
                                    pe.wait_ge(scores_used, u - 3)
                                pe.matmul(k.bank[u % 4][:, :], pj[rows, T2["rk"] + h // 2, 128 * j:128 * j + 128],
                                          pj[rows, T2["rq"] + h // 2, :], start=True, stop=True).then_inc(
                                    scores_ready, 1)
                        if h >= 1:
                            g = h - 1
                            rows = slice(64 * (g % 2), 64 * (g % 2) + 64)
                            pe.wait_ge(scores_used, 4 * g + 4)
                            for j in range(4):
                                last = pe.matmul(k.bank[4 + g // 2][rows, :], rv[:, j, 64 * g:64 * g + 64],
                                                 wsc[:, g % 2, j, :], start=j == 0, stop=j == 3)
                            last.then_inc(out_ready, 1)

                @block.vector
                def _(dve):
                    for u in range(16):
                        h, j = divmod(u, 4)
                        if j == 0 and h >= 2:
                            dve.wait_ge(out_ready, h - 1)
                        dve.wait_ge(scores_ready, u + 1)
                        dve.scalar_tensor_tensor(wsc[:, h % 2, j, :], k.bank[u % 4][:, :], 0.125,
                                                 decays[:, h, 384 - 128 * j:384 - 128 * j + SEQ], ALU.mult,
                                                 ALU.mult).then_inc(scores_used, 1)
                    for p in range(2):
                        dve.wait_ge(out_ready, 2 * p + 2)
                        dve.tensor_copy(k.yb[:, p, :], k.bank[4 + p][:, :]).then_inc(out_copied, 1)
    with stage(k, "silu_done") as (block, silu_done):
        @block.scalar
        def _(act):
            for p in range(2):
                g = pj[:, T2["rg"] + p, :]
                act.activation(g, g, ACT.Silu).then_inc(silu_done, 1)

    def finish(p):
        y = k.yb[:, p, :]

        def run(dve, step, rstd):
            step(dve.tensor_tensor(y, y, rstd, ALU.mult))
            return dve.scalar_tensor_tensor(y, y, par("ret", p), pj[:, T2["rg"] + p, :], ALU.mult, ALU.mult)
        return run

    head_norm(k, [dict(src=k.yb[:, p, :], scale=1.0 / 64, eps=k.eps[:, 1:2], finish=finish(p)) for p in range(2)])


def pooling(k, pj):
    n = SEQ + 16
    with memory(k, padded=(2, n), sums=(2, n), share=(2, SEQ)) as (padded, sums, share):
        with stage(k, "counts_in", "vector_order") as (block, counts_in, order):
            @block.sync
            def _(sp):
                at = 2 * SEQ + 2 * STRIP
                sp.dma_start(share[:, :, :], k.dram["tables"][:, at:at + 2 * SEQ].rearrange(
                    "p (a t) -> p a t", a=2)).then_inc(counts_in, 16)

            @block.vector
            def _(dve):
                step = Order(dve, order)
                step(dve.memset(padded[:, :, :], 0.0))
                step(dve.memset(sums[:, :, :], 1.0))
                for p in range(2):
                    step(dve.tensor_copy(padded[:, p, 9:9 + SEQ], pj[:, T2["pv"] + p, :]))
                for p in range(2):
                    step(dve.tensor_tensor_scan(padded[:, p, :], sums[:, p, :], padded[:, p, :], 0.0, ALU.mult,
                                                ALU.add))
                for g in range(4):
                    h = POOL_WINDOWS[g] // 2
                    r, p = slice(64 * (g % 2), 64 * (g % 2) + 64), g // 2
                    step(dve.tensor_tensor(sums[r, p, 0:SEQ], padded[r, p, 8 + h:8 + h + SEQ],
                                           padded[r, p, 8 - h:8 - h + SEQ], ALU.subtract))
                dve.wait_ge(counts_in, 16)
                for p in range(2):
                    step(dve.tensor_tensor(sums[:, p, 0:SEQ], sums[:, p, 0:SEQ], share[:, p, :], ALU.mult))
                    step(dve.tensor_tensor(sums[:, p, 0:SEQ], sums[:, p, 0:SEQ], pj[:, T2["pv"] + p, :],
                                           ALU.subtract))
        small_products(k, [(k.yb[:, 2 + p, :], k.mats2[:, 128 * p:128 * p + 128], sums[:, p, 0:SEQ],
                            k.par2[:, P2["pool"] + p:P2["pool"] + p + 1]) for p in range(2)])


def grid_bias(k, layer, bias, bias_dram):
    with memory(k, tab=(60,), made=(4096,)) as (tab, made), \
            stage(k, "rows_in", "bias_ready", "bias_copied", "bias_stored", "bias_in") as (
                block, rows_in, bias_ready, bias_copied, bias_stored, bias_in):
        @block.sync
        def _(sp):
            sp.dma_start(made[64:96, :], k.dram["na_rows"]).then_inc(rows_in, 16)
            sp.dma_start(tab[64:96, :], k.dram["na_rpb"][layer, :, :]).then_inc(rows_in, 16)
            sp.wait_ge(bias_copied, 8)
            sp.dma_start(bias_dram, made[0:60, :]).then_inc(bias_stored, 16)
            sp.wait_ge(bias_stored, 16)
            for half in range(2):
                for h in range(4):
                    src = bass.AP(tensor=bias_dram.tensor, offset=15 * 4096 * h, ap=[[64, 64], [4096, 15], [1, 64]])
                    sp.dma_start(bias[64 * half:64 * half + 64, h, half:half + 15, :], src).then_inc(bias_in, 16)
            sp.wait_ge(bias_in, 128)

        @block.tensor
        def _(pe):
            pe.wait_ge(rows_in, 32)
            for j in range(8):
                if j >= 2:
                    pe.wait_ge(bias_copied, j - 1)
                pe.matmul(k.bank[j % 2][0:60, :], tab[64:96, :], made[64:96, 512 * j:512 * j + 512], start=True,
                          stop=True).then_inc(bias_ready, 1)

        @block.vector
        def _(dve):
            for j in range(8):
                dve.wait_ge(bias_ready, j + 1)
                dve.tensor_copy(made[0:60, 512 * j:512 * j + 512], k.bank[j % 2][0:60, :]).then_inc(bias_copied, 1)


def layer(k, i, bias_dram):
    par = lambda n, j=0: k.par2[:, P2[n] + j:P2[n] + j + 1]
    with stage(k, "params_in") as (block, params_in):
        @block.sync
        def _(sp):
            sp.dma_start(k.par2[:, :], k.dram["params2"][i, :, :]).then_inc(params_in, 16)
            sp.dma_start(k.mats2[:, :], k.dram["mats2"][i, :, :]).then_inc(params_in, 16)
            sp.wait_ge(params_in, 32)
    eps = k.eps[:, 1:2]
    normalise(k, k.res, lambda t: par("mix", t), None, eps, False, k.xh, k.xl)
    with memory(k, yb=(KT, SEQ)) as k.yb:
        with memory(k, pj2=(T2_TILES, SEQ), rv=(4, 256), nv=(4, 256), mk=(2, 256), mv=(2, 256)) as (
                pj, rv, nv, mk, mv):
            project(k, T2_TILES, pj, [(rv, 256), (nv, 256)])
            with memory(k, memt=(KT, 256), memh=("r", KT, 256), meml=("r", KT, 256)) as (memt, memh, meml):
                with stage(k, "mem_in") as (block, mem_in):
                    @block.sync
                    def _(sp):
                        sp.dma_start(memt[:, :, :], k.dram["memT"]).then_inc(mem_in, 16)
                        sp.wait_ge(mem_in, 16)
                normalise(k, memt, lambda t: par("mem", t), None, eps, False, memh, meml, n=256)
                project(k, 2, mk, [(mv, 256)], (memh, meml), 256)
            jobs = []
            for name, gain in (("nq", "naq"), ("nk", "nak"), ("mq", "memq")):
                for p in range(2):
                    src = pj[:, T2[name] + p, :]
                    jobs.append(dict(src=src, scale=1.0 / 64, eps=eps, finish=gained(src, par(gain))))
            head_norm(k, jobs)
            head_norm(k, [dict(src=mk[:, p, :], scale=1.0 / 64, eps=eps, finish=gained(mk[:, p, :], par("memk")))
                          for p in range(2)], n=256)
            retention(k, pj, rv)
            pooling(k, pj)
            with memory(k, na_bias=(4, 16, 64)) as bias:
                grid_bias(k, i, bias, bias_dram)
                units = []
                for h in range(4):
                    rows = slice(64 * (h % 2), 64 * (h % 2) + 64)
                    for q in range(4):
                        cols = slice(128 * q, 128 * q + 128)
                        b = bias[:, h, 7 - 2 * q:15 - 2 * q, :].rearrange("p r c -> p (r c)")
                        units.append(dict(q=pj[rows, T2["nq"] + h // 2, cols], keys=pj[rows, T2["nk"] + h // 2, :],
                                          n=SEQ, scale=0.125, bias=b, select=None, strip=None, rows=rows, cols=cols,
                                          values=[nv[:, j, 64 * h:64 * h + 64] for j in range(4)], pair=h // 2))
                for h in range(4):
                    rows = slice(64 * (h % 2), 64 * (h % 2) + 64)
                    for q in range(4):
                        cols = slice(128 * q, 128 * q + 128)
                        units.append(dict(q=pj[rows, T2["mq"] + h // 2, cols], keys=mk[rows, h // 2, :], n=256,
                                          scale=0.125, bias=None, select=None, strip=None, rows=rows, cols=cols,
                                          values=[mv[:, j, 64 * h:64 * h + 64] for j in range(2)], pair=2 + h // 2))
                attention(k, units, [k.yb[:, 4 + p, :] for p in range(4)])
        merge(k, 1.0)
    normalise(k, k.res, lambda t: par("ffn", t), None, eps, False, k.xh, k.xl)
    feed_forward(k)


def feed_forward(k):
    ws = k.ws
    nf = FF // 128
    with memory(k, fh=("r", nf, SEQ), fl=("r", nf, SEQ), silu=(2, SEQ), mid=(1, SEQ)) as (fh, fl, silu, mid):
        ws.plan(nf * 16)
        with stage(k, "act_ready", "lin_ready", "silu_ready", "pair_read", "vector_order") as (
                block, act_ready, lin_ready, silu_ready, pair_read, order):
            @block.sync
            def _(sp):
                ws.load(sp)

            @block.gpsimd
            def _(pool):
                ws.divide(pool)

            @block.tensor
            def _(pe):
                for j in range(nf):
                    if j >= 2:
                        pe.wait_ge(pair_read, j - 1)
                    for m, done in ((0, act_ready), (1, lin_ready)):
                        for t in range(KT):
                            last = ws.product(pe, k.bank[2 * (j % 2) + m][:, :], (k.xh[:, t, :], k.xl[:, t, :]),
                                              t == 0, t == KT - 1)
                        last.then_inc(done, 1)

            @block.scalar
            def _(act):
                for j in range(nf):
                    act.wait_ge(act_ready, j + 1)
                    act.activation(silu[:, j % 2, :], k.bank[2 * (j % 2)][:, :], ACT.Silu).then_inc(silu_ready, 1)

            @block.vector
            def _(dve):
                step = Order(dve, order)
                for j in range(nf):
                    dve.wait_ge(silu_ready, j + 1)
                    dve.wait_ge(lin_ready, j + 1)
                    dve.tensor_tensor(mid[:, 0, :], silu[:, j % 2, :], k.bank[2 * (j % 2) + 1][:, :],
                                      ALU.mult).then_inc(pair_read, 1)
                    dve.wait_ge(pair_read, j + 1)
                    step(dve.tensor_copy(fh[:, j, :], mid[:, 0, :]))
                    step(dve.tensor_tensor(fl[:, j, :], mid[:, 0, :], fh[:, j, :].bitcast(F32), ALU.subtract))
        add_product(k, nf, fh, fl, 1.0)




def reload_x(k):
    with stage(k, "x_in") as (block, x_in):
        @block.sync
        def _(sp):
            sp.dma_start(k.res[:, :, :], k.dram["xT"]).then_inc(x_in, 16)
            sp.wait_ge(x_in, 16)


def scale_residual(k):
    with stage(k, "scaled") as (block, scaled):
        @block.vector
        def _(dve):
            for t in range(KT):
                dve.tensor_scalar(k.res[:, t, :], k.res[:, t, :], ALPHA, None, ALU.mult).then_inc(scaled, 1)


def store_out(k, c0):
    ws = k.ws
    end = c0 + LAYERS * LAYER_CHUNKS
    with stage(k, "stored") as (block, stored):
        @block.sync
        def _(sp):
            sp.dma_start(k.dram["outT"], k.res[:, :, :]).then_inc(stored, 16)
            sp.wait_ge(stored, 16)
            for c in (end + 1, end + 2):
                sp.wait_ge(ws.loaded[c % SLOTS], 16 * (c // SLOTS + 1))


def build(nc, dram):
    with ExitStack() as ctx:
        k = Kernel(nc, dram)
        k.bank = [ctx.enter_context(nc.psum_tensor(f"bank{b}", [128, 512], F32)) for b in range(8)]
        k.ws = Stream(nc, ctx, dram["weights"])
        k.xh, k.xl, k.res, k.consts, k.par1, k.par2, k.mats1, k.mats2, k.eps = ctx.enter_context(memory(
            k, xh=("r", KT, SEQ), xl=("r", KT, SEQ), res=(KT, SEQ), consts=(CONSTS,), par1=(P1_COLS,),
            par2=(P2_COLS,), mats1=(548,), mats2=(256,), eps=(4,)))
        bias_dram = nc.dram_tensor("distance_bias", (8, 128, 1024), F32, kind="Internal").ap()
        gate_dram = nc.dram_tensor("expert_gates", (8, 4 * SEQ), F32, kind="Internal").ap()
        grid_dram = nc.dram_tensor("grid_bias", (60, 4096), F32, kind="Internal").ap()
        load_start(k)
        with memory(k, yb=(KT, SEQ)) as k.yb:
            with memory(k, pj=(T1_TILES, SEQ), av=(4, 256), cv=(4, 256)) as (pj, av, cv):
                project(k, T1_TILES, pj, [(av, 256), (cv, 256)])
                mixers_ab(k, pj, av, bias_dram)
                mixer_c(k, pj, cv)
                mixer_d(k, pj)
            reload_x(k)
            merge(k, ALPHA)
        par = lambda n, j: k.par1[:, P1[n] + j:P1[n] + j + 1]
        normalise(k, k.res, lambda t: par("ln_g", t), lambda t: par("ln_b", t), k.eps[:, 0:1], True, k.xh, k.xl,
                  out=k.res)
        route(k, gate_dram.rearrange("g (e t) -> (g e) t", e=4))
        scale_residual(k)
        experts(k, gate_dram)
        normalise(k, k.res, lambda t: par("ln_g", 8 + t), lambda t: par("ln_b", 8 + t), k.eps[:, 0:1], True,
                  out=k.res)
        c0 = k.ws.blocks // 16
        with nc.Fori(0, LAYERS) as i:
            k.ws.turn = i * LAYER_CHUNKS
            layer(k, i, grid_dram)
            assert k.ws.blocks == 16 * (c0 + LAYER_CHUNKS)
        store_out(k, c0)




def fm_blocks(w):
    k, f = w.shape
    return w.reshape(k // 128, 128, f // 128, 128).transpose(2, 0, 1, 3).reshape(-1, 128, 128)


def tm_blocks(w):
    k, f = w.shape
    return w.reshape(k // 128, 128, f // 128, 128).transpose(0, 2, 1, 3).reshape(-1, 128, 128)


def merge_blocks(gate, branch):
    g = gate.reshape(8, 128, 4, 8, 128).transpose(3, 2, 0, 1, 4)
    b = branch.reshape(4, 2, 128, 8, 128).transpose(3, 0, 1, 2, 4)
    return np.concatenate([g, b], axis=2).reshape(-1, 128, 128)


def pair_blocks(a, b):
    x = fm_blocks(a).reshape(-1, 8, 128, 128)
    y = fm_blocks(b).reshape(-1, 8, 128, 128)
    return np.stack([x, y], axis=1).reshape(-1, 128, 128)


def weight_stream(v):
    w = v["w_in"][0]
    off = dict(aq=0, ak=256, av=512, bq=768, ckv=1024, iq=1088, ik=1344, iw=1376, cq=1384, ck=1512, cv=1640,
               ca=1896, cg=1912, dr=2168, dk=2424, dv=2680, dw=2936, da=2952, dg=2968, gate=3000)

    def cols(name, n):
        return w[:, off[name]:off[name] + n]

    low = np.zeros((D, 128), np.float32)
    low[:, 0:16] = cols("dw", 16)
    low[:, 32:48] = cols("da", 16)
    low[:, 64:96] = cols("dg", 32)
    low[:, 96:112] = cols("ca", 16)
    low[:, 112:120] = cols("iw", 8)
    router = np.zeros((D, 128), np.float32)
    router[:, 0:4] = v["router_g"][0]
    router[:, 4:36] = v["router_e"][0]
    fm = np.concatenate([cols("aq", 256), cols("ak", 256), cols("bq", 256), cols("iq", 256), cols("ckv", 64),
                         cols("ckv", 64)] + [cols("ik", 32)] * 4 + [low, cols("cq", 128), cols("ck", 128),
                         cols("cg", 256), cols("dr", 256), cols("dk", 256), cols("dv", 256)], axis=1)
    parts = [fm_blocks(fm), tm_blocks(cols("av", 256)), tm_blocks(cols("cv", 256)),
             merge_blocks(cols("gate", 4 * D), v["w_branch"][0]), fm_blocks(v["w_out"][0]), tm_blocks(router)]
    for g in range(8):
        for e in range(4 * g, 4 * g + 4):
            parts.append(pair_blocks(v["moe_w_gate"][0, e], v["moe_w_up"][0, e]))
        down = v["moe_w_down"][0, 4 * g:4 * g + 4].reshape(4, 2, 128, 8, 128).transpose(3, 0, 1, 2, 4)
        parts.append(down.reshape(-1, 128, 128))
    for l in range(LAYERS):
        w2 = v["w_in_2"][l]
        sec = [w2[:, 256 * n:256 * n + 256] for n in range(9)]
        rq, rk, rv, rg, pv, nq, nk, nv, mq = sec
        parts += [fm_blocks(np.concatenate([rq, rk, rg, pv, nq, nk, mq], axis=1)), tm_blocks(rv), tm_blocks(nv),
                  fm_blocks(v["w_mem_kv_2"][l][:, 0:256]), tm_blocks(v["w_mem_kv_2"][l][:, 256:512]),
                  merge_blocks(v["w_gate_2"][l], v["w_branch_2"][l]), fm_blocks(v["w_out_2"][l]),
                  pair_blocks(v["w_ffn_in_2"][l][:, 0:FF], v["w_ffn_in_2"][l][:, FF:2 * FF]),
                  fm_blocks(v["w_ffn_out_2"][l])]
    parts.append(np.zeros((16 * SPARE, 128, 128), np.float32))
    s = np.concatenate(parts, axis=0)
    assert s.shape[0] == 16 * (CHUNKS + SPARE)
    return np.ascontiguousarray(s.reshape(-1, 16, 128, 128).transpose(0, 2, 1, 3).reshape(-1, 128, CHUNK))


def t5_bucket(dist):
    exact = 16
    d = np.maximum(dist, 0)
    df = np.maximum(d, 1).astype(np.float32)
    large = exact + (np.log(df / np.float32(exact)) / np.float32(math.log(2048 / exact)) * np.float32(16)).astype(np.int32)
    return np.where(d < exact, d, np.minimum(large, 31))


def distance_rows():
    dist = 511 - np.arange(1024)
    r = np.zeros((34, 1024), np.float32)
    b = t5_bucket(dist)
    for y in range(1024):
        if dist[y] >= 0:
            r[b[y], y] = 1.0
    held = (dist <= 128).astype(int) + (dist % 4 == 0) + (dist % 16 == 0)
    held = np.where(dist >= 0, held, 0)
    r[32] = np.where(held > 0, np.log(np.maximum(held, 1)), MASKED)
    r[33] = np.where(dist >= 0, 0.0, MASKED)
    return r


def constants():
    c = np.zeros((128, CONSTS), np.float32)
    i, j = np.meshgrid(np.arange(128), np.arange(128), indexing="ij")

    def put(name, m):
        c[:, CONST[name]:CONST[name] + m.shape[1]] = m

    put("ident", (i == j))
    put("ones", np.ones((128, 128)))
    put("blk64", (i // 64 == j // 64))
    put("gla_mask", (i <= j) & (i // 64 == j // 64))
    put("up_same", (i < j) & (i // 16 == j // 16))
    put("up_other", (i < j) & (i // 16 != j // 16))
    put("low_same", (i > j) & (i // 16 == j // 16))
    put("up", (i < j))
    put("up_diag", (i <= j))
    put("future", np.where(j > i, MASKED, 0.0))
    a, b = np.meshgrid(np.arange(128), np.arange(256), indexing="ij")
    put("gla_heads", (a // 32 == b // 64))
    t = np.arange(512)[None, :] + np.zeros((128, 1))
    put("reset64", (t % 64 != 0))
    put("reset128", (t % 128 != 0))
    rot = np.where(j % 64 < 32, -1.0 * (i == j + 32), 1.0 * (i == j - 32))
    put("rotate", rot)
    put("rank8", np.tile(8.0 - np.arange(8), (128, 4)))
    return c


def layer_tables():
    half = 32
    inv = (np.float32(10000.0) ** (-np.arange(half, dtype=np.float32) / np.float32(half))).astype(np.float32)
    ang = (np.arange(SEQ, dtype=np.float32)[None, :] * inv[:, None]).astype(np.float32).astype(np.float64)
    cos, sin = (np.tile(f(ang), (4, 1)).astype(np.float32) for f in (np.cos, np.sin))
    p, x = np.meshgrid(np.arange(128), np.arange(STRIP), indexing="ij")
    ahead = np.maximum(x - 384 - p, 0).astype(np.float32)
    behind = np.maximum(384 + p - x, 0).astype(np.float32)
    t = np.arange(SEQ)
    counts = np.zeros((128, 2, SEQ), np.float32)
    for g in range(4):
        h = POOL_WINDOWS[g] // 2
        n = np.clip(t + h, 0, SEQ) - np.clip(t - h, 0, SEQ)
        counts[64 * (g % 2):64 * (g % 2) + 64, g // 2, :] = (1.0 / n)[None, :]
    return np.concatenate([cos, sin, ahead, behind, counts.reshape(128, -1)], axis=1)


def na_select():
    r = np.zeros((32, 64, 64), np.float32)
    for qc in range(64):
        lo = min(max(qc - 8, 0), 48)
        for kc in range(64):
            if lo <= kc < lo + 16:
                r[kc - qc + 15, qc, kc] = 1.0
            else:
                r[31, qc, kc] = MASKED
    return r.reshape(32, 4096)


def columns(*arrays):
    return np.concatenate([a.reshape(-1, 128).T for a in arrays], axis=1)


def device_arrays(v):
    f32 = np.float32
    a = {}
    a["xT"] = np.ascontiguousarray(v["x"][0].T.reshape(8, 128, SEQ).transpose(1, 0, 2))
    a["memT"] = np.ascontiguousarray(v["mem_2"][0].T.reshape(8, 128, 256).transpose(1, 0, 2))
    a["weights"] = weight_stream(v)
    a["consts"] = constants()
    a["tables"] = layer_tables()
    a["dist_rows"] = distance_rows()
    a["na_rows"] = na_select()
    tab = np.zeros((34, 8), f32)
    tab[0:32] = v["rpb_table"]
    tab[32, 0:4] = 1.0
    tab[33, 4:8] = 1.0
    a["rpb"] = tab
    mu = v["d_mu"][0]
    mu_low = np.zeros(128, f32)
    mu_low[0:16], mu_low[32:48], mu_low[64:96] = mu[768:784], mu[784:800], mu[800:832]
    dup = lambda z, n: np.tile(z, n)
    a["params1"] = np.ascontiguousarray(columns(
        v["ln_g"][0], v["ln_b"][0], dup(v["b_kv_gain"][0], 2), v["c_a_bias"][0], v["c_norm_gain"][0],
        mu[0:768], mu_low, v["d_w0"][0], v["d_a0"][0], v["d_k_k"][0], v["d_k_a"][0], v["d_r_k"][0],
        v["d_gn_w"][0], v["d_gn_b"][0]))
    low = np.zeros((128, 256), f32)
    low[0:16], low[32:48], low[64:96] = v["d_w2"][0], v["d_a2"][0], v["d_g2"][0]
    low[96:112, 0:128] = v["c_a_up"][0]
    uv = np.zeros((128, 256), f32)
    for h in range(4):
        r = 64 * (h % 2)
        uv[r:r + 64, 128 * (h // 2) + r:128 * (h // 2) + r + 64] = v["b_w_uv"][0, h]
    bias = np.concatenate([v["router_g_bias"][0], v["router_e_bias"][0]])
    a["mats1"] = np.concatenate([low, uv, np.tile(bias[None, :], (128, 1))], axis=1)
    p2, m2, rp = [], [], []
    for l in range(LAYERS):
        reps = np.concatenate([v["ret_decay_fwd_2"][l], v["ret_decay_bwd_2"][l]])
        p2.append(np.concatenate([columns(
            v["norm_mix_g_2"][l], v["norm_mem_g_2"][l], v["norm_ffn_g_2"][l], v["ret_norm_g_2"][l],
            v["pool_scale_2"][l], dup(v["na_q_norm_g_2"][l], 2), dup(v["na_k_norm_g_2"][l], 2),
            dup(v["mem_q_norm_g_2"][l], 2), dup(v["mem_k_norm_g_2"][l], 2)),
            np.tile(reps[None, :], (128, 1))], axis=1))
        pw = np.zeros((128, 256), f32)
        for g in range(4):
            r = 64 * (g % 2)
            pw[r:r + 64, 128 * (g // 2) + r:128 * (g // 2) + r + 64] = v["pool_w_2"][l, g]
        m2.append(pw)
        r = np.ones((32, 60), f32)
        r[0:31] = v["na_rpb_2"][l].reshape(60, 31).T
        rp.append(r)
    a["params2"] = np.stack(p2)
    a["mats2"] = np.stack(m2)
    a["na_rpb"] = np.stack(rp)
    return {k: np.ascontiguousarray(x) for k, x in a.items()}


def kernel(**inputs):
    import concourse.bacc as bacc
    from concourse.bass_utils import run_bass_kernel_spmd

    arrays = device_arrays({k: np.asarray(x) for k, x in inputs.items()})
    nc = bacc.Bacc("TRN2", target_bir_lowering=False, num_devices=1)
    dram = {k: nc.dram_tensor(k, x.shape, F32, kind="ExternalInput").ap() for k, x in arrays.items()}
    dram["outT"] = nc.dram_tensor("outT", (128, 8, SEQ), F32, kind="ExternalOutput").ap()
    build(nc, dram)
    r = run_bass_kernel_spmd(nc, [arrays], core_ids=[0])
    out = np.asarray(r.results[0]["outT"])
    return np.ascontiguousarray(out.transpose(2, 1, 0).reshape(1, SEQ, D))
```

```python
import math
from contextlib import ExitStack, contextmanager

import numpy as np

import concourse.bass as bass
from concourse import mybir

F32 = mybir.dt.float32
F32R = mybir.dt.float32r
ALU = mybir.AluOpType
ACT = mybir.ActivationFunctionType
AX = mybir.AxisListType

SEQ, D, FF, LAYERS, EXPERTS = 512, 1024, 2816, 2, 32
KT = D // 128
CHUNK = 2048
SLOTS = 2
ALPHA = 2.0 ** 0.25
MASKED = -1e30
TAKEN = -3e38
STRIP = 896
POOL_WINDOWS = (2, 4, 8, 16)
FIRST_CHUNKS = 37
MOE_CHUNKS = 12
LAYER_CHUNKS = 68
CHUNKS = FIRST_CHUNKS + 8 * MOE_CHUNKS + LAYERS * LAYER_CHUNKS
SPARE = 4

_widths = dict(ident=128, ones=128, blk64=128, gla_mask=128, up_same=128, up_other=128, low_same=128, up=128,
               up_diag=128, future=128, gla_heads=256, reset64=512, reset128=512, rotate=128, rank8=32)
CONST = {}
CONSTS = 0
for _n, _w in _widths.items():
    CONST[_n] = CONSTS
    CONSTS += _w

P1 = dict(ln_g=0, ln_b=16, kv_gain=32, a_bias=33, c_norm=34, mu=36, w0=43, a0=45, k_k=47, k_a=49, r_k=51, gn_w=53,
          gn_b=55)
P1_COLS = 57
P2 = dict(mix=0, mem=8, ffn=16, ret=24, pool=26, naq=28, nak=29, memq=30, memk=31, decay=32)
P2_COLS = 40
T1 = dict(aq=0, ak=2, bq=4, iq=6, ckv=8, ik=9, low=10, cq=11, ck=12, cg=13, dr=15, dk=17, dv=19)
T1_TILES = 21
T2 = dict(rq=0, rk=2, rg=4, pv=6, nq=8, nk=10, mq=12)
T2_TILES = 14


class Kernel:

    def __init__(self, nc, dram):
        self.nc, self.dram, self.tensors = nc, dram, 0


class Order:

    def __init__(self, engine, sem):
        self.engine, self.sem, self.n = engine, sem, 0

    def __call__(self, instruction):
        instruction.then_inc(self.sem, 1)
        self.n += 1
        self.engine.wait_ge(self.sem, self.n)


class Stream:

    def __init__(self, nc, ctx, dram):
        self.dram = dram
        self.raw = ctx.enter_context(nc.sbuf_tensor("w_raw", [128, SLOTS, CHUNK], F32))
        self.hi = ctx.enter_context(nc.sbuf_tensor("w_hi", [128, SLOTS, CHUNK], F32R))
        self.lo = ctx.enter_context(nc.sbuf_tensor("w_lo", [128, SLOTS, CHUNK], F32R))
        self.zero = ctx.enter_context(nc.sbuf_tensor("w_zero", [128, 1], F32))
        self.loaded = [ctx.enter_context(nc.semaphore(f"w_loaded{s}")) for s in range(SLOTS)]
        self.rounded = ctx.enter_context(nc.semaphore("w_rounded"))
        self.split = ctx.enter_context(nc.semaphore("w_split"))
        self.used = ctx.enter_context(nc.semaphore("w_used"))
        self.blocks = 0
        self.n_loaded = 0
        self.n_split = 0
        self.turn = 0
        self.want = 0

    def plan(self, n_blocks):
        self.want = self.blocks + n_blocks
        started = -(-self.want // 16)
        self.to_split = started + 1
        self.to_load = started + 3

    def load(self, sp, upto=None):
        for c in range(self.n_loaded, self.to_load if upto is None else upto):
            if c >= SLOTS:
                sp.wait_ge(self.split, self.turn + (c - SLOTS + 1))
            sp.dma_start(self.raw[:, c % SLOTS, :], self.dram[self.turn + c, :, :]).then_inc(
                self.loaded[c % SLOTS], 16)
        self.n_loaded = max(self.n_loaded, self.to_load)

    def divide(self, pool):
        for c in range(self.n_split, self.to_split):
            s = c % SLOTS
            pool.wait_ge(self.loaded[s], self.turn * (16 // SLOTS) + 16 * (c // SLOTS + 1))
            if c >= SLOTS:
                pool.wait_ge(self.used, self.turn + (c - SLOTS + 1))
            pool.tensor_tensor(self.hi[:, s, :], self.raw[:, s, :], self.zero[:, 0:1].to_broadcast([128, CHUNK]),
                               ALU.add).then_inc(self.rounded, 1)
            pool.wait_ge(self.rounded, self.turn + (c + 1))
            pool.tensor_tensor(self.lo[:, s, :], self.raw[:, s, :], self.hi[:, s, :].bitcast(F32),
                               ALU.subtract).then_inc(self.split, 1)
        self.n_split = self.to_split

    def take(self, pe, n=1):
        c, b = divmod(self.blocks, 16)
        assert b + n <= 16
        if b == 0:
            pe.wait_ge(self.split, self.turn + (c + 1))
            self.release = c > 0
        self.blocks += n
        cols = slice(128 * b, 128 * (b + n))
        return self.hi[:, c % SLOTS, cols], self.lo[:, c % SLOTS, cols]

    def released(self, matmul):
        if self.release:
            matmul.then_inc(self.used, 1)
            self.release = False

    def product(self, pe, out, moving, start, stop):
        hi, lo = self.take(pe)
        self.released(pe.matmul(out, hi, moving[0], start=start, stop=False))
        pe.matmul(out, hi, moving[1], start=False, stop=False)
        return pe.matmul(out, lo, moving[0], start=False, stop=stop)

    def product_tm(self, pe, outs, still, n, start, stop):
        hi, lo = self.take(pe, n)
        for out, (sh, sl) in zip(outs, still):
            self.released(pe.matmul(out, sh, hi, start=start, stop=False))
            pe.matmul(out, sh, lo, start=False, stop=False)
            last = pe.matmul(out, sl, hi, start=False, stop=stop)
        return last


@contextmanager
def stage(k, *names):
    nc = k.nc
    with ExitStack() as ctx:
        sems = [ctx.enter_context(nc.semaphore(n)) for n in names]
        with nc.Block(no_gpsimd_drain=True) as block:
            yield (block, *sems)
        for s in sems:
            nc.sync.sem_clear(s)
        nc.all_engine_barrier()


@contextmanager
def memory(k, **shapes):
    with ExitStack() as ctx:
        out = []
        for name, shape in shapes.items():
            dt = F32
            if shape[0] == "r":
                dt, shape = F32R, shape[1:]
            k.tensors += 1
            out.append(ctx.enter_context(k.nc.sbuf_tensor(f"{name}_{k.tensors}", [128, *shape], dt)))
        yield out[0] if len(out) == 1 else out


def const(k, name, rows=slice(0, 128)):
    return k.consts[rows, CONST[name]:CONST[name] + _widths[name]]




def split_start(k):
    names = ("zeroed", "consts_in", "x_in", "rounded_x", "split_x")

    def scalar(act, zeroed, consts_in, x_in, rounded_x, split_x):
        for t in range(KT):
            act.dma_start(k.res[:, t, :], k.dram["xT"][:, t, :]).then_inc(x_in, 16)
        act.dma_start(k.consts[:, :], k.dram["consts"]).then_inc(consts_in, 16)
        act.dma_start(k.par1[:, :], k.dram["params1"]).then_inc(consts_in, 16)
        act.dma_start(k.mats1[:, :], k.dram["mats1"]).then_inc(consts_in, 16)
        act.wait_ge(consts_in, 48)

    def gpsimd(pool, zeroed, *_):
        pool.wait_ge(zeroed, 1)

    def tensor(pe, t, zeroed, consts_in, x_in, rounded_x, split_x):
        pe.wait_ge(split_x, t + 1)

    def vector(dve, zeroed, consts_in, x_in, rounded_x, split_x):
        dve.memset(k.ws.zero[:, :], 0.0).then_inc(zeroed, 1)
        dve.memset(k.eps[:, 0:1], 1e-5).then_inc(zeroed, 1)
        dve.memset(k.eps[:, 1:2], 1e-6).then_inc(zeroed, 1)
        dve.memset(k.eps[:, 2:3], 64e-5).then_inc(zeroed, 1)
        dve.memset(k.eps[:, 3:4], 1.0).then_inc(zeroed, 1)
        for t in range(KT):
            if t == 0:
                dve.wait_ge(x_in, 16 * KT)
            dve.tensor_copy(k.xh[:, t, :], k.res[:, t, :]).then_inc(rounded_x, 1)
            dve.wait_ge(rounded_x, t + 1)
            dve.tensor_tensor(k.xl[:, t, :], k.res[:, t, :], k.xh[:, t, :].bitcast(F32), ALU.subtract).then_inc(
                split_x, 1)
    return names, dict(scalar=scalar, gpsimd=gpsimd, tensor=tensor, vector=vector)


def project(k, tiles, out, token_major, moving=None, n_moving=SEQ, first=None, aside=None):
    ws = k.ws
    moving = moving or (k.xh, k.xl)
    nt = n_moving // 128
    ws.plan(tiles * KT + sum(KT * w // 128 for _, w in token_major))
    first_names, first_run = first or ((), {})
    aside_names, aside_run = aside or ((), {})
    with stage(k, "product_ready", "product_copied", "rows_ready", "rows_copied", *first_names, *aside_names) as (
            block, product_ready, product_copied, rows_ready, rows_copied, *sems):
        first_sems, aside_sems = sems[:len(first_names)], sems[len(first_names):]

        @block.sync
        def _(sp):
            if "loads" in aside_run:
                aside_run["loads"](sp, *aside_sems)
            ws.load(sp)

        @block.scalar
        def _(act):
            if "scalar" in first_run:
                first_run["scalar"](act, *first_sems)
            if "scalar" in aside_run:
                aside_run["scalar"](act, *aside_sems)

        @block.gpsimd
        def _(pool):
            if "gpsimd" in first_run:
                first_run["gpsimd"](pool, *first_sems)
            ws.divide(pool)

        @block.tensor
        def _(pe):
            for j in range(tiles):
                if j >= 2:
                    pe.wait_ge(product_copied, j - 1)
                for t in range(KT):
                    if j == 0 and "tensor" in first_run:
                        first_run["tensor"](pe, t, *first_sems)
                    last = ws.product(pe, k.bank[j % 2][:, 0:n_moving],
                                      (moving[0][:, t, 0:n_moving], moving[1][:, t, 0:n_moving]), t == 0, t == KT - 1)
                last.then_inc(product_ready, 1)
                if j == tiles // 2 and "tensor" in aside_run:
                    aside_run["tensor"](pe, *aside_sems)
            for m, (_, width) in enumerate(token_major):
                if m:
                    pe.wait_ge(rows_copied, m)
                for t in range(KT):
                    still = [(moving[0][:, t, 128 * q:128 * q + 128], moving[1][:, t, 128 * q:128 * q + 128])
                             for q in range(nt)]
                    last = ws.product_tm(pe, [k.bank[4 + q][:, 0:width] for q in range(nt)], still, width // 128,
                                         t == 0, t == KT - 1)
                last.then_inc(rows_ready, 1)

        @block.vector
        def _(dve):
            if "vector" in first_run:
                first_run["vector"](dve, *first_sems)
            for j in range(tiles):
                dve.wait_ge(product_ready, j + 1)
                dve.tensor_copy(out[:, j, 0:n_moving], k.bank[j % 2][:, 0:n_moving]).then_inc(product_copied, 1)
                if j == tiles // 2 and "vector" in aside_run:
                    aside_run["vector"](dve, *aside_sems)
            for m, (rows, width) in enumerate(token_major):
                dve.wait_ge(rows_ready, m + 1)
                for q in range(nt):
                    last = dve.tensor_copy(rows[:, q, :], k.bank[4 + q][:, 0:width])
                last.then_inc(rows_copied, 1)


def normalise(k, src, gain, bias, eps, mean, hi=None, lo=None, out=None, n=SEQ, loads=()):
    ones = const(k, "ones")
    with memory(k, nrm_sq=(2, n), nrm_mean=(n,), nrm_rstd=(n,), nrm_c=(KT, n) if mean else (1, 1),
                nrm_y=(3, n)) as (sq, mu, rstd, cent, y), \
            stage(k, "summed", "mean_ready", "centred", "squared", "square_used", "log_ready", "rstd_ready",
                  "scaled", "rounded", "tile_done", "vector_order", "loads_in") as (
                block, summed, mean_ready, centred, squared, square_used, log_ready, rstd_ready, scaled, rounded,
                tile_done, order, loads_in):
        x = cent if mean else src

        @block.sync
        def _(sp):
            for dst, from_dram in loads:
                sp.dma_start(dst, from_dram).then_inc(loads_in, 16)

        @block.tensor
        def _(pe):
            if mean:
                for t in range(KT):
                    last = pe.matmul(k.bank[0][:, 0:n], ones, src[:, t, :], start=t == 0, stop=t == KT - 1)
                last.then_inc(summed, 1)
            for t in range(KT):
                pe.wait_ge(squared, t + 1)
                pe.matmul(k.bank[1][:, 0:n], ones, sq[:, t % 2, :], start=t == 0, stop=t == KT - 1).then_inc(
                    square_used, 1)

        @block.scalar
        def _(act):
            for t in range(KT):
                if mean:
                    act.wait_ge(centred, t + 1)
                if t >= 2:
                    act.wait_ge(square_used, t - 1)
                act.activation(sq[:, t % 2, :], x[:, t, :], ACT.Square).then_inc(squared, 1)
            act.wait_ge(square_used, KT)
            act.activation(rstd[:, :], k.bank[1][:, 0:n], ACT.Ln, scale=1.0 / D, bias=eps).then_inc(log_ready, 1)
            act.wait_ge(log_ready, 1)
            act.activation(rstd[:, :], rstd[:, :], ACT.Exp, scale=-0.5).then_inc(rstd_ready, 1)
            if hi is not None:
                if loads:
                    act.wait_ge(loads_in, 16 * len(loads))
                for t in range(KT):
                    act.wait_ge(scaled, t + 1)
                    act.activation(hi[:, t, :], y[:, t % 3, :], ACT.Identity, scale=gain(t),
                                   bias=0.0 if bias is None else bias(t)).then_inc(rounded, 1)

        @block.vector
        def _(dve):
            if mean:
                dve.wait_ge(summed, 1)
                dve.tensor_scalar(mu[:, :], k.bank[0][:, 0:n], 1.0 / D, None, ALU.mult).then_inc(mean_ready, 1)
                dve.wait_ge(mean_ready, 1)
                for t in range(KT):
                    dve.tensor_tensor(cent[:, t, :], src[:, t, :], mu[:, :], ALU.subtract).then_inc(centred, 1)
            dve.wait_ge(rstd_ready, 1)
            if loads:
                dve.wait_ge(loads_in, 16 * len(loads))
            for i in range(KT + 1):
                if i < KT:
                    if i >= 3:
                        dve.wait_ge(tile_done, i - 2)
                    dve.tensor_tensor(y[:, i % 3, :], x[:, i, :], rstd[:, :], ALU.mult).then_inc(scaled, 1)
                t = i - 1
                if t < 0:
                    continue
                dve.wait_ge(scaled, t + 1)
                if out is not None:
                    last = dve.tensor_scalar(out[:, t, :], y[:, t % 3, :], gain(t), bias(t), ALU.mult, ALU.add)
                    if hi is not None:
                        last.then_inc(order, 1)
                        dve.wait_ge(order, t + 1)
                        dve.wait_ge(rounded, t + 1)
                        last = dve.tensor_tensor(lo[:, t, :], out[:, t, :], hi[:, t, :].bitcast(F32), ALU.subtract)
                else:
                    dve.wait_ge(rounded, t + 1)
                    last = dve.scalar_tensor_tensor(lo[:, t, :], y[:, t % 3, :], gain(t), hi[:, t, :].bitcast(F32),
                                                    ALU.mult, ALU.subtract)
                last.then_inc(tile_done, 1)


def merge(k, scale_residual, x_dram=None):
    ws = k.ws
    with memory(k, yh=("r", KT, SEQ), yl=("r", KT, SEQ), mh=("r", KT, SEQ), ml=("r", KT, SEQ), sig=(2, SEQ),
                part=(2, SEQ)) as (yh, yl, mh, ml, sig, part):
        ws.plan(KT * 40)
        with stage(k, "gate_ready", "sigmoid_ready", "branch_ready", "banks_free", "branch_rounded", "merge_order",
                   "branch_split", "x_in") as (block, gate_ready, sigmoid_ready, branch_ready, banks_free, rounded,
                                               order, branch_split, x_in):
            @block.sync
            def _(sp):
                if x_dram is not None:
                    sp.dma_start(k.res[:, :, :], x_dram).then_inc(x_in, 16)
                ws.load(sp)
                if x_dram is not None:
                    sp.wait_ge(x_in, 16)

            @block.gpsimd
            def _(pool):
                ws.divide(pool)

            @block.tensor
            def _(pe):
                for dt in range(KT):
                    for n in range(4):
                        u = 4 * dt + n
                        if u >= 2:
                            pe.wait_ge(banks_free, u - 1)
                        g, b = k.bank[2 * (u % 2)], k.bank[2 * (u % 2) + 1]
                        for t in range(KT):
                            last = ws.product(pe, g[:, :], (k.xh[:, t, :], k.xl[:, t, :]), t == 0, t == KT - 1)
                        last.then_inc(gate_ready, 1)
                        if u == 0:
                            pe.wait_ge(branch_split, KT)
                        for c in range(2):
                            last = ws.product(pe, b[:, :], (yh[:, 2 * n + c, :], yl[:, 2 * n + c, :]), c == 0, c == 1)
                        last.then_inc(branch_ready, 1)

            @block.scalar
            def _(act):
                for u in range(4 * KT):
                    act.wait_ge(gate_ready, u + 1)
                    if u >= 2:
                        act.wait_ge(banks_free, u - 1)
                    act.activation(sig[:, u % 2, :], k.bank[2 * (u % 2)][:, :], ACT.Sigmoid).then_inc(
                        sigmoid_ready, 1)

            @block.vector
            def _(dve):
                step = Order(dve, order)
                for t in range(KT):
                    step(dve.tensor_copy(yh[:, t, :], k.yb[:, t, :]))
                    dve.tensor_tensor(yl[:, t, :], k.yb[:, t, :], yh[:, t, :].bitcast(F32), ALU.subtract).then_inc(
                        branch_split, 1)
                for dt in range(KT):
                    for n in range(4):
                        u = 4 * dt + n
                        dve.wait_ge(sigmoid_ready, u + 1)
                        dve.wait_ge(branch_ready, u + 1)
                        dve.tensor_tensor(part[:, 0 if n == 0 else 1, :], sig[:, u % 2, :],
                                          k.bank[2 * (u % 2) + 1][:, :], ALU.mult).then_inc(banks_free, 1)
                        dve.wait_ge(banks_free, u + 1)
                        if n:
                            step(dve.tensor_tensor(part[:, 0, :], part[:, 0, :], part[:, 1, :], ALU.add))
                    step(dve.tensor_copy(mh[:, dt, :], part[:, 0, :]))
                    step(dve.tensor_tensor(ml[:, dt, :], part[:, 0, :], mh[:, dt, :].bitcast(F32), ALU.subtract))
        add_product(k, KT, mh, ml, scale_residual)


def add_product(k, tiles_in, hi, lo, scale_residual):
    ws = k.ws
    ws.plan(KT * tiles_in)
    with stage(k, "product_ready", "product_added") as (block, product_ready, product_added):
        @block.sync
        def _(sp):
            ws.load(sp)

        @block.gpsimd
        def _(pool):
            ws.divide(pool)

        @block.tensor
        def _(pe):
            for dt in range(KT):
                if dt >= 2:
                    pe.wait_ge(product_added, dt - 1)
                for t in range(tiles_in):
                    last = ws.product(pe, k.bank[dt % 2][:, :], (hi[:, t, :], lo[:, t, :]), t == 0,
                                      t == tiles_in - 1)
                last.then_inc(product_ready, 1)

        @block.vector
        def _(dve):
            for dt in range(KT):
                dve.wait_ge(product_ready, dt + 1)
                dve.scalar_tensor_tensor(k.res[:, dt, :], k.res[:, dt, :], scale_residual, k.bank[dt % 2][:, :],
                                         ALU.mult, ALU.add).then_inc(product_added, 1)


def attention(k, units, outs, strip_loads=(), strips_per=1):
    n_units = len(units)
    last_of_pair = {}
    last_of_strip = {}
    for i, u in enumerate(units):
        last_of_pair[u["pair"]] = i
        if u["strip"] is not None:
            last_of_strip[u["strip"]] = i
    with memory(k, att_p=(3, SEQ), att_t=(2, SEQ), att_s=(3, 4)) as (prob, probt, small), \
            stage(k, "scores_ready", "biased", "exp_ready", "probs_ready", "turned", "turned_copied", "unit_done",
                  "pair_copied", "vector_order", "strip_even", "strip_odd") as (
                block, scores_ready, biased, exp_ready, probs_ready, turned, turned_copied, unit_done, pair_copied,
                order, strip_even, strip_odd):
        strip_sem = (strip_even, strip_odd)
        score_bank = lambda i: k.bank[i % 3]
        turn_bank = lambda i: k.bank[3 + i % 2]
        pair_bank = lambda p: k.bank[5 + p % 2]

        @block.sync
        def _(sp):
            for s, (dst, src) in enumerate(strip_loads):
                if s >= 2:
                    sp.wait_ge(biased, last_of_strip[s - 2] + 1)
                sp.dma_start(dst, src).then_inc(strip_sem[s % 2], 16)

        @block.tensor
        def _(pe):
            for i in range(n_units + 3):
                if i < n_units:
                    u = units[i]
                    if i >= 3:
                        pe.wait_ge(biased, i - 2)
                    pe.matmul(score_bank(i)[:, 0:u["n"]], u["q"], u["keys"], start=True, stop=True).then_inc(
                        scores_ready, 1)
                v = i - 2
                if 0 <= v < n_units:
                    pe.wait_ge(probs_ready, v + 1)
                    if v >= 2:
                        pe.wait_ge(turned_copied, v - 1)
                    for j in range(units[v]["n"] // 128):
                        last = pe.transpose(turn_bank(v)[:, 128 * j:128 * j + 128],
                                            prob[:, v % 3, 128 * j:128 * j + 128], const(k, "ident"))
                    last.then_inc(turned, 1)
                w = i - 3
                if w >= 0:
                    u = units[w]
                    pe.wait_ge(turned_copied, w + 1)
                    if u["pair"] >= 2:
                        pe.wait_ge(pair_copied, u["pair"] - 1)
                    nj = u["n"] // 128
                    for j in range(nj):
                        last = pe.matmul(pair_bank(u["pair"])[u["rows"], u["cols"]], u["values"][j],
                                         probt[:, w % 2, 128 * j:128 * j + 128], start=j == 0, stop=j == nj - 1)
                    last.then_inc(unit_done, 1)

        @block.scalar
        def _(act):
            for i in range(n_units + 2):
                if i < n_units:
                    u = units[i]
                    act.wait_ge(biased, i + 1)
                    act.activation(prob[:, i % 3, 0:u["n"]], prob[:, i % 3, 0:u["n"]], ACT.Exp,
                                   bias=small[:, i % 3, 0:1], accum_out=small[:, i % 3, 1:2]).then_inc(exp_ready, 1)
                v = i - 2
                if v >= 0:
                    n = units[v]["n"]
                    act.wait_ge(turned, v + 1)
                    if v >= 2:
                        act.wait_ge(unit_done, v - 1)
                    act.activation(probt[:, v % 2, 0:n], turn_bank(v)[:, 0:n], ACT.Copy).then_inc(turned_copied, 1)

        @block.vector
        def _(dve):
            step = Order(dve, order)
            waited = -1
            for i in range(n_units + 1):
                if i < n_units:
                    u = units[i]
                    p = prob[:, i % 3, 0:u["n"]]
                    dve.wait_ge(scores_ready, i + 1)
                    if i >= 3:
                        dve.wait_ge(turned, i - 2)
                    if u["strip"] is not None and u["strip"] != waited:
                        waited = u["strip"]
                        dve.wait_ge(strip_sem[waited % 2], 16 * (waited // 2 + 1))
                    s = score_bank(i)[:, 0:u["n"]]
                    if u["bias"] is None:
                        step(dve.tensor_scalar(p, s, u["scale"], None, ALU.mult))
                    else:
                        step(dve.scalar_tensor_tensor(p, s, u["scale"], u["bias"], ALU.mult, ALU.add))
                    if u["select"] is not None:
                        step(dve.tensor_tensor(p, p, u["select"], ALU.add))
                    dve.tensor_reduce(small[:, i % 3, 0:1], p, AX.X, ALU.max, negate=True).then_inc(biased, 1)
                v = i - 1
                if v >= 0:
                    b, n = v % 3, units[v]["n"]
                    dve.wait_ge(exp_ready, v + 1)
                    step(dve.reciprocal(small[:, b, 2:3], small[:, b, 1:2]))
                    dve.tensor_scalar(prob[:, b, 0:n], prob[:, b, 0:n], small[:, b, 2:3], None, ALU.mult).then_inc(
                        probs_ready, 1)
                    pair = units[v]["pair"]
                    if last_of_pair[pair] == v and pair >= 1:
                        dve.wait_ge(unit_done, last_of_pair[pair - 1] + 1)
                        dve.tensor_copy(outs[pair - 1], pair_bank(pair - 1)[:, :]).then_inc(pair_copied, 1)
            pair = units[-1]["pair"]
            dve.wait_ge(unit_done, n_units)
            dve.tensor_copy(outs[pair], pair_bank(pair)[:, :]).then_inc(pair_copied, 1)




def distance_bias(k, bias_dram, rows, tab, out):
    names = ("rows_in", "bias_ready", "bias_copied", "bias_stored")

    def loads(sp, rows_in, *_):
        sp.dma_start(rows[0:34, :], k.dram["dist_rows"]).then_inc(rows_in, 16)
        sp.dma_start(tab[0:34, :], k.dram["rpb"]).then_inc(rows_in, 16)

    def scalar(act, rows_in, bias_ready, bias_copied, bias_stored):
        act.wait_ge(bias_copied, 2)
        for h in range(8):
            row = out[h:h + 1, :].rearrange("p (a x) -> p a x", a=1).to_broadcast([1, 128, 1024])
            act.dma_start(bias_dram[h:h + 1, :, :], row).then_inc(bias_stored, 16)
        act.wait_ge(bias_stored, 128)

    def tensor(pe, rows_in, bias_ready, bias_copied, bias_stored):
        pe.wait_ge(rows_in, 32)
        for j in range(2):
            pe.matmul(k.bank[2 + j][0:8, :], tab[0:34, :], rows[0:34, 512 * j:512 * j + 512], start=True,
                      stop=True).then_inc(bias_ready, 1)

    def vector(dve, rows_in, bias_ready, bias_copied, bias_stored):
        for j in range(2):
            dve.wait_ge(bias_ready, j + 1)
            dve.tensor_copy(out[0:8, 512 * j:512 * j + 512], k.bank[2 + j][0:8, :]).then_inc(bias_copied, 1)
    return names, dict(loads=loads, scalar=scalar, tensor=tensor, vector=vector)


def head_norm(k, jobs, n=SEQ):
    blk = const(k, "blk64")
    with memory(k, hn_sq=(2, n), hn_r=(2, n)) as (sq, r), \
            stage(k, "squared", "summed", "log_ready", "rstd_ready", "finished", "vector_order") as (
                block, squared, summed, log_ready, rstd_ready, finished, order):
        @block.tensor
        def _(pe):
            for i, job in enumerate(jobs):
                pe.wait_ge(squared, i + 1)
                if i >= 2:
                    pe.wait_ge(log_ready, i - 1)
                pe.matmul(k.bank[i % 2][:, 0:n], blk, sq[:, i % 2, :], start=True, stop=True).then_inc(summed, 1)

        @block.scalar
        def _(act):
            for i in range(len(jobs) + 1):
                if i < len(jobs):
                    if i >= 2:
                        act.wait_ge(summed, i - 1)
                    act.activation(sq[:, i % 2, :], jobs[i]["src"], ACT.Square).then_inc(squared, 1)
                if i >= 1:
                    b = (i - 1) % 2
                    act.wait_ge(summed, i)
                    if i >= 3:
                        act.wait_ge(finished, i - 2)
                    act.activation(r[:, b, :], k.bank[b][:, 0:n], ACT.Ln, scale=jobs[i - 1]["scale"],
                                   bias=jobs[i - 1]["eps"]).then_inc(log_ready, 1)
                    act.wait_ge(log_ready, i)
                    act.activation(r[:, b, :], r[:, b, :], ACT.Exp, scale=-0.5).then_inc(rstd_ready, 1)

        @block.vector
        def _(dve):
            step = Order(dve, order)
            for i, job in enumerate(jobs):
                dve.wait_ge(rstd_ready, i + 1)
                job["finish"](dve, step, r[:, i % 2, :]).then_inc(finished, 1)
                dve.wait_ge(finished, i + 1)


def gained(src, gain):
    def finish(dve, step, rstd):
        step(dve.tensor_tensor(src, src, rstd, ALU.mult))
        return dve.tensor_scalar(src, src, gain, None, ALU.mult)
    return finish


def turn(k, jobs):
    with stage(k, "turned", "turned_copied") as (block, turned, turned_copied):
        @block.tensor
        def _(pe):
            for i, (_, srcs) in enumerate(jobs):
                if i >= 2:
                    pe.wait_ge(turned_copied, i - 1)
                for j, s in enumerate(srcs):
                    last = pe.transpose(k.bank[i % 2][:, 128 * j:128 * j + 128], s, const(k, "ident"))
                last.then_inc(turned, 1)

        @block.vector
        def _(dve):
            for i, (out, srcs) in enumerate(jobs):
                dve.wait_ge(turned, i + 1)
                dve.tensor_copy(out, k.bank[i % 2][:, 0:128 * len(srcs)]).then_inc(turned_copied, 1)


def select_keys(k, pj, lowt, select):
    heads, keep = 8, 128
    with memory(k, ix_rel=(2, SEQ), ix_score=(SEQ,), ix_top=(8,)) as (rel, score, top), \
            stage(k, "score_ready", "rel_ready", "rel_used", "bank_read", "vector_order") as (
                block, score_ready, rel_ready, rel_used, bank_read, order):
        units = [(i, h) for i in (1, 2, 3) for h in range(heads)]

        @block.tensor
        def _(pe):
            for u, (i, h) in enumerate(units):
                if u >= 2:
                    pe.wait_ge(rel_ready, u - 1)
                rows = slice(32 * (h % 4), 32 * (h % 4) + 32)
                pe.matmul(k.bank[u % 2][:, 0:128 * i + 128],
                          pj[rows, T1["iq"] + h // 4, 128 * i:128 * i + 128],
                          pj[rows, T1["ik"], 0:128 * i + 128], start=True, stop=True).then_inc(score_ready, 1)

        @block.scalar
        def _(act):
            for u, (i, h) in enumerate(units):
                act.wait_ge(score_ready, u + 1)
                if u >= 2:
                    act.wait_ge(rel_used, u - 1)
                n = 128 * i + 128
                act.activation(rel[:, u % 2, 0:n], k.bank[u % 2][:, 0:n], ACT.Relu, scale=32 ** -0.5).then_inc(
                    rel_ready, 1)

        @block.vector
        def _(dve):
            step = Order(dve, order)
            for u, (i, h) in enumerate(units):
                n = 128 * i + 128
                s = score[:, 0:n]
                dve.wait_ge(rel_ready, u + 1)
                weight = lowt[:, i, 112 + h:113 + h]
                if h == 0:
                    dve.tensor_scalar(s, rel[:, u % 2, 0:n], weight, None, ALU.mult).then_inc(rel_used, 1)
                else:
                    dve.scalar_tensor_tensor(s, rel[:, u % 2, 0:n], weight, s, ALU.mult, ALU.add).then_inc(
                        rel_used, 1)
                dve.wait_ge(rel_used, u + 1)
                if h < heads - 1:
                    continue
                step(dve.tensor_scalar(s, s, heads ** -0.5, None, ALU.mult))
                step(dve.tensor_tensor(score[:, n - 128:n], score[:, n - 128:n], const(k, "future"), ALU.add))
                for _ in range(keep // 8):
                    step(dve.max(top[:, :], s))
                    step(dve.match_replace(s, top[:, :], s, TAKEN))
                step(dve.tensor_scalar(select[:, i - 1, 0:n], s, TAKEN / 2, MASKED, ALU.is_gt, ALU.mult))


def mixers_ab(k, pj, av, bias_dram):
    yb = k.yb
    kv = pj[:, T1["ckv"], :]
    g = k.par1[:, P1["kv_gain"]:P1["kv_gain"] + 1]
    head_norm(k, [dict(src=kv, scale=1.0 / 64, eps=k.eps[:, 1:2], finish=gained(kv, g))])
    with memory(k, low_t=(4, 128), kv_t=(4, 128), strips=(2, STRIP)) as (lowt, kvt, strips):
        tiles = [slice(128 * t, 128 * t + 128) for t in range(4)]
        turn(k, [(lowt[:, :, :], [pj[:, T1["low"], t] for t in tiles]),
                 (kvt[:, :, :], [pj[:, T1["ckv"], t] for t in tiles])])
        select = k.res[:, 0:3, :]
        select_keys(k, pj, lowt, select)
        units, loads = [], []
        for head in range(8):
            b, h = divmod(head, 4)
            rows = slice(64 * (h % 2), 64 * (h % 2) + 64)
            loads.append((strips[:, head % 2, :],
                          bass.AP(tensor=bias_dram.tensor, offset=128 * 1024 * head + 127,
                                  ap=[[1023, 128], [1, STRIP]])))
            for i in range(4):
                n = 128 * i + 128
                q = pj[rows, (T1["aq"], T1["bq"])[b] + h // 2, tiles[i]]
                if b == 0:
                    keys = pj[rows, T1["ak"] + h // 2, 0:n]
                    values = [av[:, j, 64 * h:64 * h + 64] for j in range(i + 1)]
                else:
                    keys = pj[rows, T1["ckv"], 0:n]
                    values = [kvt[:, j, 0:64] for j in range(i + 1)]
                units.append(dict(q=q, keys=keys, n=n, scale=0.125, strip=head, values=values, pair=2 * b + h // 2,
                                  bias=strips[:, head % 2, 384 - 128 * i:384 - 128 * i + n],
                                  select=select[:, i - 1, 0:n] if b and i else None, rows=rows, cols=tiles[i]))
        attention(k, units, [yb[:, 0, :], yb[:, 1, :], yb[:, 2, :], yb[:, 3, :]], strip_loads=loads)
    small_products(k, [(yb[:, 2 + p, :], k.mats1[:, 256 + 128 * p:384 + 128 * p], yb[:, 2 + p, :], None)
                       for p in range(2)])


def small_products(k, jobs):
    with stage(k, "product_ready", "product_copied") as (block, product_ready, product_copied):
        @block.tensor
        def _(pe):
            for i, (_, lhs, rhs, _) in enumerate(jobs):
                if i >= 2:
                    pe.wait_ge(product_copied, i - 1)
                pe.matmul(k.bank[i % 2][:, 0:rhs.shape[-1]], lhs, rhs, start=True, stop=True).then_inc(
                    product_ready, 1)

        @block.vector
        def _(dve):
            for i, (out, _, rhs, scale) in enumerate(jobs):
                dve.wait_ge(product_ready, i + 1)
                b = k.bank[i % 2][:, 0:rhs.shape[-1]]
                if scale is None:
                    dve.tensor_copy(out, b).then_inc(product_copied, 1)
                else:
                    dve.tensor_scalar(out, b, scale, None, ALU.mult).then_inc(product_copied, 1)


def mixer_c(k, pj, cv):
    p1 = lambda n, j=0: k.par1[:, P1[n] + j:P1[n] + j + 1]
    q, key = pj[:, T1["cq"], :], pj[:, T1["ck"], :]
    chunked = lambda ap: ap.rearrange("p (c t) -> p c t", t=64)
    with memory(k, cum=(SEQ,), dec=(8,), e_tmp=(SEQ,), qd=(SEQ,), ki=(SEQ,), ku=(SEQ,), kut=(4, 128), att=(4, 4, 128),
                st=(8, 256)) as (cum, dec, tmp, qd, ki, ku, kut, att, st):
        with stage(k, "gate_ready", "abs_ready", "exp_ready", "log_ready", "cum_ready", "decays_ready",
                   "vector_order") as (block, gate_ready, abs_ready, exp_ready, log_ready, cum_ready, decays_ready,
                                       order):
            @block.tensor
            def _(pe):
                pe.matmul(k.bank[0][:, :], k.mats1[96:112, 0:128], pj[96:112, T1["low"], :], start=True,
                          stop=True).then_inc(gate_ready, 1)

            @block.scalar
            def _(act):
                act.wait_ge(abs_ready, 1)
                act.activation(tmp[:, :], tmp[:, :], ACT.Exp, scale=-1.0).then_inc(exp_ready, 1)
                act.wait_ge(exp_ready, 1)
                act.activation(tmp[:, :], tmp[:, :], ACT.Ln, bias=k.eps[:, 3:4]).then_inc(log_ready, 1)
                act.wait_ge(cum_ready, 1)
                act.activation(qd[:, :], cum[:, :], ACT.Exp).then_inc(decays_ready, 1)
                act.activation(ki[:, :], cum[:, :], ACT.Exp, scale=-1.0).then_inc(decays_ready, 1)
                act.activation(dec[:, :], chunked(cum[:, :])[:, :, 63], ACT.Exp).then_inc(decays_ready, 1)
                act.wait_ge(cum_ready, 2)
                act.activation(ku[:, :], tmp[:, :], ACT.Exp).then_inc(decays_ready, 1)

            @block.vector
            def _(dve):
                step = Order(dve, order)
                dve.wait_ge(gate_ready, 1)
                step(dve.tensor_scalar(cum[:, :], k.bank[0][:, :], p1("a_bias"), None, ALU.add))
                step(dve.tensor_scalar(ku[:, :], cum[:, :], -1.0, None, ALU.mult))
                dve.tensor_tensor(tmp[:, :], cum[:, :], ku[:, :], ALU.max).then_inc(abs_ready, 1)
                dve.wait_ge(abs_ready, 1)
                step(dve.tensor_scalar(ku[:, :], cum[:, :], 0.0, 1.0 / 16, ALU.min, ALU.mult))
                dve.wait_ge(log_ready, 1)
                step(dve.scalar_tensor_tensor(ku[:, :], tmp[:, :], -1.0 / 16, ku[:, :], ALU.mult, ALU.add))
                dve.tensor_tensor_scan(cum[:, :], const(k, "reset64"), ku[:, :], 0.0, ALU.mult, ALU.add).then_inc(
                    cum_ready, 1)
                dve.wait_ge(cum_ready, 1)
                last = chunked(cum[:, :])[:, :, 63:64].to_broadcast([128, 8, 64])
                dve.tensor_tensor(chunked(tmp[:, :]), last, chunked(cum[:, :]), ALU.subtract).then_inc(cum_ready, 1)
                dve.wait_ge(decays_ready, 4)
                step(dve.scalar_tensor_tensor(qd[:, :], q, 32 ** -0.5, qd[:, :], ALU.mult, ALU.mult))
                step(dve.tensor_tensor(ki[:, :], key, ki[:, :], ALU.mult))
                step(dve.tensor_tensor(ku[:, :], key, ku[:, :], ALU.mult))
                step(dve.memset(st[:, 0, :], 0.0))
        update_bank = lambda n: 2 * (n % 2) + n // 4
        update_cols = lambda n: slice(256 * (n // 2 % 2), 256 * (n // 2 % 2) + 256)
        turn(k, [(kut[:, :, :], [ku[:, 128 * t:128 * t + 128] for t in range(4)])])
        with stage(k, "att_ready", "att_masked", "update_ready", "update_masked", "states_ready", "out_ready",
                   "out_copied", "vector_order") as (block, att_ready, att_masked, update_ready, update_masked,
                                                     states_ready, out_ready, out_copied, order):
            @block.tensor
            def _(pe):
                for n in range(8):
                    rows = slice(64 * (n % 2), 64 * (n % 2) + 64)
                    pe.matmul(k.bank[update_bank(n)][:, update_cols(n)], kut[rows, n // 2, :], cv[rows, n // 2, :],
                              start=True, stop=True).then_inc(update_ready, 1)
                for h in range(4):
                    rows = slice(32 * h, 32 * h + 32)
                    for t in range(4):
                        c = slice(128 * t, 128 * t + 128)
                        last = pe.matmul(k.bank[4 + h][:, c], ki[rows, c], qd[rows, c], start=True, stop=True)
                    last.then_inc(att_ready, 1)
                pe.wait_ge(states_ready, 1)
                pe.wait_ge(att_masked, 4)
                for p in range(2):
                    out = k.bank[p]
                    for n in range(8):
                        pe.matmul(out[:, 64 * n:64 * n + 64], st[:, n, 128 * p:128 * p + 128],
                                  qd[:, 64 * n:64 * n + 64], start=n == 0, stop=False, skip_group_check=True)
                    for h in (2 * p, 2 * p + 1):
                        rows = slice(64 * (h % 2), 64 * (h % 2) + 64)
                        for t in range(4):
                            last = pe.matmul(out[rows, 128 * t:128 * t + 128], cv[:, t, 64 * h:64 * h + 64],
                                             att[:, h, t, :], start=False, stop=(h % 2 == 1 and t == 3),
                                             skip_group_check=True)
                    last.then_inc(out_ready, 1)

            @block.vector
            def _(dve):
                step = Order(dve, order)
                heads = const(k, "gla_heads")
                for n in range(8):
                    dve.wait_ge(update_ready, 8)
                    upd = k.bank[update_bank(n)][:, update_cols(n)]
                    if n < 7:
                        step(dve.tensor_tensor(st[:, n + 1, :], upd, heads, ALU.mult))
                        step(dve.scalar_tensor_tensor(st[:, n + 1, :], st[:, n, :], dec[:, n:n + 1], st[:, n + 1, :],
                                                      ALU.mult, ALU.add))
                dve.tensor_copy(tmp[:, 0:8], dec[:, :]).then_inc(states_ready, 1)
                mask = const(k, "gla_mask").rearrange("p (a t) -> p a t", a=1).to_broadcast([128, 4, 128])
                for h in range(4):
                    dve.wait_ge(att_ready, h + 1)
                    dve.tensor_tensor(att[:, h, :, :], k.bank[4 + h][:, :].rearrange("p (a t) -> p a t", a=4), mask,
                                      ALU.mult).then_inc(att_masked, 1)
                for p in range(2):
                    dve.wait_ge(out_ready, p + 1)
                    dve.tensor_copy(k.yb[:, 4 + p, :], k.bank[p][:, :]).then_inc(out_copied, 1)
    with stage(k, "silu_ready") as (block, silu_ready):
        @block.scalar
        def _(act):
            for p in range(2):
                g = pj[:, T1["cg"] + p, :]
                act.activation(g, g, ACT.Silu).then_inc(silu_ready, 1)

    def finish(p):
        y = k.yb[:, 4 + p, :]

        def run(dve, step, rstd):
            step(dve.tensor_tensor(y, y, rstd, ALU.mult))
            return dve.scalar_tensor_tensor(y, y, p1("c_norm", p), pj[:, T1["cg"] + p, :], ALU.mult, ALU.mult)
        return run

    head_norm(k, [dict(src=k.yb[:, 4 + p, :], scale=1.0 / 64, eps=k.eps[:, 1:2], finish=finish(p))
                  for p in range(2)])


def mixer_d(k, pj, av, cv):
    p1 = lambda n, j=0: k.par1[:, P1[n] + j:P1[n] + j + 1]
    low = pj[:, T1["low"], :]
    tiled = lambda ap: ap.rearrange("p (c t) -> p c t", t=128)
    R, K_, V = T1["dr"], T1["dk"], T1["dv"]
    wk = [pj[:, n, :] for n in range(T1["low"])]
    rs = [k.res[:, n, :] for n in range(KT)]
    lg, cw, ic, ga = wk[0:2], wk[2:4], wk[4:6], wk[6:8]
    kk, bonus = rs[0:2], rs[2:4]
    at, bt = rs[4:6], rs[6:8]
    tmp, tmp2 = wk[8], wk[9]
    rt, kt = pj[:, R:R + 2, :], pj[:, K_:K_ + 2, :]
    cg = [pj[:, n, :] for n in range(T1["cq"], T1["cq"] + 4)]
    sh = cg[0]
    e_dn, e_up, e_a = cg[1], cg[2], cg[3]
    with memory(k, tl=(SEQ,), zs=(2, 4)) as (tl, zs):
        with stage(k, "vector_order") as (block, order):
            @block.vector
            def _(dve):
                step = Order(dve, order)
                for j, t in enumerate([R, R + 1, K_, K_ + 1, V, V + 1, T1["low"]]):
                    z = pj[:, t, :]
                    step(dve.tensor_tensor(sh[:, 1:SEQ], z[:, 0:SEQ - 1], z[:, 1:SEQ], ALU.subtract))
                    step(dve.tensor_scalar(sh[:, 0:1], z[:, 0:1], -1.0, None, ALU.mult))
                    step(dve.scalar_tensor_tensor(z, sh, p1("mu", j), z, ALU.mult, ALU.add))
        with stage(k, "inner_ready", "low_ready", "sigmoids_ready", "gates_copied", "vector_order") as (
                block, inner_ready, low_ready, sigmoids_ready, gates_copied, order):
            @block.scalar
            def _(act):
                act.activation(tl[0:16, :], low[0:16, :], ACT.Tanh).then_inc(inner_ready, 1)
                act.activation(tl[32:48, :], low[32:48, :], ACT.Copy).then_inc(inner_ready, 1)
                act.activation(tl[64:96, :], low[64:96, :], ACT.Sigmoid).then_inc(inner_ready, 1)
                act.wait_ge(low_ready, 6)
                for p in range(2):
                    act.activation(lg[p], k.bank[p][:, :], ACT.Sigmoid, bias=p1("w0", p)).then_inc(sigmoids_ready, 1)
                    act.activation(ic[p], k.bank[2 + p][:, :], ACT.Sigmoid, bias=p1("a0", p)).then_inc(
                        sigmoids_ready, 1)

            @block.tensor
            def _(pe):
                pe.wait_ge(inner_ready, 3)
                for m, rows in enumerate((slice(0, 16), slice(32, 48), slice(64, 96))):
                    for p in range(2):
                        pe.matmul(k.bank[2 * m + p][:, :], k.mats1[rows, 128 * p:128 * p + 128], tl[rows, :],
                                  start=True, stop=True).then_inc(low_ready, 1)

            @block.vector
            def _(dve):
                step = Order(dve, order)
                dve.wait_ge(low_ready, 6)
                for p in range(2):
                    step(dve.tensor_copy(ga[p], k.bank[4 + p][:, :]))
                dve.wait_ge(sigmoids_ready, 4)
                for p in range(2):
                    step(dve.tensor_scalar(lg[p], lg[p], -math.exp(-0.5), None, ALU.mult))
                    step(dve.tensor_tensor_scan(cw[p], const(k, "reset128"), lg[p], 0.0, ALU.mult, ALU.add))
                    step(dve.tensor_scalar(kk[p], pj[:, K_ + p, :], p1("k_k", p), None, ALU.mult))
                    step(dve.tensor_scalar(tmp, ic[p], 1.0, p1("k_a", p), ALU.subtract, ALU.mult))
                    step(dve.scalar_tensor_tensor(pj[:, K_ + p, :], tmp, 1.0, pj[:, K_ + p, :], ALU.add, ALU.mult))
                    step(dve.scalar_tensor_tensor(bonus[p], pj[:, R + p, :], p1("r_k", p), pj[:, K_ + p, :],
                                                  ALU.mult, ALU.mult))
        with stage(k, "squared", "summed", "norm_ready", "exponent_ready", "exps_ready", "exps_used",
                   "scales_ready", "vector_order") as (block, squared, summed, norm_ready, exponent_ready,
                                                       exps_ready, exps_used, scales_ready, order):
            @block.tensor
            def _(pe):
                for p in range(2):
                    pe.matmul(k.bank[2 + p][:, :], const(k, "blk64"), bonus[p], start=True, stop=True)
                for p in range(2):
                    pe.wait_ge(squared, p + 1)
                    pe.matmul(k.bank[p][:, :], const(k, "blk64"), (tl[:, :], sh)[p], start=True, stop=True).then_inc(
                        summed, 1)

            @block.scalar
            def _(act):
                for p in range(2):
                    act.activation((tl[:, :], sh)[p], kk[p], ACT.Square).then_inc(squared, 1)
                for p in range(2):
                    act.wait_ge(summed, p + 1)
                    act.activation((tl[:, :], sh)[p], k.bank[p][:, :], ACT.Sqrt).then_inc(norm_ready, 1)
                for p in range(2):
                    act.wait_ge(exponent_ready, 3 * p + 3)
                    act.activation(e_dn, cw[p], ACT.Exp).then_inc(exps_ready, 1)
                    act.activation(e_up, cw[p], ACT.Exp, scale=-1.0).then_inc(exps_ready, 1)
                    act.activation(e_a, lg[p], ACT.Exp).then_inc(exps_ready, 1)
                    act.activation(zs[:, p, :], zs[:, p, :], ACT.Exp).then_inc(exps_ready, 1)
                    act.wait_ge(exps_used, p + 1)

            @block.vector
            def _(dve):
                step = Order(dve, order)
                dve.wait_ge(summed, 2)
                for p in range(2):
                    nrm = (tl[:, :], sh)[p]
                    step(dve.tensor_tensor(bonus[p], k.bank[2 + p][:, :], pj[:, V + p, :], ALU.mult))
                    dve.wait_ge(norm_ready, p + 1)
                    step(dve.tensor_scalar(nrm, nrm, 1e-12, None, ALU.max))
                    step(dve.reciprocal(nrm, nrm))
                    step(dve.tensor_tensor(kk[p], kk[p], nrm, ALU.mult))
                for p in range(2):
                    c = tiled(cw[p])
                    step(dve.tensor_tensor(zs[:, p, :], c[:, :, 127], c[:, :, 63], ALU.subtract))
                    dve.tensor_tensor(zs[:, p, 0:3], zs[:, p, 0:3], c[:, 1:4, 63], ALU.add).then_inc(
                        exponent_ready, 1)
                    step(dve.tensor_copy(tmp2[:, 0:4], c[:, :, 63]))
                    mid = tmp2[:, 0:4].rearrange("p (c t) -> p c t", t=1).to_broadcast([128, 4, 128])
                    dve.tensor_tensor(c, c, mid, ALU.subtract).then_inc(exponent_ready, 1)
                    dve.wait_ge(exponent_ready, 3 * p + 2)
                    dve.tensor_tensor(lg[p], cw[p], lg[p], ALU.subtract).then_inc(exponent_ready, 1)
                    dve.wait_ge(exps_ready, 4 * p + 4)
                    step(dve.scalar_tensor_tensor(at[p], kk[p], -1.0, e_a, ALU.mult, ALU.mult))
                    step(dve.tensor_tensor(bt[p], kk[p], ic[p], ALU.mult))
                    step(dve.tensor_tensor(bt[p], bt[p], e_up, ALU.mult))
                    step(dve.tensor_tensor(kt[:, p, :], kt[:, p, :], e_up, ALU.mult))
                    dve.tensor_tensor(rt[:, p, :], rt[:, p, :], e_dn, ALU.mult).then_inc(exps_used, 1)
                    dve.wait_ge(exps_used, p + 1)
        vt = pj[:, 0:2, :].rearrange("p a (c n) -> p (a c) n", c=2)
        btt = pj[:, 2:4, :].rearrange("p a (c n) -> p (a c) n", c=2)
        ktt = pj[:, 4:6, :].rearrange("p a (c n) -> p (a c) n", c=2)
        tiles = [slice(128 * t, 128 * t + 128) for t in range(4)]
        jobs = []
        for dst, src in ((vt, [pj[:, V + p, :] for p in range(2)]), (btt, bt), (ktt, [kt[:, 0, :], kt[:, 1, :]])):
            for c in range(0, 4, 2):
                jobs.append((dst[:, c:c + 2, :].rearrange("p c n -> p (c n)"),
                             [src[p][:, tiles[c + e]] for e in range(2) for p in range(2)]))
        turn(k, jobs)
        pairs = lambda rows: [rows[:, t:t + 2, :].rearrange("p a n -> p (a n)") for t in (0, 2)]
        free = cg + [wk[8], wk[9], rs[0], rs[1], low, pj[:, V, :], pj[:, V + 1, :]] + pairs(av) + pairs(cv)
        delta_chunks(k, at, bt, kt, rt, vt, btt, ktt, zs, free)
        y = [k.yb[:, 6, :], k.yb[:, 7, :]]
        with stage(k, "mean_ready", "vector_order") as (block, mean_ready, order):
            @block.tensor
            def _(pe):
                for p in range(2):
                    pe.matmul(k.bank[p][:, :], const(k, "blk64"), y[p], start=True, stop=True).then_inc(
                        mean_ready, 1)

            @block.vector
            def _(dve):
                step = Order(dve, order)
                for p in range(2):
                    dve.wait_ge(mean_ready, p + 1)
                    step(dve.scalar_tensor_tensor(y[p], k.bank[p][:, :], -1.0 / 64, y[p], ALU.mult, ALU.add))

        def finish(p):
            def run(dve, step, rstd):
                step(dve.tensor_tensor(y[p], y[p], rstd, ALU.mult))
                step(dve.tensor_scalar(y[p], y[p], p1("gn_w", p), p1("gn_b", p), ALU.mult, ALU.add))
                step(dve.tensor_tensor(y[p], y[p], bonus[p], ALU.add))
                return dve.tensor_tensor(y[p], y[p], ga[p], ALU.mult)
            return run

        head_norm(k, [dict(src=y[p], scale=1.0 / 64, eps=k.eps[:, 2:3], finish=finish(p)) for p in range(2)])


def delta_chunks(k, at, bt, kt, rt, vt, btt, ktt, zs, free):
    SETS, LAG = 15, 3
    four = lambda ap: ap.rearrange("p (h t) -> p h t", h=4)
    wide = lambda name, n: const(k, name).rearrange("p (a t) -> p a t", a=1).to_broadcast([128, n, 128])
    rows = [slice(64 * (h % 2), 64 * (h % 2) + 64) for h in range(4)]
    quarter = [slice(128 * h, 128 * h + 128) for h in range(4)]
    order_of_sets = []
    for n in range(2 * SETS + LAG):
        if n < 2 * SETS:
            order_of_sets.append((2 * (n // SETS), n % SETS))
        if n >= LAG:
            order_of_sets.append((2 * ((n - LAG) // SETS) + 1, (n - LAG) % SETS))
    before = lambda c, n: SETS * (c // 2) + n
    with memory(k, d_own=(9, SEQ), d_r=(2, 256), d_u=(2, 256), d_z=(2, 64)) as (own, rr_all, uu_all, z), \
            stage(k, "even_products", "odd_products", "even_evacuated", "odd_evacuated", "vector_order") as (
                block, even_products, odd_products, even_evacuated, odd_evacuated, order):
        tiles = free + [own[:, 0, :]]
        lanes = []
        for lane in range(2):
            ed, el, md, nt, bi, ki, s1, s2 = (four(x) for x in tiles[8 * lane:8 * lane + 8])
            pq, pq2 = (own[:, 1 + 4 * lane + 2 * j:3 + 4 * lane + 2 * j, :].rearrange(
                "p a n -> p (a n)").rearrange("p (h t) -> p h t", h=4) for j in range(2))
            lanes.append(dict(ed=ed, el=el, md=md, nt=nt, bi=bi, ki=ki, s1=s1, s2=s2, s3=el, s4=md, s5=ed, pq=pq,
                              pq2=pq2, x=pq2[:, :, 0:128], q=pq2[:, :, 128:256], rr=rr_all[:, lane, :],
                              uu=uu_all[:, lane, :], bank=k.bank[4 * lane:4 * lane + 4]))
        products_done = (even_products, odd_products)
        evacuated = (even_evacuated, odd_evacuated)

        @block.tensor
        def _(pe):
            def by_head(out, left, right):
                for h in range(4):
                    last = pe.matmul(out[:, quarter[h]], left[:, h, :], right[:, h, :], start=True, stop=True)
                return last

            def by_head_wide(outs, left, right):
                for h in range(4):
                    last = pe.matmul(outs[h // 2][:, 256 * (h % 2):256 * (h % 2) + 256], left[:, h, :],
                                     right[:, h, :], start=True, stop=True)
                return last

            for c, n in order_of_sets:
                ln = lanes[c % 2]
                bank, cols = ln["bank"], quarter[c]
                if before(c, n):
                    pe.wait_ge(evacuated[c % 2], before(c, n))
                if n == 0:
                    for h in range(4):
                        p, r = h // 2, rows[h]
                        for m, left in enumerate((bt[p], kt[:, p, :])):
                            b = bank[2 * m + h % 2]
                            pe.matmul(b[:, 256 * p:256 * p + 128], left[r, cols], at[p][r, cols], start=True,
                                      stop=True)
                            last = pe.matmul(b[:, 256 * p + 128:256 * p + 256], left[r, cols], rt[r, p, cols],
                                             start=True, stop=True)
                elif n == 1:
                    for h in range(4):
                        p, r = h // 2, rows[h]
                        last = pe.matmul(bank[h % 2][:, 128 * p:128 * p + 128], at[p][r, cols], bt[p][r, cols],
                                         start=True, stop=True)
                elif n == 2:
                    by_head(bank[0], ln["md"], ln["el"])
                    by_head(bank[1], ln["md"], ln["ed"])
                    last = by_head(bank[2], ln["ed"], ln["md"])
                elif n == 3:
                    by_head(bank[0], ln["s2"], ln["s1"])
                    by_head(bank[1], ln["s1"], ln["s2"])
                    last = by_head_wide(bank[2:4], ln["s2"], ln["pq"])
                elif n == 4:
                    by_head(bank[1], ln["s3"], ln["s4"])
                    last = by_head_wide(bank[2:4], ln["s4"], ln["pq2"])
                elif n == 5:
                    last = by_head_wide(bank[2:4], ln["s2"], ln["pq"])
                elif n == 6:
                    for h in range(4):
                        last = pe.transpose(bank[0][:, quarter[h]], ln["pq2"][:, h, 128:256], const(k, "ident"))
                elif n == 7:
                    by_head(bank[1], ln["s5"], ln["q"])
                    last = by_head(bank[2], ln["q"], ln["s5"])
                elif n == 8:
                    last = by_head(bank[1], ln["s1"], ln["s2"])
                elif n <= 11:
                    last = by_head(bank[0], ln[("s3", "s2", "s5")[n - 9]], ln["x"])
                elif n == 12:
                    if c:
                        pe.wait_ge(evacuated[(c - 1) % 2], before(c - 1, SETS))
                    for h in range(4):
                        p, r = h // 2, rows[h]
                        o = bank[1 + h % 2][:, 64 * p:64 * p + 64]
                        if c:
                            pe.matmul(o, at[p][r, cols], z[r, p, :], start=True, stop=False)
                        last = pe.matmul(o, ln["nt"][:, h, :], vt[:, c, 64 * h:64 * h + 64], start=not c, stop=True)
                elif n == 13:
                    for h in range(4):
                        hs = slice(64 * h, 64 * h + 64)
                        last = pe.matmul(bank[3][:, hs], ln["x"][:, h, :], ln["rr"][:, hs], start=True, stop=True)
                else:
                    for h in range(4):
                        p, r = h // 2, rows[h]
                        us, vs = ln["uu"][:, 64 * h:64 * h + 64], vt[:, c, 64 * h:64 * h + 64]
                        if c < 3:
                            o = bank[2][r, 64 * p:64 * p + 64]
                            pe.matmul(o, btt[:, c, 64 * h:64 * h + 64], us, start=True, stop=False)
                            pe.matmul(o, ktt[:, c, 64 * h:64 * h + 64], vs, start=False, stop=True)
                        o = bank[h % 2][r, 128 * p:128 * p + 128]
                        if c:
                            pe.matmul(o, z[r, p, :], rt[r, p, cols], start=True, stop=False)
                        pe.matmul(o, us, ln["bi"][:, h, :], start=not c, stop=False)
                        last = pe.matmul(o, vs, ln["ki"][:, h, :], start=False, stop=True)
                last.then_inc(products_done[c % 2], 1)

        @block.vector
        def _(dve):
            step = Order(dve, order)

            def grow(dst, src, banks):
                for p in range(2):
                    a = slice(2 * p, 2 * p + 2)
                    last = dve.tensor_tensor(dst[:, a, :], src[:, a, :],
                                             banks[p][:, :].rearrange("p (h t) -> p h t", h=2), ALU.add)
                    if p == 0:
                        step(last)
                return last

            for c, n in order_of_sets:
                ln = lanes[c % 2]
                bank = ln["bank"]
                dve.wait_ge(products_done[c % 2], before(c, n) + 1)
                if n == 0:
                    for p in range(2):
                        b = bank[p][:, :].rearrange("p (h g t) -> p h g t", h=2, g=2)
                        m = bank[2 + p][:, :].rearrange("p (h g t) -> p h g t", h=2, g=2)
                        hs = slice(p, 4, 2)
                        step(dve.tensor_tensor(ln["ed"][:, hs, :], b[:, :, 0, :], wide("up_same", 2), ALU.mult))
                        step(dve.tensor_tensor(ln["el"][:, hs, :], b[:, :, 0, :], wide("up_other", 2), ALU.mult))
                        step(dve.tensor_tensor(ln["bi"][:, hs, :], b[:, :, 1, :], wide("up_diag", 2), ALU.mult))
                        step(dve.tensor_tensor(ln["nt"][:, hs, :], m[:, :, 0, :], wide("up", 2), ALU.mult))
                        step(dve.tensor_tensor(ln["ki"][:, hs, :], m[:, :, 1, :], wide("up_diag", 2), ALU.mult))
                    last = dve.tensor_tensor(ln["pq"][:, :, 0:128], ln["ed"][:, :, :], wide("ident", 4), ALU.add)
                elif n == 1:
                    for p in range(2):
                        last = dve.tensor_tensor(ln["md"][:, p:4:2, :],
                                                 bank[p][:, 0:256].rearrange("p (h t) -> p h t", h=2),
                                                 wide("low_same", 2), ALU.mult)
                        if p == 0:
                            step(last)
                elif n == 2:
                    step(dve.tensor_tensor(ln["pq"][:, :, 128:256], ln["el"][:, :, :], four(bank[0][:, :]), ALU.add))
                    step(dve.tensor_copy(ln["s1"][:, :, :], four(bank[1][:, :])))
                    last = dve.tensor_copy(ln["s2"][:, :, :], four(bank[2][:, :]))
                elif n == 3:
                    step(dve.tensor_copy(ln["s3"][:, :, :], four(bank[0][:, :])))
                    step(dve.tensor_copy(ln["s4"][:, :, :], four(bank[1][:, :])))
                    last = grow(ln["pq2"], ln["pq"], bank[2:4])
                elif n == 4:
                    step(dve.tensor_copy(ln["s2"][:, :, :], four(bank[1][:, :])))
                    last = grow(ln["pq"], ln["pq2"], bank[2:4])
                elif n == 5:
                    last = grow(ln["pq2"], ln["pq"], bank[2:4])
                elif n == 6:
                    last = dve.tensor_copy(ln["s5"][:, :, :], four(bank[0][:, :]))
                elif n == 7:
                    step(dve.tensor_copy(ln["s1"][:, :, :], four(bank[1][:, :])))
                    last = dve.tensor_copy(ln["s2"][:, :, :], four(bank[2][:, :]))
                elif n == 8:
                    last = dve.tensor_copy(ln["s3"][:, :, :], four(bank[1][:, :]))
                elif n <= 11:
                    last = dve.tensor_tensor(ln["x"], ln["x"], four(bank[0][:, :]), ALU.add)
                elif n == 12:
                    for p in range(2):
                        last = dve.tensor_copy(ln["rr"].rearrange("p (h v) -> p h v", h=4)[:, p:4:2, :],
                                               bank[1 + p][:, 0:128].rearrange("p (h v) -> p h v", h=2))
                        if p == 0:
                            step(last)
                elif n == 13:
                    last = dve.tensor_copy(ln["uu"], bank[3][:, 0:256])
                else:
                    for p in range(2):
                        r = rows[p]
                        last = dve.tensor_copy(k.yb[r, 6:8, quarter[c]],
                                               bank[p][r, 0:256].rearrange("p (a t) -> p a t", a=2))
                        if p == 0:
                            step(last)
                    if c < 3:
                        step(last)
                        b = bank[2][:, 0:128].rearrange("p (a t) -> p a t", a=2)
                        if c:
                            step(dve.tensor_tensor(z[:, :, :], z[:, :, :], b, ALU.add))
                        else:
                            step(dve.tensor_copy(z[:, :, :], b))
                        step(dve.tensor_scalar(z[:, 0, :], z[:, 0, :], zs[:, 0, c:c + 1], None, ALU.mult))
                        last = dve.tensor_scalar(z[:, 1, :], z[:, 1, :], zs[:, 1, c:c + 1], None, ALU.mult)
                last.then_inc(evacuated[c % 2], 1)




def route(k, gate_dram):
    ws = k.ws
    ws.plan(8)
    bias = k.mats1[:, 512:548]
    four = lambda name: const(k, name).rearrange("p (q e) -> p q e", q=4)
    with memory(k, lg=(4, 128), pick=(4, 4), m=(4, 8), le=(4, 32), hot=(4, 32), hot2=(4, 32), gate=(4, 32),
                wide=(4, 32), gate_t=(512,)) as (lg, pick, m, le, hot, hot2, gate, wide, gate_t), \
            stage(k, "logits_ready", "exp_ready", "best_ready", "gates_ready", "turned", "turned_copied", "stored",
                  "vector_order") as (block, logits_ready, exp_ready, best_ready, gates_ready, turned,
                                      turned_copied, stored, order):
        bc = lambda ap, n: ap.to_broadcast([128, 4, n])

        @block.sync
        def _(sp):
            ws.load(sp)
            sp.wait_ge(turned_copied, 1)
            sp.dma_start(gate_dram, gate_t[0:32, :]).then_inc(stored, 16)
            sp.wait_ge(stored, 16)

        @block.gpsimd
        def _(pool):
            ws.divide(pool)

        @block.tensor
        def _(pe):
            for t in range(KT):
                still = [(k.xh[:, t, 128 * q:128 * q + 128], k.xl[:, t, 128 * q:128 * q + 128]) for q in range(4)]
                last = ws.product_tm(pe, [k.bank[q][:, 0:128] for q in range(4)], still, 1, t == 0, t == KT - 1)
            last.then_inc(logits_ready, 1)
            pe.wait_ge(gates_ready, 1)
            for q in range(4):
                last = pe.transpose(k.bank[4][0:32, 128 * q:128 * q + 128], gate[:, q, :], const(k, "ident"))
            last.then_inc(turned, 1)

        @block.scalar
        def _(act):
            act.wait_ge(best_ready, 1)
            act.activation(m[:, :, 4:8], lg[:, :, 0:4], ACT.Exp).then_inc(exp_ready, 1)
            act.wait_ge(best_ready, 2)
            act.activation(m[:, :, 3:4], m[:, :, 3:4], ACT.Exp).then_inc(exp_ready, 1)

        @block.vector
        def _(dve):
            step = Order(dve, order)
            dve.wait_ge(logits_ready, 1)
            for q in range(4):
                step(dve.tensor_tensor(lg[:, q, 0:36], k.bank[q][:, 0:36], bias, ALU.add))
            step(dve.tensor_reduce(m[:, :, 0:1], lg[:, :, 0:4], AX.X, ALU.max))
            step(dve.tensor_tensor(pick[:, :, :], lg[:, :, 0:4], bc(m[:, :, 0:1], 4), ALU.is_equal))
            dve.tensor_tensor(lg[:, :, 0:4], lg[:, :, 0:4], bc(m[:, :, 0:1], 4), ALU.subtract).then_inc(best_ready, 1)
            step(dve.tensor_tensor(pick[:, :, :], pick[:, :, :], four("rank8")[:, :, 0:4], ALU.mult))
            step(dve.tensor_reduce(m[:, :, 1:2], pick[:, :, :], AX.X, ALU.max))
            step(dve.tensor_tensor(pick[:, :, :], pick[:, :, :], bc(m[:, :, 1:2], 4), ALU.is_equal))
            dve.wait_ge(exp_ready, 1)
            step(dve.tensor_reduce(m[:, :, 2:3], m[:, :, 4:8], AX.X, ALU.add))
            step(dve.reciprocal(m[:, :, 2:3], m[:, :, 2:3]))
            spread = pick[:, :, :].rearrange("p q (g a) -> p (q g) a", a=1).to_broadcast([128, 16, 8])
            groups = lambda ap: ap.rearrange("p q (g e) -> p (q g) e", e=8)
            step(dve.tensor_copy(groups(wide[:, :, :]), spread))
            step(dve.tensor_tensor(le[:, :, :], lg[:, :, 4:36], wide[:, :, :], ALU.mult))
            step(dve.tensor_scalar(wide[:, :, :], wide[:, :, :], 1.0, -MASKED, ALU.subtract, ALU.mult))
            step(dve.tensor_tensor(le[:, :, :], le[:, :, :], wide[:, :, :], ALU.add))
            for hots, at in ((hot, 0), (hot2, 1)):
                step(dve.tensor_reduce(m[:, :, at:at + 1], le[:, :, :], AX.X, ALU.max))
                step(dve.tensor_tensor(hots[:, :, :], le[:, :, :], bc(m[:, :, at:at + 1], 32), ALU.is_equal))
                step(dve.tensor_tensor(hots[:, :, :], hots[:, :, :],
                                       const(k, "rank8").rearrange("p (a e) -> p a e", a=1).to_broadcast([128, 4, 32]),
                                       ALU.mult))
                step(dve.tensor_reduce(m[:, :, 4:5], hots[:, :, :], AX.X, ALU.max))
                step(dve.tensor_tensor(hots[:, :, :], hots[:, :, :], bc(m[:, :, 4:5], 32), ALU.is_equal))
                if at == 0:
                    step(dve.scalar_tensor_tensor(le[:, :, :], hots[:, :, :], 2 * MASKED, le[:, :, :], ALU.mult,
                                                  ALU.add))
            dve.tensor_tensor(m[:, :, 3:4], m[:, :, 1:2], m[:, :, 0:1], ALU.subtract).then_inc(best_ready, 1)
            dve.wait_ge(exp_ready, 2)
            step(dve.tensor_scalar(m[:, :, 5:6], m[:, :, 3:4], 1.0, None, ALU.add))
            step(dve.reciprocal(m[:, :, 5:6], m[:, :, 5:6]))
            step(dve.tensor_tensor(m[:, :, 5:6], m[:, :, 5:6], m[:, :, 2:3], ALU.mult))
            step(dve.tensor_tensor(m[:, :, 6:7], m[:, :, 5:6], m[:, :, 3:4], ALU.mult))
            step(dve.tensor_tensor(gate[:, :, :], hot[:, :, :], bc(m[:, :, 5:6], 32), ALU.mult))
            step(dve.tensor_tensor(hot2[:, :, :], hot2[:, :, :], bc(m[:, :, 6:7], 32), ALU.mult))
            dve.tensor_tensor(gate[:, :, :], gate[:, :, :], hot2[:, :, :], ALU.add).then_inc(gates_ready, 1)
            dve.wait_ge(turned, 1)
            dve.tensor_copy(gate_t[0:32, :], k.bank[4][0:32, :]).then_inc(turned_copied, 1)


def experts(k, gate_dram):
    ws = k.ws
    turns, per = EXPERTS // 4, MOE_CHUNKS
    c0 = ws.blocks // 16
    assert ws.blocks % 16 == 0 and ws.n_loaded == c0 + 3 and ws.n_split == c0 + 1
    with memory(k, hh=("r", 8, SEQ), hl=("r", 8, SEQ), gates=(4, SEQ), silu=(2, SEQ), mid=(2, SEQ)) as (
            hh, hl, gates, silu, mid), \
            stage(k, "gates_in", "gate_ready", "up_ready", "silu_ready", "pair_read", "hidden_ready", "down_ready",
                  "down_added", "vector_order") as (
                block, gates_in, gate_ready, up_ready, silu_ready, pair_read, hidden_ready, down_ready, down_added,
                order):

        @block.sync
        def _(sp):
            with sp.Fori(0, turns) as i:
                row = gate_dram[i, :].partition_broadcast(128).rearrange("p (e t) -> p e t", e=4)
                sp.wait_ge(order, i * 16 + 1)
                sp.dma_start(gates[:, :, :], row).then_inc(gates_in, 16)
                for c in range(c0 + 3, c0 + 3 + per):
                    sp.wait_ge(ws.split, i * per + (c - SLOTS + 1))
                    sp.dma_start(ws.raw[:, c % SLOTS, :], ws.dram[i * per + c, :, :]).then_inc(
                        ws.loaded[c % SLOTS], 16)

        @block.gpsimd
        def _(pool):
            with pool.Fori(0, turns) as i:
                ws.turn = i * per
                ws.n_split, ws.to_split = c0 + 1, c0 + 1 + per
                ws.divide(pool)

        @block.tensor
        def _(pe):
            with pe.Fori(0, turns) as i:
                ws.turn = i * per
                ws.blocks = 16 * c0
                for u in range(8):
                    a, b = k.bank[2 * (u % 2)], k.bank[2 * (u % 2) + 1]
                    pe.wait_ge(pair_read, i * 8 + (u + 1))
                    for t in range(KT):
                        last = ws.product(pe, a[:, :], (k.xh[:, t, :], k.xl[:, t, :]), t == 0, t == KT - 1)
                    last.then_inc(gate_ready, 1)
                    for t in range(KT):
                        last = ws.product(pe, b[:, :], (k.xh[:, t, :], k.xl[:, t, :]), t == 0, t == KT - 1)
                    last.then_inc(up_ready, 1)
                for dt in range(KT):
                    pe.wait_ge(down_added, i * 8 + (dt + 1))
                    for u in range(8):
                        if dt == 0:
                            pe.wait_ge(hidden_ready, i * 8 + (u + 1))
                        last = ws.product(pe, k.bank[4 + dt % 2][:, :], (hh[:, u, :], hl[:, u, :]), u == 0, u == 7)
                    last.then_inc(down_ready, 1)

        @block.scalar
        def _(act):
            with act.Fori(0, turns) as i:
                for u in range(8):
                    act.wait_ge(gate_ready, i * 8 + (u + 1))
                    act.activation(silu[:, u % 2, :], k.bank[2 * (u % 2)][:, :], ACT.Silu).then_inc(silu_ready, 1)

        @block.vector
        def _(dve):
            for s in range(2):
                dve.memset(mid[:, s, 0:1], 0.0).then_inc(pair_read, 1)
                dve.memset(mid[:, s, 1:2], 0.0).then_inc(down_added, 1)
            dve.memset(mid[:, 0, 2:3], 0.0).then_inc(order, 1)
            dve.wait_ge(pair_read, 2)
            dve.wait_ge(down_added, 2)
            dve.wait_ge(order, 1)
            with dve.Fori(0, turns) as i:
                n = 1
                for u in range(8):
                    m = mid[:, u % 2, :]
                    dve.wait_ge(silu_ready, i * 8 + (u + 1))
                    dve.wait_ge(up_ready, i * 8 + (u + 1))
                    if u == 0:
                        dve.wait_ge(gates_in, i * 16 + 16)
                    dve.tensor_tensor(m, silu[:, u % 2, :], k.bank[2 * (u % 2) + 1][:, :], ALU.mult).then_inc(
                        pair_read, 1)
                    dve.wait_ge(pair_read, i * 8 + (u + 3))
                    dve.tensor_tensor(m, m, gates[:, u // 2, :], ALU.mult).then_inc(order, 1)
                    n += 1
                    dve.wait_ge(order, i * 16 + n)
                    dve.tensor_copy(hh[:, u, :], m).then_inc(order, 1)
                    n += 1
                    dve.wait_ge(order, i * 16 + n)
                    dve.tensor_tensor(hl[:, u, :], m, hh[:, u, :].bitcast(F32), ALU.subtract).then_inc(
                        hidden_ready, 1)
                for dt in range(KT):
                    dve.wait_ge(down_ready, i * 8 + (dt + 1))
                    dve.tensor_tensor(k.res[:, dt, :], k.res[:, dt, :], k.bank[4 + dt % 2][:, :], ALU.add).then_inc(
                        down_added, 1)
    total = turns * per
    ws.turn = 0
    ws.blocks = 16 * (c0 + total)
    ws.n_loaded, ws.n_split = c0 + total + 3, c0 + total + 1




def retention(k, pj, rv):
    par = lambda n, j=0: k.par2[:, P2[n] + j:P2[n] + j + 1]
    rotate = const(k, "rotate")
    with memory(k, decays=(4, STRIP)) as decays:
        with memory(k, tabs=(2 * SEQ + 2 * STRIP,), rot_t=(SEQ,), lgam=(3, 8)) as (tabs, tmp, lgam):
            cos, sin = tabs[:, 0:SEQ], tabs[:, SEQ:2 * SEQ]
            ahead, behind = tabs[:, 2 * SEQ:2 * SEQ + STRIP], tabs[:, 2 * SEQ + STRIP:2 * SEQ + 2 * STRIP]
            with stage(k, "tables_in", "rotated", "rotated_read", "abs_ready", "exp_ready", "log_ready", "powers_ready",
                       "strips_ready", "vector_order") as (block, tables_in, rotated, rotated_read, abs_ready, exp_ready,
                                                           log_ready, powers_ready, strips_ready, order):
                @block.sync
                def _(sp):
                    sp.dma_start(tabs[:, :], k.dram["tables"][:, 0:2 * SEQ + 2 * STRIP]).then_inc(tables_in, 16)

                @block.tensor
                def _(pe):
                    for j in range(4):
                        if j >= 2:
                            pe.wait_ge(rotated_read, j - 1)
                        pe.matmul(k.bank[j % 2][:, :], rotate, pj[:, T2["rq"] + j, :], start=True, stop=True).then_inc(
                            rotated, 1)

                @block.scalar
                def _(act):
                    act.wait_ge(abs_ready, 1)
                    act.activation(lgam[:, 1, :], lgam[:, 1, :], ACT.Exp, scale=-1.0).then_inc(exp_ready, 1)
                    act.wait_ge(exp_ready, 1)
                    act.activation(lgam[:, 1, :], lgam[:, 1, :], ACT.Ln, bias=k.eps[:, 3:4]).then_inc(log_ready, 1)
                    for h in range(4):
                        act.wait_ge(powers_ready, h + 1)
                        act.activation(decays[:, h, :], decays[:, h, :], ACT.Exp).then_inc(strips_ready, 1)

                @block.vector
                def _(dve):
                    step = Order(dve, order)
                    g = k.par2[:, P2["decay"]:P2["decay"] + 8]
                    step(dve.tensor_scalar(lgam[:, 0, :], g, -1.0, None, ALU.mult))
                    dve.tensor_tensor(lgam[:, 1, :], lgam[:, 0, :], g, ALU.max).then_inc(abs_ready, 1)
                    step(dve.tensor_scalar(lgam[:, 2, :], g, 0.0, None, ALU.min))
                    dve.wait_ge(log_ready, 1)
                    step(dve.tensor_tensor(lgam[:, 2, :], lgam[:, 2, :], lgam[:, 1, :], ALU.subtract))
                    dve.wait_ge(tables_in, 16)
                    for h in range(4):
                        d = decays[:, h, :]
                        step(dve.tensor_scalar(d, behind, lgam[:, 2, 4 + h:5 + h], None, ALU.mult))
                        dve.scalar_tensor_tensor(d, ahead, lgam[:, 2, h:h + 1], d, ALU.mult, ALU.add).then_inc(
                            powers_ready, 1)
                    for j in range(4):
                        z = pj[:, T2["rq"] + j, :]
                        dve.wait_ge(rotated, j + 1)
                        dve.tensor_tensor(tmp[:, :], k.bank[j % 2][:, :], sin, ALU.mult).then_inc(rotated_read, 1)
                        dve.wait_ge(rotated_read, j + 1)
                        step(dve.tensor_tensor(z, z, cos, ALU.mult))
                        step(dve.tensor_tensor(z, z, tmp[:, :], ALU.add))
        with memory(k, wsc=(2, 4, SEQ)) as wsc:
            with stage(k, "scores_ready", "scores_used", "out_ready", "out_copied") as (
                    block, scores_ready, scores_used, out_ready, out_copied):
                @block.tensor
                def _(pe):
                    for h in range(5):
                        if h < 4:
                            rows = slice(64 * (h % 2), 64 * (h % 2) + 64)
                            for j in range(4):
                                u = 4 * h + j
                                if u >= 4:
                                    pe.wait_ge(scores_used, u - 3)
                                pe.matmul(k.bank[u % 4][:, :], pj[rows, T2["rk"] + h // 2, 128 * j:128 * j + 128],
                                          pj[rows, T2["rq"] + h // 2, :], start=True, stop=True).then_inc(
                                    scores_ready, 1)
                        if h >= 1:
                            g = h - 1
                            rows = slice(64 * (g % 2), 64 * (g % 2) + 64)
                            pe.wait_ge(scores_used, 4 * g + 4)
                            for j in range(4):
                                last = pe.matmul(k.bank[4 + g // 2][rows, :], rv[:, j, 64 * g:64 * g + 64],
                                                 wsc[:, g % 2, j, :], start=j == 0, stop=j == 3)
                            last.then_inc(out_ready, 1)

                @block.vector
                def _(dve):
                    for u in range(16):
                        h, j = divmod(u, 4)
                        if j == 0 and h >= 2:
                            dve.wait_ge(out_ready, h - 1)
                        dve.wait_ge(scores_ready, u + 1)
                        dve.scalar_tensor_tensor(wsc[:, h % 2, j, :], k.bank[u % 4][:, :], 0.125,
                                                 decays[:, h, 384 - 128 * j:384 - 128 * j + SEQ], ALU.mult,
                                                 ALU.mult).then_inc(scores_used, 1)
                    for p in range(2):
                        dve.wait_ge(out_ready, 2 * p + 2)
                        dve.tensor_copy(k.yb[:, p, :], k.bank[4 + p][:, :]).then_inc(out_copied, 1)
    with stage(k, "silu_done") as (block, silu_done):
        @block.scalar
        def _(act):
            for p in range(2):
                g = pj[:, T2["rg"] + p, :]
                act.activation(g, g, ACT.Silu).then_inc(silu_done, 1)

    def finish(p):
        y = k.yb[:, p, :]

        def run(dve, step, rstd):
            step(dve.tensor_tensor(y, y, rstd, ALU.mult))
            return dve.scalar_tensor_tensor(y, y, par("ret", p), pj[:, T2["rg"] + p, :], ALU.mult, ALU.mult)
        return run

    head_norm(k, [dict(src=k.yb[:, p, :], scale=1.0 / 64, eps=k.eps[:, 1:2], finish=finish(p)) for p in range(2)])


def pooling(k, pj, loads):
    n = SEQ + 16
    with memory(k, padded=(2, n), sums=(2, n), share=(2, SEQ)) as (padded, sums, share):
        with stage(k, "counts_in", "loads_in", "vector_order") as (block, counts_in, loads_in, order):
            @block.sync
            def _(sp):
                at = 2 * SEQ + 2 * STRIP
                sp.dma_start(share[:, :, :], k.dram["tables"][:, at:at + 2 * SEQ].rearrange(
                    "p (a t) -> p a t", a=2)).then_inc(counts_in, 16)
                for dst, src in loads:
                    sp.dma_start(dst, src).then_inc(loads_in, 16)
                sp.wait_ge(loads_in, 16 * len(loads))

            @block.vector
            def _(dve):
                step = Order(dve, order)
                step(dve.memset(padded[:, :, :], 0.0))
                step(dve.memset(sums[:, :, :], 1.0))
                for p in range(2):
                    step(dve.tensor_copy(padded[:, p, 9:9 + SEQ], pj[:, T2["pv"] + p, :]))
                for p in range(2):
                    step(dve.tensor_tensor_scan(padded[:, p, :], sums[:, p, :], padded[:, p, :], 0.0, ALU.mult,
                                                ALU.add))
                for g in range(4):
                    h = POOL_WINDOWS[g] // 2
                    r, p = slice(64 * (g % 2), 64 * (g % 2) + 64), g // 2
                    step(dve.tensor_tensor(sums[r, p, 0:SEQ], padded[r, p, 8 + h:8 + h + SEQ],
                                           padded[r, p, 8 - h:8 - h + SEQ], ALU.subtract))
                dve.wait_ge(counts_in, 16)
                for p in range(2):
                    step(dve.tensor_tensor(sums[:, p, 0:SEQ], sums[:, p, 0:SEQ], share[:, p, :], ALU.mult))
                    step(dve.tensor_tensor(sums[:, p, 0:SEQ], sums[:, p, 0:SEQ], pj[:, T2["pv"] + p, :],
                                           ALU.subtract))
        small_products(k, [(k.yb[:, 2 + p, :], k.mats2[:, 128 * p:128 * p + 128], sums[:, p, 0:SEQ],
                            k.par2[:, P2["pool"] + p:P2["pool"] + p + 1]) for p in range(2)])


def grid_bias(k, layer, bias_dram, tab, made):
    names = ("rows_in", "bias_ready", "bias_copied", "bias_stored")

    def loads(sp, rows_in, *_):
        sp.dma_start(made[64:96, :], k.dram["na_rows"]).then_inc(rows_in, 16)
        sp.dma_start(tab[64:96, :], k.dram["na_rpb"][layer, :, :]).then_inc(rows_in, 16)

    def scalar(act, rows_in, bias_ready, bias_copied, bias_stored):
        act.wait_ge(bias_copied, 8)
        act.dma_start(bias_dram, made[0:60, :]).then_inc(bias_stored, 16)
        act.wait_ge(bias_stored, 16)

    def tensor(pe, rows_in, bias_ready, bias_copied, bias_stored):
        pe.wait_ge(rows_in, 32)
        for j in range(8):
            if j >= 2:
                pe.wait_ge(bias_copied, j - 1)
            pe.matmul(k.bank[2 + j % 2][0:60, :], tab[64:96, :], made[64:96, 512 * j:512 * j + 512], start=True,
                      stop=True).then_inc(bias_ready, 1)

    def vector(dve, rows_in, bias_ready, bias_copied, bias_stored):
        for j in range(8):
            dve.wait_ge(bias_ready, j + 1)
            dve.tensor_copy(made[0:60, 512 * j:512 * j + 512], k.bank[2 + j % 2][0:60, :]).then_inc(bias_copied, 1)
    return names, dict(loads=loads, scalar=scalar, tensor=tensor, vector=vector)


def grid_bias_loads(bias, bias_dram):
    out = []
    for half in range(2):
        for h in range(4):
            src = bass.AP(tensor=bias_dram.tensor, offset=15 * 4096 * h, ap=[[64, 64], [4096, 15], [1, 64]])
            out.append((bias[64 * half:64 * half + 64, h, half:half + 15, :], src))
    return out


def layer(k, i, bias_dram):
    par = lambda n, j=0: k.par2[:, P2[n] + j:P2[n] + j + 1]
    eps = k.eps[:, 1:2]
    normalise(k, k.res, lambda t: par("mix", t), None, eps, False, k.xh, k.xl,
              loads=[(k.par2[:, :], k.dram["params2"][i, :, :]), (k.mats2[:, :], k.dram["mats2"][i, :, :])])
    with memory(k, yb=(KT, SEQ)) as k.yb:
        with memory(k, pj2=(T2_TILES, SEQ), rv=(4, 256), nv=(4, 256), mk=(2, 256), mv=(2, 256)) as (
                pj, rv, nv, mk, mv):
            with memory(k, tab=(60,), made=(4096,)) as (tab, made):
                project(k, T2_TILES, pj, [(rv, 256), (nv, 256)], aside=grid_bias(k, i, bias_dram, tab, made))
            with memory(k, memt=(KT, 256), memh=("r", KT, 256), meml=("r", KT, 256)) as (memt, memh, meml):
                with stage(k, "mem_in") as (block, mem_in):
                    @block.sync
                    def _(sp):
                        sp.dma_start(memt[:, :, :], k.dram["memT"]).then_inc(mem_in, 16)
                        sp.wait_ge(mem_in, 16)
                normalise(k, memt, lambda t: par("mem", t), None, eps, False, memh, meml, n=256)
                project(k, 2, mk, [(mv, 256)], (memh, meml), 256)
            jobs = []
            for name, gain in (("nq", "naq"), ("nk", "nak"), ("mq", "memq")):
                for p in range(2):
                    src = pj[:, T2[name] + p, :]
                    jobs.append(dict(src=src, scale=1.0 / 64, eps=eps, finish=gained(src, par(gain))))
            head_norm(k, jobs)
            head_norm(k, [dict(src=mk[:, p, :], scale=1.0 / 64, eps=eps, finish=gained(mk[:, p, :], par("memk")))
                          for p in range(2)], n=256)
            retention(k, pj, rv)
            with memory(k, na_bias=(4, 16, 64)) as bias:
                pooling(k, pj, grid_bias_loads(bias, bias_dram))
                units = []
                for h in range(4):
                    rows = slice(64 * (h % 2), 64 * (h % 2) + 64)
                    for q in range(4):
                        cols = slice(128 * q, 128 * q + 128)
                        b = bias[:, h, 7 - 2 * q:15 - 2 * q, :].rearrange("p r c -> p (r c)")
                        units.append(dict(q=pj[rows, T2["nq"] + h // 2, cols], keys=pj[rows, T2["nk"] + h // 2, :],
                                          n=SEQ, scale=0.125, bias=b, select=None, strip=None, rows=rows, cols=cols,
                                          values=[nv[:, j, 64 * h:64 * h + 64] for j in range(4)], pair=h // 2))
                for h in range(4):
                    rows = slice(64 * (h % 2), 64 * (h % 2) + 64)
                    for q in range(4):
                        cols = slice(128 * q, 128 * q + 128)
                        units.append(dict(q=pj[rows, T2["mq"] + h // 2, cols], keys=mk[rows, h // 2, :], n=256,
                                          scale=0.125, bias=None, select=None, strip=None, rows=rows, cols=cols,
                                          values=[mv[:, j, 64 * h:64 * h + 64] for j in range(2)], pair=2 + h // 2))
                attention(k, units, [k.yb[:, 4 + p, :] for p in range(4)])
        merge(k, 1.0)
    normalise(k, k.res, lambda t: par("ffn", t), None, eps, False, k.xh, k.xl)
    feed_forward(k)


def feed_forward(k):
    ws = k.ws
    nf = FF // 128
    with memory(k, fh=("r", nf, SEQ), fl=("r", nf, SEQ), silu=(2, SEQ), mid=(1, SEQ)) as (fh, fl, silu, mid):
        ws.plan(nf * 16)
        with stage(k, "act_ready", "lin_ready", "silu_ready", "pair_read", "vector_order") as (
                block, act_ready, lin_ready, silu_ready, pair_read, order):
            @block.sync
            def _(sp):
                ws.load(sp)

            @block.gpsimd
            def _(pool):
                ws.divide(pool)

            @block.tensor
            def _(pe):
                for j in range(nf):
                    if j >= 2:
                        pe.wait_ge(pair_read, j - 1)
                    for m, done in ((0, act_ready), (1, lin_ready)):
                        for t in range(KT):
                            last = ws.product(pe, k.bank[2 * (j % 2) + m][:, :], (k.xh[:, t, :], k.xl[:, t, :]),
                                              t == 0, t == KT - 1)
                        last.then_inc(done, 1)

            @block.scalar
            def _(act):
                for j in range(nf):
                    act.wait_ge(act_ready, j + 1)
                    act.activation(silu[:, j % 2, :], k.bank[2 * (j % 2)][:, :], ACT.Silu).then_inc(silu_ready, 1)

            @block.vector
            def _(dve):
                step = Order(dve, order)
                for j in range(nf):
                    dve.wait_ge(silu_ready, j + 1)
                    dve.wait_ge(lin_ready, j + 1)
                    dve.tensor_tensor(mid[:, 0, :], silu[:, j % 2, :], k.bank[2 * (j % 2) + 1][:, :],
                                      ALU.mult).then_inc(pair_read, 1)
                    dve.wait_ge(pair_read, j + 1)
                    step(dve.tensor_copy(fh[:, j, :], mid[:, 0, :]))
                    step(dve.tensor_tensor(fl[:, j, :], mid[:, 0, :], fh[:, j, :].bitcast(F32), ALU.subtract))
        add_product(k, nf, fh, fl, 1.0)




def scale_residual(k):
    with stage(k, "scaled") as (block, scaled):
        @block.vector
        def _(dve):
            for t in range(KT):
                dve.tensor_scalar(k.res[:, t, :], k.res[:, t, :], ALPHA, None, ALU.mult).then_inc(scaled, 1)


def store_out(k, c0):
    ws = k.ws
    end = c0 + LAYERS * LAYER_CHUNKS
    with stage(k, "stored") as (block, stored):
        @block.sync
        def _(sp):
            sp.dma_start(k.dram["outT"], k.res[:, :, :]).then_inc(stored, 16)
            sp.wait_ge(stored, 16)
            for c in (end + 1, end + 2):
                sp.wait_ge(ws.loaded[c % SLOTS], 16 * (c // SLOTS + 1))


def build(nc, dram):
    with ExitStack() as ctx:
        k = Kernel(nc, dram)
        k.bank = [ctx.enter_context(nc.psum_tensor(f"bank{b}", [128, 512], F32)) for b in range(8)]
        k.ws = Stream(nc, ctx, dram["weights"])
        k.xh, k.xl, k.res, k.consts, k.par1, k.par2, k.mats1, k.mats2, k.eps = ctx.enter_context(memory(
            k, xh=("r", KT, SEQ), xl=("r", KT, SEQ), res=(KT, SEQ), consts=(CONSTS,), par1=(P1_COLS,),
            par2=(P2_COLS,), mats1=(548,), mats2=(256,), eps=(4,)))
        bias_dram = nc.dram_tensor("distance_bias", (8, 128, 1024), F32, kind="Internal").ap()
        gate_dram = nc.dram_tensor("expert_gates", (8, 4 * SEQ), F32, kind="Internal").ap()
        grid_dram = nc.dram_tensor("grid_bias", (60, 4096), F32, kind="Internal").ap()
        with memory(k, yb=(KT, SEQ)) as k.yb:
            with memory(k, pj=(T1_TILES, SEQ), av=(4, 256), cv=(4, 256)) as (pj, av, cv):
                with memory(k, rows=(1024,), tab=(8,), bias_rows=(1024,)) as (rows, tab, bias_rows):
                    project(k, T1_TILES, pj, [(av, 256), (cv, 256)], first=split_start(k),
                            aside=distance_bias(k, bias_dram, rows, tab, bias_rows))
                mixers_ab(k, pj, av, bias_dram)
                mixer_c(k, pj, cv)
                mixer_d(k, pj, av, cv)
            merge(k, ALPHA, k.dram["xT"])
        par = lambda n, j: k.par1[:, P1[n] + j:P1[n] + j + 1]
        normalise(k, k.res, lambda t: par("ln_g", t), lambda t: par("ln_b", t), k.eps[:, 0:1], True, k.xh, k.xl,
                  out=k.res)
        route(k, gate_dram.rearrange("g (e t) -> (g e) t", e=4))
        scale_residual(k)
        experts(k, gate_dram)
        normalise(k, k.res, lambda t: par("ln_g", 8 + t), lambda t: par("ln_b", 8 + t), k.eps[:, 0:1], True,
                  out=k.res)
        c0 = k.ws.blocks // 16
        with nc.Fori(0, LAYERS) as i:
            k.ws.turn = i * LAYER_CHUNKS
            layer(k, i, grid_dram)
            assert k.ws.blocks == 16 * (c0 + LAYER_CHUNKS)
        store_out(k, c0)




def fm_blocks(w):
    k, f = w.shape
    return w.reshape(k // 128, 128, f // 128, 128).transpose(2, 0, 1, 3).reshape(-1, 128, 128)


def tm_blocks(w):
    k, f = w.shape
    return w.reshape(k // 128, 128, f // 128, 128).transpose(0, 2, 1, 3).reshape(-1, 128, 128)


def merge_blocks(gate, branch):
    g = gate.reshape(8, 128, 4, 8, 128).transpose(3, 2, 0, 1, 4)
    b = branch.reshape(4, 2, 128, 8, 128).transpose(3, 0, 1, 2, 4)
    return np.concatenate([g, b], axis=2).reshape(-1, 128, 128)


def pair_blocks(a, b):
    x = fm_blocks(a).reshape(-1, 8, 128, 128)
    y = fm_blocks(b).reshape(-1, 8, 128, 128)
    return np.stack([x, y], axis=1).reshape(-1, 128, 128)


def weight_stream(v):
    w = v["w_in"][0]
    off = dict(aq=0, ak=256, av=512, bq=768, ckv=1024, iq=1088, ik=1344, iw=1376, cq=1384, ck=1512, cv=1640,
               ca=1896, cg=1912, dr=2168, dk=2424, dv=2680, dw=2936, da=2952, dg=2968, gate=3000)

    def cols(name, n):
        return w[:, off[name]:off[name] + n]

    low = np.zeros((D, 128), np.float32)
    low[:, 0:16] = cols("dw", 16)
    low[:, 32:48] = cols("da", 16)
    low[:, 64:96] = cols("dg", 32)
    low[:, 96:112] = cols("ca", 16)
    low[:, 112:120] = cols("iw", 8)
    router = np.zeros((D, 128), np.float32)
    router[:, 0:4] = v["router_g"][0]
    router[:, 4:36] = v["router_e"][0]
    fm = np.concatenate([cols("aq", 256), cols("ak", 256), cols("bq", 256), cols("iq", 256), cols("ckv", 64),
                         cols("ckv", 64)] + [cols("ik", 32)] * 4 + [low, cols("cq", 128), cols("ck", 128),
                         cols("cg", 256), cols("dr", 256), cols("dk", 256), cols("dv", 256)], axis=1)
    parts = [fm_blocks(fm), tm_blocks(cols("av", 256)), tm_blocks(cols("cv", 256)),
             merge_blocks(cols("gate", 4 * D), v["w_branch"][0]), fm_blocks(v["w_out"][0]), tm_blocks(router)]
    for g in range(8):
        for e in range(4 * g, 4 * g + 4):
            parts.append(pair_blocks(v["moe_w_gate"][0, e], v["moe_w_up"][0, e]))
        down = v["moe_w_down"][0, 4 * g:4 * g + 4].reshape(4, 2, 128, 8, 128).transpose(3, 0, 1, 2, 4)
        parts.append(down.reshape(-1, 128, 128))
    for l in range(LAYERS):
        w2 = v["w_in_2"][l]
        sec = [w2[:, 256 * n:256 * n + 256] for n in range(9)]
        rq, rk, rv, rg, pv, nq, nk, nv, mq = sec
        parts += [fm_blocks(np.concatenate([rq, rk, rg, pv, nq, nk, mq], axis=1)), tm_blocks(rv), tm_blocks(nv),
                  fm_blocks(v["w_mem_kv_2"][l][:, 0:256]), tm_blocks(v["w_mem_kv_2"][l][:, 256:512]),
                  merge_blocks(v["w_gate_2"][l], v["w_branch_2"][l]), fm_blocks(v["w_out_2"][l]),
                  pair_blocks(v["w_ffn_in_2"][l][:, 0:FF], v["w_ffn_in_2"][l][:, FF:2 * FF]),
                  fm_blocks(v["w_ffn_out_2"][l])]
    parts.append(np.zeros((16 * SPARE, 128, 128), np.float32))
    s = np.concatenate(parts, axis=0)
    assert s.shape[0] == 16 * (CHUNKS + SPARE)
    return np.ascontiguousarray(s.reshape(-1, 16, 128, 128).transpose(0, 2, 1, 3).reshape(-1, 128, CHUNK))


def t5_bucket(dist):
    exact = 16
    d = np.maximum(dist, 0)
    df = np.maximum(d, 1).astype(np.float32)
    large = exact + (np.log(df / np.float32(exact)) / np.float32(math.log(2048 / exact)) * np.float32(16)).astype(np.int32)
    return np.where(d < exact, d, np.minimum(large, 31))


def distance_rows():
    dist = 511 - np.arange(1024)
    r = np.zeros((34, 1024), np.float32)
    b = t5_bucket(dist)
    for y in range(1024):
        if dist[y] >= 0:
            r[b[y], y] = 1.0
    held = (dist <= 128).astype(int) + (dist % 4 == 0) + (dist % 16 == 0)
    held = np.where(dist >= 0, held, 0)
    r[32] = np.where(held > 0, np.log(np.maximum(held, 1)), MASKED)
    r[33] = np.where(dist >= 0, 0.0, MASKED)
    return r


def constants():
    c = np.zeros((128, CONSTS), np.float32)
    i, j = np.meshgrid(np.arange(128), np.arange(128), indexing="ij")

    def put(name, m):
        c[:, CONST[name]:CONST[name] + m.shape[1]] = m

    put("ident", (i == j))
    put("ones", np.ones((128, 128)))
    put("blk64", (i // 64 == j // 64))
    put("gla_mask", (i <= j) & (i // 64 == j // 64))
    put("up_same", (i < j) & (i // 16 == j // 16))
    put("up_other", (i < j) & (i // 16 != j // 16))
    put("low_same", (i > j) & (i // 16 == j // 16))
    put("up", (i < j))
    put("up_diag", (i <= j))
    put("future", np.where(j > i, MASKED, 0.0))
    a, b = np.meshgrid(np.arange(128), np.arange(256), indexing="ij")
    put("gla_heads", (a // 32 == b // 64))
    t = np.arange(512)[None, :] + np.zeros((128, 1))
    put("reset64", (t % 64 != 0))
    put("reset128", (t % 128 != 0))
    rot = np.where(j % 64 < 32, -1.0 * (i == j + 32), 1.0 * (i == j - 32))
    put("rotate", rot)
    put("rank8", np.tile(8.0 - np.arange(8), (128, 4)))
    return c


def layer_tables():
    half = 32
    inv = (np.float32(10000.0) ** (-np.arange(half, dtype=np.float32) / np.float32(half))).astype(np.float32)
    ang = (np.arange(SEQ, dtype=np.float32)[None, :] * inv[:, None]).astype(np.float32).astype(np.float64)
    cos, sin = (np.tile(f(ang), (4, 1)).astype(np.float32) for f in (np.cos, np.sin))
    p, x = np.meshgrid(np.arange(128), np.arange(STRIP), indexing="ij")
    ahead = np.maximum(x - 384 - p, 0).astype(np.float32)
    behind = np.maximum(384 + p - x, 0).astype(np.float32)
    t = np.arange(SEQ)
    counts = np.zeros((128, 2, SEQ), np.float32)
    for g in range(4):
        h = POOL_WINDOWS[g] // 2
        n = np.clip(t + h, 0, SEQ) - np.clip(t - h, 0, SEQ)
        counts[64 * (g % 2):64 * (g % 2) + 64, g // 2, :] = (1.0 / n)[None, :]
    return np.concatenate([cos, sin, ahead, behind, counts.reshape(128, -1)], axis=1)


def na_select():
    r = np.zeros((32, 64, 64), np.float32)
    for qc in range(64):
        lo = min(max(qc - 8, 0), 48)
        for kc in range(64):
            if lo <= kc < lo + 16:
                r[kc - qc + 15, qc, kc] = 1.0
            else:
                r[31, qc, kc] = MASKED
    return r.reshape(32, 4096)


def columns(*arrays):
    return np.concatenate([a.reshape(-1, 128).T for a in arrays], axis=1)


def device_arrays(v):
    f32 = np.float32
    a = {}
    a["xT"] = np.ascontiguousarray(v["x"][0].T.reshape(8, 128, SEQ).transpose(1, 0, 2))
    a["memT"] = np.ascontiguousarray(v["mem_2"][0].T.reshape(8, 128, 256).transpose(1, 0, 2))
    a["weights"] = weight_stream(v)
    a["consts"] = constants()
    a["tables"] = layer_tables()
    a["dist_rows"] = distance_rows()
    a["na_rows"] = na_select()
    tab = np.zeros((34, 8), f32)
    tab[0:32] = v["rpb_table"]
    tab[32, 0:4] = 1.0
    tab[33, 4:8] = 1.0
    a["rpb"] = tab
    mu = v["d_mu"][0]
    mu_low = np.zeros(128, f32)
    mu_low[0:16], mu_low[32:48], mu_low[64:96] = mu[768:784], mu[784:800], mu[800:832]
    dup = lambda z, n: np.tile(z, n)
    a["params1"] = np.ascontiguousarray(columns(
        v["ln_g"][0], v["ln_b"][0], dup(v["b_kv_gain"][0], 2), v["c_a_bias"][0], v["c_norm_gain"][0],
        mu[0:768], mu_low, v["d_w0"][0], v["d_a0"][0], v["d_k_k"][0], v["d_k_a"][0], v["d_r_k"][0],
        v["d_gn_w"][0], v["d_gn_b"][0]))
    low = np.zeros((128, 256), f32)
    low[0:16], low[32:48], low[64:96] = v["d_w2"][0], v["d_a2"][0], v["d_g2"][0]
    low[96:112, 0:128] = v["c_a_up"][0]
    uv = np.zeros((128, 256), f32)
    for h in range(4):
        r = 64 * (h % 2)
        uv[r:r + 64, 128 * (h // 2) + r:128 * (h // 2) + r + 64] = v["b_w_uv"][0, h]
    bias = np.concatenate([v["router_g_bias"][0], v["router_e_bias"][0]])
    a["mats1"] = np.concatenate([low, uv, np.tile(bias[None, :], (128, 1))], axis=1)
    p2, m2, rp = [], [], []
    for l in range(LAYERS):
        reps = np.concatenate([v["ret_decay_fwd_2"][l], v["ret_decay_bwd_2"][l]])
        p2.append(np.concatenate([columns(
            v["norm_mix_g_2"][l], v["norm_mem_g_2"][l], v["norm_ffn_g_2"][l], v["ret_norm_g_2"][l],
            v["pool_scale_2"][l], dup(v["na_q_norm_g_2"][l], 2), dup(v["na_k_norm_g_2"][l], 2),
            dup(v["mem_q_norm_g_2"][l], 2), dup(v["mem_k_norm_g_2"][l], 2)),
            np.tile(reps[None, :], (128, 1))], axis=1))
        pw = np.zeros((128, 256), f32)
        for g in range(4):
            r = 64 * (g % 2)
            pw[r:r + 64, 128 * (g // 2) + r:128 * (g // 2) + r + 64] = v["pool_w_2"][l, g]
        m2.append(pw)
        r = np.ones((32, 60), f32)
        r[0:31] = v["na_rpb_2"][l].reshape(60, 31).T
        rp.append(r)
    a["params2"] = np.stack(p2)
    a["mats2"] = np.stack(m2)
    a["na_rpb"] = np.stack(rp)
    return {k: np.ascontiguousarray(x) for k, x in a.items()}


def kernel(**inputs):
    import concourse.bacc as bacc
    from concourse.bass_utils import run_bass_kernel_spmd

    arrays = device_arrays({k: np.asarray(x) for k, x in inputs.items()})
    nc = bacc.Bacc("TRN2", target_bir_lowering=False, num_devices=1)
    dram = {k: nc.dram_tensor(k, x.shape, F32, kind="ExternalInput").ap() for k, x in arrays.items()}
    dram["outT"] = nc.dram_tensor("outT", (128, 8, SEQ), F32, kind="ExternalOutput").ap()
    build(nc, dram)
    r = run_bass_kernel_spmd(nc, [arrays], core_ids=[0])
    out = np.asarray(r.results[0]["outT"])
    return np.ascontiguousarray(out.transpose(2, 1, 0).reshape(1, SEQ, D))
```

```python
import math
from contextlib import ExitStack, contextmanager

import numpy as np

import concourse.bass as bass
from concourse import mybir

F32 = mybir.dt.float32
F32R = mybir.dt.float32r
ALU = mybir.AluOpType
ACT = mybir.ActivationFunctionType
AX = mybir.AxisListType

SEQ, D, FF, LAYERS, EXPERTS = 512, 1024, 2816, 2, 32
KT = D // 128
CHUNK = 2048
SLOTS = 2
ALPHA = 2.0 ** 0.25
MASKED = -1e30
TAKEN = -3e38
STRIP = 896
POOL_WINDOWS = (2, 4, 8, 16)
FIRST_CHUNKS = 37
MOE_CHUNKS = 3
LAYER_CHUNKS = 68
CHUNKS = FIRST_CHUNKS + EXPERTS * MOE_CHUNKS + LAYERS * LAYER_CHUNKS
ROWS = 128
BLOCKS = (2 * SEQ + EXPERTS * (ROWS - 1)) // ROWS
TURNS = -(-BLOCKS // 2)
SPARE = 4

_widths = dict(ident=128, ones=128, blk64=128, gla_mask=128, up_same=128, up_other=128, low_same=128, up=128,
               up_diag=128, future=128, gla_heads=256, reset64=512, reset128=512, rotate=128, rank8=32, count=256, row=2)
CONST = {}
CONSTS = 0
for _n, _w in _widths.items():
    CONST[_n] = CONSTS
    CONSTS += _w

P1 = dict(ln_g=0, ln_b=16, kv_gain=32, a_bias=33, c_norm=34, mu=36, w0=43, a0=45, k_k=47, k_a=49, r_k=51, gn_w=53,
          gn_b=55)
P1_COLS = 57
P2 = dict(mix=0, mem=8, ffn=16, ret=24, pool=26, naq=28, nak=29, memq=30, memk=31, decay=32)
P2_COLS = 40
T1 = dict(aq=0, ak=2, bq=4, iq=6, ckv=8, ik=9, low=10, cq=11, ck=12, cg=13, dr=15, dk=17, dv=19)
T1_TILES = 21
T2 = dict(rq=0, rk=2, rg=4, pv=6, nq=8, nk=10, mq=12)
T2_TILES = 14


class Kernel:

    def __init__(self, nc, dram):
        self.nc, self.dram, self.tensors = nc, dram, 0


class Order:

    def __init__(self, engine, sem):
        self.engine, self.sem, self.n = engine, sem, 0

    def __call__(self, instruction):
        instruction.then_inc(self.sem, 1)
        self.n += 1
        self.engine.wait_ge(self.sem, self.n)


class Stream:

    def __init__(self, nc, ctx, dram):
        self.dram = dram
        self.raw = ctx.enter_context(nc.sbuf_tensor("w_raw", [128, SLOTS, CHUNK], F32))
        self.hi = ctx.enter_context(nc.sbuf_tensor("w_hi", [128, SLOTS, CHUNK], F32R))
        self.lo = ctx.enter_context(nc.sbuf_tensor("w_lo", [128, SLOTS, CHUNK], F32R))
        self.zero = ctx.enter_context(nc.sbuf_tensor("w_zero", [128, 1], F32))
        self.loaded = [ctx.enter_context(nc.semaphore(f"w_loaded{s}")) for s in range(SLOTS)]
        self.rounded = ctx.enter_context(nc.semaphore("w_rounded"))
        self.split = ctx.enter_context(nc.semaphore("w_split"))
        self.used = ctx.enter_context(nc.semaphore("w_used"))
        self.blocks = 0
        self.n_loaded = 0
        self.n_split = 0
        self.turn = 0
        self.skipped = 0
        self.limit = None
        self.want = 0

    def plan(self, n_blocks):
        self.want = self.blocks + n_blocks
        started = -(-self.want // 16)
        self.to_split = started + 1
        self.to_load = started + 3
        if self.limit is not None:
            self.to_split, self.to_load = min(self.to_split, self.limit), min(self.to_load, self.limit)

    def load(self, sp, upto=None):
        for c in range(self.n_loaded, self.to_load if upto is None else upto):
            if c >= SLOTS:
                sp.wait_ge(self.split, self.turn + (c - SLOTS + 1))
            sp.dma_start(self.raw[:, c % SLOTS, :], self.dram[self.turn + (self.skipped + c), :, :]).then_inc(
                self.loaded[c % SLOTS], 16)
        self.n_loaded = max(self.n_loaded, self.to_load)

    def divide(self, pool):
        for c in range(self.n_split, self.to_split):
            s = c % SLOTS
            pool.wait_ge(self.loaded[s], self.turn * (16 // SLOTS) + 16 * (c // SLOTS + 1))
            if c >= SLOTS:
                pool.wait_ge(self.used, self.turn + (c - SLOTS + 1))
            pool.tensor_tensor(self.hi[:, s, :], self.raw[:, s, :], self.zero[:, 0:1].to_broadcast([128, CHUNK]),
                               ALU.add).then_inc(self.rounded, 1)
            pool.wait_ge(self.rounded, self.turn + (c + 1))
            pool.tensor_tensor(self.lo[:, s, :], self.raw[:, s, :], self.hi[:, s, :].bitcast(F32),
                               ALU.subtract).then_inc(self.split, 1)
        self.n_split = self.to_split

    def take(self, pe, n=1):
        c, b = divmod(self.blocks, 16)
        assert b + n <= 16
        if b == 0:
            pe.wait_ge(self.split, self.turn + (c + 1))
            self.release = c > 0
        self.blocks += n
        cols = slice(128 * b, 128 * (b + n))
        return self.hi[:, c % SLOTS, cols], self.lo[:, c % SLOTS, cols]

    def released(self, matmul):
        if self.release:
            matmul.then_inc(self.used, 1)
            self.release = False

    def product(self, pe, out, moving, start, stop):
        hi, lo = self.take(pe)
        self.released(pe.matmul(out, hi, moving[0], start=start, stop=False))
        pe.matmul(out, hi, moving[1], start=False, stop=False)
        return pe.matmul(out, lo, moving[0], start=False, stop=stop)

    def product_tm(self, pe, outs, still, n, start, stop):
        hi, lo = self.take(pe, n)
        for out, (sh, sl) in zip(outs, still):
            self.released(pe.matmul(out, sh, hi, start=start, stop=False))
            pe.matmul(out, sh, lo, start=False, stop=False)
            last = pe.matmul(out, sl, hi, start=False, stop=stop)
        return last


@contextmanager
def stage(k, *names):
    nc = k.nc
    with ExitStack() as ctx:
        sems = [ctx.enter_context(nc.semaphore(n)) for n in names]
        with nc.Block(no_gpsimd_drain=True) as block:
            yield (block, *sems)
        for s in sems:
            nc.sync.sem_clear(s)
        nc.all_engine_barrier()


@contextmanager
def memory(k, **shapes):
    with ExitStack() as ctx:
        out = []
        for name, shape in shapes.items():
            dt = F32
            if shape[0] in ("r", "i"):
                dt, shape = (F32R if shape[0] == "r" else mybir.dt.int32), shape[1:]
            k.tensors += 1
            out.append(ctx.enter_context(k.nc.sbuf_tensor(f"{name}_{k.tensors}", [128, *shape], dt)))
        yield out[0] if len(out) == 1 else out


def const(k, name, rows=slice(0, 128)):
    return k.consts[rows, CONST[name]:CONST[name] + _widths[name]]




def split_start(k):
    names = ("zeroed", "consts_in", "x_in", "rounded_x", "split_x")

    def scalar(act, zeroed, consts_in, x_in, rounded_x, split_x):
        for t in range(KT):
            act.dma_start(k.res[:, t, :], k.dram["xT"][:, t, :]).then_inc(x_in, 16)
        act.dma_start(k.consts[:, :], k.dram["consts"]).then_inc(consts_in, 16)
        act.dma_start(k.par1[:, :], k.dram["params1"]).then_inc(consts_in, 16)
        act.dma_start(k.mats1[:, :], k.dram["mats1"]).then_inc(consts_in, 16)
        act.wait_ge(consts_in, 48)

    def gpsimd(pool, zeroed, *_):
        pool.wait_ge(zeroed, 1)

    def tensor(pe, t, zeroed, consts_in, x_in, rounded_x, split_x):
        pe.wait_ge(split_x, t + 1)

    def vector(dve, zeroed, consts_in, x_in, rounded_x, split_x):
        dve.memset(k.ws.zero[:, :], 0.0).then_inc(zeroed, 1)
        dve.memset(k.eps[:, 0:1], 1e-5).then_inc(zeroed, 1)
        dve.memset(k.eps[:, 1:2], 1e-6).then_inc(zeroed, 1)
        dve.memset(k.eps[:, 2:3], 64e-5).then_inc(zeroed, 1)
        dve.memset(k.eps[:, 3:4], 1.0).then_inc(zeroed, 1)
        for t in range(KT):
            if t == 0:
                dve.wait_ge(x_in, 16 * KT)
            dve.tensor_copy(k.xh[:, t, :], k.res[:, t, :]).then_inc(rounded_x, 1)
            dve.wait_ge(rounded_x, t + 1)
            dve.tensor_tensor(k.xl[:, t, :], k.res[:, t, :], k.xh[:, t, :].bitcast(F32), ALU.subtract).then_inc(
                split_x, 1)
    return names, dict(scalar=scalar, gpsimd=gpsimd, tensor=tensor, vector=vector)


def project(k, tiles, out, token_major, moving=None, n_moving=SEQ, first=None, aside=None):
    ws = k.ws
    moving = moving or (k.xh, k.xl)
    nt = n_moving // 128
    ws.plan(tiles * KT + sum(KT * w // 128 for _, w in token_major))
    first_names, first_run = first or ((), {})
    aside_names, aside_run = aside or ((), {})
    with stage(k, "product_ready", "product_copied", "rows_ready", "rows_copied", *first_names, *aside_names) as (
            block, product_ready, product_copied, rows_ready, rows_copied, *sems):
        first_sems, aside_sems = sems[:len(first_names)], sems[len(first_names):]

        @block.sync
        def _(sp):
            if "sync" in first_run:
                first_run["sync"](sp, *first_sems)
            if "loads" in aside_run:
                aside_run["loads"](sp, *aside_sems)
            ws.load(sp)

        @block.scalar
        def _(act):
            if "scalar" in first_run:
                first_run["scalar"](act, *first_sems)
            if "scalar" in aside_run:
                aside_run["scalar"](act, *aside_sems)

        @block.gpsimd
        def _(pool):
            if "gpsimd" in first_run:
                first_run["gpsimd"](pool, *first_sems)
            ws.divide(pool)

        @block.tensor
        def _(pe):
            if "tensor_start" in first_run:
                first_run["tensor_start"](pe, *first_sems)
            for j in range(tiles):
                if j >= 2:
                    pe.wait_ge(product_copied, j - 1)
                for t in range(KT):
                    if j == 0 and "tensor" in first_run:
                        first_run["tensor"](pe, t, *first_sems)
                    last = ws.product(pe, k.bank[j % 2][:, 0:n_moving],
                                      (moving[0][:, t, 0:n_moving], moving[1][:, t, 0:n_moving]), t == 0, t == KT - 1)
                last.then_inc(product_ready, 1)
                if j == tiles // 2 and "tensor" in aside_run:
                    aside_run["tensor"](pe, *aside_sems)
            for m, (_, width) in enumerate(token_major):
                if m:
                    pe.wait_ge(rows_copied, m)
                for t in range(KT):
                    still = [(moving[0][:, t, 128 * q:128 * q + 128], moving[1][:, t, 128 * q:128 * q + 128])
                             for q in range(nt)]
                    last = ws.product_tm(pe, [k.bank[4 + q][:, 0:width] for q in range(nt)], still, width // 128,
                                         t == 0, t == KT - 1)
                last.then_inc(rows_ready, 1)

        @block.vector
        def _(dve):
            if "vector" in first_run:
                first_run["vector"](dve, *first_sems)
            for j in range(tiles):
                dve.wait_ge(product_ready, j + 1)
                dve.tensor_copy(out[:, j, 0:n_moving], k.bank[j % 2][:, 0:n_moving]).then_inc(product_copied, 1)
                if j == tiles // 2 and "vector" in aside_run:
                    aside_run["vector"](dve, *aside_sems)
            for m, (rows, width) in enumerate(token_major):
                dve.wait_ge(rows_ready, m + 1)
                for q in range(nt):
                    last = dve.tensor_copy(rows[:, q, :], k.bank[4 + q][:, 0:width])
                last.then_inc(rows_copied, 1)


@contextmanager
def norm_buffers(k, n=SEQ, mean=False):
    with memory(k, nrm=((13 if mean else 4), n)) as b:
        yield b[:, 0:2, :], b[:, 0:3, :], b[:, 3, :], b[:, 4, :] if mean else None, b[:, 5:13, :] if mean else None


def norm_programs(k, src, gain, bias, eps, mean, buffers, hi=None, lo=None, out=None, n=SEQ, loads=()):
    ones = const(k, "ones")
    sq, y, rstd, mu, cent = buffers
    x = cent if mean else src
    names = ("summed", "mean_ready", "centred", "squared", "square_used", "log_ready", "rstd_ready", "norm_scaled",
             "norm_rounded", "tile_done", "norm_order", "loads_in")

    def sync(sp, summed, mean_ready, centred, squared, square_used, log_ready, rstd_ready, scaled,
             rounded, tile_done, order, loads_in):
        for dst, from_dram in loads:
            sp.dma_start(dst, from_dram).then_inc(loads_in, 16)

    def tensor_start(pe, summed, mean_ready, centred, squared, square_used, log_ready, rstd_ready, scaled,
                     rounded, tile_done, order, loads_in):
        if mean:
            for t in range(KT):
                last = pe.matmul(k.bank[0][:, 0:n], ones, src[:, t, :], start=t == 0, stop=t == KT - 1)
            last.then_inc(summed, 1)
        for t in range(KT):
            pe.wait_ge(squared, t + 1)
            pe.matmul(k.bank[1][:, 0:n], ones, sq[:, t % 2, :], start=t == 0, stop=t == KT - 1).then_inc(
                square_used, 1)

    def tensor(pe, t, summed, mean_ready, centred, squared, square_used, log_ready, rstd_ready, scaled,
               rounded, tile_done, order, loads_in):
        pe.wait_ge(tile_done, t + 1)

    def scalar(act, summed, mean_ready, centred, squared, square_used, log_ready, rstd_ready, scaled,
               rounded, tile_done, order, loads_in):
        for t in range(KT):
            if mean:
                act.wait_ge(centred, t + 1)
            if t >= 2:
                act.wait_ge(square_used, t - 1)
            act.activation(sq[:, t % 2, :], x[:, t, :], ACT.Square).then_inc(squared, 1)
        act.wait_ge(square_used, KT)
        act.activation(rstd, k.bank[1][:, 0:n], ACT.Ln, scale=1.0 / D, bias=eps).then_inc(log_ready, 1)
        act.wait_ge(log_ready, 1)
        act.activation(rstd, rstd, ACT.Exp, scale=-0.5).then_inc(rstd_ready, 1)
        if hi is not None:
            if loads:
                act.wait_ge(loads_in, 16 * len(loads))
            for t in range(KT):
                act.wait_ge(scaled, t + 1)
                act.activation(hi[:, t, :], y[:, t % 3, :], ACT.Identity, scale=gain(t),
                               bias=0.0 if bias is None else bias(t)).then_inc(rounded, 1)

    def vector(dve, summed, mean_ready, centred, squared, square_used, log_ready, rstd_ready, scaled,
               rounded, tile_done, order, loads_in):
        if mean:
            dve.wait_ge(summed, 1)
            dve.tensor_scalar(mu, k.bank[0][:, 0:n], 1.0 / D, None, ALU.mult).then_inc(mean_ready, 1)
            dve.wait_ge(mean_ready, 1)
            for t in range(KT):
                dve.tensor_tensor(cent[:, t, :], src[:, t, :], mu, ALU.subtract).then_inc(centred, 1)
        dve.wait_ge(rstd_ready, 1)
        if loads:
            dve.wait_ge(loads_in, 16 * len(loads))
        for i in range(KT + 1):
            if i < KT:
                if i >= 3:
                    dve.wait_ge(tile_done, i - 2)
                dve.tensor_tensor(y[:, i % 3, :], x[:, i, :], rstd, ALU.mult).then_inc(scaled, 1)
            t = i - 1
            if t < 0:
                continue
            dve.wait_ge(scaled, t + 1)
            if out is not None:
                last = dve.tensor_scalar(out[:, t, :], y[:, t % 3, :], gain(t), bias(t), ALU.mult, ALU.add)
                if hi is not None:
                    last.then_inc(order, 1)
                    dve.wait_ge(order, t + 1)
                    dve.wait_ge(rounded, t + 1)
                    last = dve.tensor_tensor(lo[:, t, :], out[:, t, :], hi[:, t, :].bitcast(F32), ALU.subtract)
            else:
                dve.wait_ge(rounded, t + 1)
                last = dve.scalar_tensor_tensor(lo[:, t, :], y[:, t % 3, :], gain(t), hi[:, t, :].bitcast(F32),
                                                ALU.mult, ALU.subtract)
            last.then_inc(tile_done, 1)

    return names, dict(sync=sync, tensor_start=tensor_start, tensor=tensor, scalar=scalar, vector=vector)


def normalise(k, src, gain, bias, eps, mean, hi=None, lo=None, out=None, n=SEQ, stream=False):
    with norm_buffers(k, n, mean) as buffers:
        names, run = norm_programs(k, src, gain, bias, eps, mean, buffers, hi, lo, out, n)
        with stage(k, *names) as (block, *sems):
            @block.sync
            def _(sp):
                run["sync"](sp, *sems)
                if stream:
                    k.ws.load(sp)

            @block.gpsimd
            def _(pool):
                if stream:
                    k.ws.divide(pool)

            @block.tensor
            def _(pe):
                run["tensor_start"](pe, *sems)

            @block.scalar
            def _(act):
                run["scalar"](act, *sems)

            @block.vector
            def _(dve):
                run["vector"](dve, *sems)


def merge(k, scale_residual, x_dram=None):
    ws = k.ws
    with memory(k, yh=("r", KT, SEQ), yl=("r", KT, SEQ), mh=("r", KT, SEQ), ml=("r", KT, SEQ), sig=(2, SEQ),
                part=(2, SEQ)) as (yh, yl, mh, ml, sig, part):
        ws.plan(KT * 40)
        with stage(k, "gate_ready", "sigmoid_ready", "branch_ready", "banks_free", "branch_rounded", "merge_order",
                   "branch_split", "x_in") as (block, gate_ready, sigmoid_ready, branch_ready, banks_free, rounded,
                                               order, branch_split, x_in):
            @block.sync
            def _(sp):
                if x_dram is not None:
                    sp.dma_start(k.res[:, :, :], x_dram).then_inc(x_in, 16)
                ws.load(sp)
                if x_dram is not None:
                    sp.wait_ge(x_in, 16)

            @block.gpsimd
            def _(pool):
                ws.divide(pool)

            @block.tensor
            def _(pe):
                for dt in range(KT):
                    for n in range(4):
                        u = 4 * dt + n
                        if u >= 2:
                            pe.wait_ge(banks_free, u - 1)
                        g, b = k.bank[2 * (u % 2)], k.bank[2 * (u % 2) + 1]
                        for t in range(KT):
                            last = ws.product(pe, g[:, :], (k.xh[:, t, :], k.xl[:, t, :]), t == 0, t == KT - 1)
                        last.then_inc(gate_ready, 1)
                        if u == 0:
                            pe.wait_ge(branch_split, KT)
                        for c in range(2):
                            last = ws.product(pe, b[:, :], (yh[:, 2 * n + c, :], yl[:, 2 * n + c, :]), c == 0, c == 1)
                        last.then_inc(branch_ready, 1)

            @block.scalar
            def _(act):
                for u in range(4 * KT):
                    act.wait_ge(gate_ready, u + 1)
                    if u >= 2:
                        act.wait_ge(banks_free, u - 1)
                    act.activation(sig[:, u % 2, :], k.bank[2 * (u % 2)][:, :], ACT.Sigmoid).then_inc(
                        sigmoid_ready, 1)

            @block.vector
            def _(dve):
                step = Order(dve, order)
                for t in range(KT):
                    step(dve.tensor_copy(yh[:, t, :], k.yb[:, t, :]))
                    dve.tensor_tensor(yl[:, t, :], k.yb[:, t, :], yh[:, t, :].bitcast(F32), ALU.subtract).then_inc(
                        branch_split, 1)
                for dt in range(KT):
                    for n in range(4):
                        u = 4 * dt + n
                        dve.wait_ge(sigmoid_ready, u + 1)
                        dve.wait_ge(branch_ready, u + 1)
                        dve.tensor_tensor(part[:, 0 if n == 0 else 1, :], sig[:, u % 2, :],
                                          k.bank[2 * (u % 2) + 1][:, :], ALU.mult).then_inc(banks_free, 1)
                        dve.wait_ge(banks_free, u + 1)
                        if n:
                            step(dve.tensor_tensor(part[:, 0, :], part[:, 0, :], part[:, 1, :], ALU.add))
                    step(dve.tensor_copy(mh[:, dt, :], part[:, 0, :]))
                    step(dve.tensor_tensor(ml[:, dt, :], part[:, 0, :], mh[:, dt, :].bitcast(F32), ALU.subtract))
        add_product(k, KT, mh, ml, scale_residual)


def add_product(k, tiles_in, hi, lo, scale_residual):
    ws = k.ws
    ws.plan(KT * tiles_in)
    with stage(k, "product_ready", "product_added") as (block, product_ready, product_added):
        @block.sync
        def _(sp):
            ws.load(sp)

        @block.gpsimd
        def _(pool):
            ws.divide(pool)

        @block.tensor
        def _(pe):
            for dt in range(KT):
                if dt >= 2:
                    pe.wait_ge(product_added, dt - 1)
                for t in range(tiles_in):
                    last = ws.product(pe, k.bank[dt % 2][:, :], (hi[:, t, :], lo[:, t, :]), t == 0,
                                      t == tiles_in - 1)
                last.then_inc(product_ready, 1)

        @block.vector
        def _(dve):
            for dt in range(KT):
                dve.wait_ge(product_ready, dt + 1)
                dve.scalar_tensor_tensor(k.res[:, dt, :], k.res[:, dt, :], scale_residual, k.bank[dt % 2][:, :],
                                         ALU.mult, ALU.add).then_inc(product_added, 1)


def attention(k, units, outs, strip_loads=(), strips_per=1):
    n_units = len(units)
    last_of_pair = {}
    last_of_strip = {}
    for i, u in enumerate(units):
        last_of_pair[u["pair"]] = i
        if u["strip"] is not None:
            last_of_strip[u["strip"]] = i
    with memory(k, att_p=(3, SEQ), att_t=(2, SEQ), att_s=(3, 4)) as (prob, probt, small), \
            stage(k, "scores_ready", "biased", "exp_ready", "probs_ready", "turned", "turned_copied", "unit_done",
                  "pair_copied", "vector_order", "strip_even", "strip_odd") as (
                block, scores_ready, biased, exp_ready, probs_ready, turned, turned_copied, unit_done, pair_copied,
                order, strip_even, strip_odd):
        strip_sem = (strip_even, strip_odd)
        score_bank = lambda i: k.bank[i % 3]
        turn_bank = lambda i: k.bank[3 + i % 2]
        pair_bank = lambda p: k.bank[5 + p % 2]

        @block.sync
        def _(sp):
            for s, (dst, src) in enumerate(strip_loads):
                if s >= 2:
                    sp.wait_ge(biased, last_of_strip[s - 2] + 1)
                sp.dma_start(dst, src).then_inc(strip_sem[s % 2], 16)

        @block.tensor
        def _(pe):
            for i in range(n_units + 3):
                if i < n_units:
                    u = units[i]
                    if i >= 3:
                        pe.wait_ge(biased, i - 2)
                    pe.matmul(score_bank(i)[:, 0:u["n"]], u["q"], u["keys"], start=True, stop=True).then_inc(
                        scores_ready, 1)
                v = i - 2
                if 0 <= v < n_units:
                    pe.wait_ge(probs_ready, v + 1)
                    if v >= 2:
                        pe.wait_ge(turned_copied, v - 1)
                    for j in range(units[v]["n"] // 128):
                        last = pe.transpose(turn_bank(v)[:, 128 * j:128 * j + 128],
                                            prob[:, v % 3, 128 * j:128 * j + 128], const(k, "ident"))
                    last.then_inc(turned, 1)
                w = i - 3
                if w >= 0:
                    u = units[w]
                    pe.wait_ge(turned_copied, w + 1)
                    if u["pair"] >= 2:
                        pe.wait_ge(pair_copied, u["pair"] - 1)
                    nj = u["n"] // 128
                    for j in range(nj):
                        last = pe.matmul(pair_bank(u["pair"])[u["rows"], u["cols"]], u["values"][j],
                                         probt[:, w % 2, 128 * j:128 * j + 128], start=j == 0, stop=j == nj - 1)
                    last.then_inc(unit_done, 1)

        @block.scalar
        def _(act):
            for i in range(n_units + 2):
                if i < n_units:
                    u = units[i]
                    act.wait_ge(biased, i + 1)
                    act.activation(prob[:, i % 3, 0:u["n"]], prob[:, i % 3, 0:u["n"]], ACT.Exp,
                                   bias=small[:, i % 3, 0:1], accum_out=small[:, i % 3, 1:2]).then_inc(exp_ready, 1)
                v = i - 2
                if v >= 0:
                    n = units[v]["n"]
                    act.wait_ge(turned, v + 1)
                    if v >= 2:
                        act.wait_ge(unit_done, v - 1)
                    act.activation(probt[:, v % 2, 0:n], turn_bank(v)[:, 0:n], ACT.Copy).then_inc(turned_copied, 1)

        @block.vector
        def _(dve):
            step = Order(dve, order)
            waited = -1
            for i in range(n_units + 1):
                if i < n_units:
                    u = units[i]
                    p = prob[:, i % 3, 0:u["n"]]
                    dve.wait_ge(scores_ready, i + 1)
                    if i >= 3:
                        dve.wait_ge(turned, i - 2)
                    if u["strip"] is not None and u["strip"] != waited:
                        waited = u["strip"]
                        dve.wait_ge(strip_sem[waited % 2], 16 * (waited // 2 + 1))
                    s = score_bank(i)[:, 0:u["n"]]
                    if u["bias"] is None:
                        step(dve.tensor_scalar(p, s, u["scale"], None, ALU.mult))
                    else:
                        step(dve.scalar_tensor_tensor(p, s, u["scale"], u["bias"], ALU.mult, ALU.add))
                    if u["select"] is not None:
                        step(dve.tensor_tensor(p, p, u["select"], ALU.add))
                    dve.tensor_reduce(small[:, i % 3, 0:1], p, AX.X, ALU.max, negate=True).then_inc(biased, 1)
                v = i - 1
                if v >= 0:
                    b, n = v % 3, units[v]["n"]
                    dve.wait_ge(exp_ready, v + 1)
                    step(dve.reciprocal(small[:, b, 2:3], small[:, b, 1:2]))
                    dve.tensor_scalar(prob[:, b, 0:n], prob[:, b, 0:n], small[:, b, 2:3], None, ALU.mult).then_inc(
                        probs_ready, 1)
                    pair = units[v]["pair"]
                    if last_of_pair[pair] == v and pair >= 1:
                        dve.wait_ge(unit_done, last_of_pair[pair - 1] + 1)
                        dve.tensor_copy(outs[pair - 1], pair_bank(pair - 1)[:, :]).then_inc(pair_copied, 1)
            pair = units[-1]["pair"]
            dve.wait_ge(unit_done, n_units)
            dve.tensor_copy(outs[pair], pair_bank(pair)[:, :]).then_inc(pair_copied, 1)




def distance_bias(k, bias_dram, rows, tab, out):
    names = ("rows_in", "bias_ready", "bias_copied", "bias_stored")

    def loads(sp, rows_in, *_):
        sp.dma_start(rows[0:34, :], k.dram["dist_rows"]).then_inc(rows_in, 16)
        sp.dma_start(tab[0:34, :], k.dram["rpb"]).then_inc(rows_in, 16)

    def scalar(act, rows_in, bias_ready, bias_copied, bias_stored):
        act.wait_ge(bias_copied, 2)
        for h in range(8):
            row = out[h:h + 1, :].rearrange("p (a x) -> p a x", a=1).to_broadcast([1, 128, 1024])
            act.dma_start(bias_dram[h:h + 1, :, :], row).then_inc(bias_stored, 16)
        act.wait_ge(bias_stored, 128)

    def tensor(pe, rows_in, bias_ready, bias_copied, bias_stored):
        pe.wait_ge(rows_in, 32)
        for j in range(2):
            pe.matmul(k.bank[2 + j][0:8, :], tab[0:34, :], rows[0:34, 512 * j:512 * j + 512], start=True,
                      stop=True).then_inc(bias_ready, 1)

    def vector(dve, rows_in, bias_ready, bias_copied, bias_stored):
        for j in range(2):
            dve.wait_ge(bias_ready, j + 1)
            dve.tensor_copy(out[0:8, 512 * j:512 * j + 512], k.bank[2 + j][0:8, :]).then_inc(bias_copied, 1)
    return names, dict(loads=loads, scalar=scalar, tensor=tensor, vector=vector)


def head_norm(k, jobs):
    blk = const(k, "blk64")
    width = [job["src"].shape[-1] for job in jobs]
    with memory(k, hn_sq=(2, SEQ), hn_r=(len(jobs), SEQ)) as (sq, r), \
            stage(k, "squared", "summed", "log_ready", "rstd_ready", "finished", "vector_order") as (
                block, squared, summed, log_ready, rstd_ready, finished, order):
        @block.tensor
        def _(pe):
            for i, n in enumerate(width):
                pe.wait_ge(squared, i + 1)
                pe.matmul(k.bank[i][:, 0:n], blk, sq[:, i % 2, 0:n], start=True, stop=True).then_inc(summed, 1)

        @block.scalar
        def _(act):
            for i, n in enumerate(width):
                if i >= 2:
                    act.wait_ge(summed, i - 1)
                act.activation(sq[:, i % 2, 0:n], jobs[i]["src"], ACT.Square).then_inc(squared, 1)
            for i, n in enumerate(width):
                act.wait_ge(summed, i + 1)
                act.activation(r[:, i, 0:n], k.bank[i][:, 0:n], ACT.Ln, scale=jobs[i]["scale"],
                               bias=jobs[i]["eps"]).then_inc(log_ready, 1)
            for i, n in enumerate(width):
                act.wait_ge(log_ready, i + 1)
                act.activation(r[:, i, 0:n], r[:, i, 0:n], ACT.Exp, scale=-0.5).then_inc(rstd_ready, 1)

        @block.vector
        def _(dve):
            step = Order(dve, order)
            for i, n in enumerate(width):
                dve.wait_ge(rstd_ready, i + 1)
                jobs[i]["finish"](dve, step, r[:, i, 0:n]).then_inc(finished, 1)
                dve.wait_ge(finished, i + 1)


def gained(src, gain):
    def finish(dve, step, rstd):
        step(dve.tensor_tensor(src, src, rstd, ALU.mult))
        return dve.tensor_scalar(src, src, gain, None, ALU.mult)
    return finish


def turn(k, jobs):
    with stage(k, "turned", "turned_copied") as (block, turned, turned_copied):
        @block.tensor
        def _(pe):
            for i, (_, srcs) in enumerate(jobs):
                if i >= 2:
                    pe.wait_ge(turned_copied, i - 1)
                for j, s in enumerate(srcs):
                    last = pe.transpose(k.bank[i % 2][:, 128 * j:128 * j + 128], s, const(k, "ident"))
                last.then_inc(turned, 1)

        @block.vector
        def _(dve):
            for i, (out, srcs) in enumerate(jobs):
                dve.wait_ge(turned, i + 1)
                dve.tensor_copy(out, k.bank[i % 2][:, 0:128 * len(srcs)]).then_inc(turned_copied, 1)


def select_keys(k, pj, lowt, select):
    heads, keep = 8, 128
    with memory(k, ix_rel=(4, SEQ), ix_score=(3, SEQ), ix_top=(3, 8)) as (rel, score, top), \
            stage(k, "score_ready", "rel_ready", "rel_used", "step_done") as (
                block, score_ready, rel_ready, rel_used, step_done):
        units = [(i, h) for h in range(heads) for i in (1, 2, 3)]

        @block.tensor
        def _(pe):
            for u, (i, h) in enumerate(units):
                if u >= 4:
                    pe.wait_ge(rel_ready, u - 3)
                rows = slice(32 * (h % 4), 32 * (h % 4) + 32)
                pe.matmul(k.bank[u % 4][:, 0:128 * i + 128],
                          pj[rows, T1["iq"] + h // 4, 128 * i:128 * i + 128],
                          pj[rows, T1["ik"], 0:128 * i + 128], start=True, stop=True).then_inc(score_ready, 1)

        @block.scalar
        def _(act):
            for u, (i, h) in enumerate(units):
                act.wait_ge(score_ready, u + 1)
                if u >= 4:
                    act.wait_ge(rel_used, u - 3)
                n = 128 * i + 128
                act.activation(rel[:, u % 4, 0:n], k.bank[u % 4][:, 0:n], ACT.Relu, scale=32 ** -0.5).then_inc(
                    rel_ready, 1)

        @block.vector
        def _(dve):
            for u, (i, h) in enumerate(units):
                n = 128 * i + 128
                s = score[:, i - 1, 0:n]
                dve.wait_ge(rel_ready, u + 1)
                weight = lowt[:, i, 112 + h:113 + h]
                if h == 0:
                    dve.tensor_scalar(s, rel[:, u % 4, 0:n], weight, None, ALU.mult).then_inc(rel_used, 1)
                else:
                    dve.wait_ge(rel_used, u - 2)
                    dve.scalar_tensor_tensor(s, rel[:, u % 4, 0:n], weight, s, ALU.mult, ALU.add).then_inc(
                        rel_used, 1)
            dve.wait_ge(rel_used, len(units))
            tiles = [(score[:, i - 1, 0:128 * i + 128], top[:, i - 1, :], select[:, i - 1, 0:128 * i + 128])
                     for i in (1, 2, 3)]
            done = 0
            for n in range(2 * (keep // 8) + 3):
                for s, best, out in tiles:
                    if done >= 3:
                        dve.wait_ge(step_done, done - 2)
                    if n == 0:
                        last = dve.tensor_scalar(s, s, heads ** -0.5, None, ALU.mult)
                    elif n == 1:
                        own = s[:, s.shape[-1] - 128:s.shape[-1]]
                        last = dve.tensor_tensor(own, own, const(k, "future"), ALU.add)
                    elif n == 2 * (keep // 8) + 2:
                        last = dve.tensor_scalar(out, s, TAKEN / 2, MASKED, ALU.is_gt, ALU.mult)
                    elif n % 2 == 0:
                        last = dve.max(best, s)
                    else:
                        last = dve.match_replace(s, best, s, TAKEN)
                    last.then_inc(step_done, 1)
                    done += 1


def mixers_ab(k, pj, av, bias_dram):
    yb = k.yb
    kv = pj[:, T1["ckv"], :]
    g = k.par1[:, P1["kv_gain"]:P1["kv_gain"] + 1]
    head_norm(k, [dict(src=kv, scale=1.0 / 64, eps=k.eps[:, 1:2], finish=gained(kv, g))])
    with memory(k, low_t=(4, 128), kv_t=(4, 128), strips=(2, STRIP)) as (lowt, kvt, strips):
        tiles = [slice(128 * t, 128 * t + 128) for t in range(4)]
        turn(k, [(lowt[:, :, :], [pj[:, T1["low"], t] for t in tiles]),
                 (kvt[:, :, :], [pj[:, T1["ckv"], t] for t in tiles])])
        select = k.res[:, 0:3, :]
        select_keys(k, pj, lowt, select)
        units, loads = [], []
        for head in range(8):
            b, h = divmod(head, 4)
            rows = slice(64 * (h % 2), 64 * (h % 2) + 64)
            loads.append((strips[:, head % 2, :],
                          bass.AP(tensor=bias_dram.tensor, offset=128 * 1024 * head + 127,
                                  ap=[[1023, 128], [1, STRIP]])))
            for i in range(4):
                n = 128 * i + 128
                q = pj[rows, (T1["aq"], T1["bq"])[b] + h // 2, tiles[i]]
                if b == 0:
                    keys = pj[rows, T1["ak"] + h // 2, 0:n]
                    values = [av[:, j, 64 * h:64 * h + 64] for j in range(i + 1)]
                else:
                    keys = pj[rows, T1["ckv"], 0:n]
                    values = [kvt[:, j, 0:64] for j in range(i + 1)]
                units.append(dict(q=q, keys=keys, n=n, scale=0.125, strip=head, values=values, pair=2 * b + h // 2,
                                  bias=strips[:, head % 2, 384 - 128 * i:384 - 128 * i + n],
                                  select=select[:, i - 1, 0:n] if b and i else None, rows=rows, cols=tiles[i]))
        attention(k, units, [yb[:, 0, :], yb[:, 1, :], yb[:, 2, :], yb[:, 3, :]], strip_loads=loads)
    small_products(k, [(yb[:, 2 + p, :], k.mats1[:, 256 + 128 * p:384 + 128 * p], yb[:, 2 + p, :], None)
                       for p in range(2)])


def small_products(k, jobs):
    with stage(k, "product_ready", "product_copied") as (block, product_ready, product_copied):
        @block.tensor
        def _(pe):
            for i, (_, lhs, rhs, _) in enumerate(jobs):
                if i >= 2:
                    pe.wait_ge(product_copied, i - 1)
                pe.matmul(k.bank[i % 2][:, 0:rhs.shape[-1]], lhs, rhs, start=True, stop=True).then_inc(
                    product_ready, 1)

        @block.vector
        def _(dve):
            for i, (out, _, rhs, scale) in enumerate(jobs):
                dve.wait_ge(product_ready, i + 1)
                b = k.bank[i % 2][:, 0:rhs.shape[-1]]
                if scale is None:
                    dve.tensor_copy(out, b).then_inc(product_copied, 1)
                else:
                    dve.tensor_scalar(out, b, scale, None, ALU.mult).then_inc(product_copied, 1)


def mixer_c(k, pj, cv):
    p1 = lambda n, j=0: k.par1[:, P1[n] + j:P1[n] + j + 1]
    q, key = pj[:, T1["cq"], :], pj[:, T1["ck"], :]
    chunked = lambda ap: ap.rearrange("p (c t) -> p c t", t=64)
    with memory(k, cum=(SEQ,), dec=(8,), e_tmp=(SEQ,), qd=(SEQ,), ki=(SEQ,), ku=(SEQ,), kut=(4, 128), att=(4, 4, 128),
                st=(8, 256)) as (cum, dec, tmp, qd, ki, ku, kut, att, st):
        with stage(k, "gate_ready", "abs_ready", "exp_ready", "log_ready", "cum_ready", "decays_ready",
                   "vector_order") as (block, gate_ready, abs_ready, exp_ready, log_ready, cum_ready, decays_ready,
                                       order):
            @block.tensor
            def _(pe):
                pe.matmul(k.bank[0][:, :], k.mats1[96:112, 0:128], pj[96:112, T1["low"], :], start=True,
                          stop=True).then_inc(gate_ready, 1)

            @block.scalar
            def _(act):
                act.wait_ge(abs_ready, 1)
                act.activation(tmp[:, :], tmp[:, :], ACT.Exp, scale=-1.0).then_inc(exp_ready, 1)
                act.wait_ge(exp_ready, 1)
                act.activation(tmp[:, :], tmp[:, :], ACT.Ln, bias=k.eps[:, 3:4]).then_inc(log_ready, 1)
                act.wait_ge(cum_ready, 1)
                act.activation(qd[:, :], cum[:, :], ACT.Exp).then_inc(decays_ready, 1)
                act.activation(ki[:, :], cum[:, :], ACT.Exp, scale=-1.0).then_inc(decays_ready, 1)
                act.activation(dec[:, :], chunked(cum[:, :])[:, :, 63], ACT.Exp).then_inc(decays_ready, 1)
                act.wait_ge(cum_ready, 2)
                act.activation(ku[:, :], tmp[:, :], ACT.Exp).then_inc(decays_ready, 1)

            @block.vector
            def _(dve):
                step = Order(dve, order)
                dve.wait_ge(gate_ready, 1)
                step(dve.tensor_scalar(cum[:, :], k.bank[0][:, :], p1("a_bias"), None, ALU.add))
                step(dve.tensor_scalar(ku[:, :], cum[:, :], -1.0, None, ALU.mult))
                dve.tensor_tensor(tmp[:, :], cum[:, :], ku[:, :], ALU.max).then_inc(abs_ready, 1)
                dve.wait_ge(abs_ready, 1)
                step(dve.tensor_scalar(ku[:, :], cum[:, :], 0.0, 1.0 / 16, ALU.min, ALU.mult))
                dve.wait_ge(log_ready, 1)
                step(dve.scalar_tensor_tensor(ku[:, :], tmp[:, :], -1.0 / 16, ku[:, :], ALU.mult, ALU.add))
                dve.tensor_tensor_scan(cum[:, :], const(k, "reset64"), ku[:, :], 0.0, ALU.mult, ALU.add).then_inc(
                    cum_ready, 1)
                dve.wait_ge(cum_ready, 1)
                last = chunked(cum[:, :])[:, :, 63:64].to_broadcast([128, 8, 64])
                dve.tensor_tensor(chunked(tmp[:, :]), last, chunked(cum[:, :]), ALU.subtract).then_inc(cum_ready, 1)
                dve.wait_ge(decays_ready, 4)
                step(dve.scalar_tensor_tensor(qd[:, :], q, 32 ** -0.5, qd[:, :], ALU.mult, ALU.mult))
                step(dve.tensor_tensor(ki[:, :], key, ki[:, :], ALU.mult))
                step(dve.tensor_tensor(ku[:, :], key, ku[:, :], ALU.mult))
                step(dve.memset(st[:, 0, :], 0.0))
        update_bank = lambda n: 2 * (n % 2) + n // 4
        update_cols = lambda n: slice(256 * (n // 2 % 2), 256 * (n // 2 % 2) + 256)
        turn(k, [(kut[:, :, :], [ku[:, 128 * t:128 * t + 128] for t in range(4)])])
        with stage(k, "att_ready", "att_masked", "update_ready", "silu_ready", "states_ready", "out_ready",
                   "out_copied", "vector_order") as (block, att_ready, att_masked, update_ready, silu_ready,
                                                     states_ready, out_ready, out_copied, order):
            @block.scalar
            def _(act):
                for p in range(2):
                    g = pj[:, T1["cg"] + p, :]
                    act.activation(g, g, ACT.Silu).then_inc(silu_ready, 1)

            @block.tensor
            def _(pe):
                for n in range(8):
                    rows = slice(64 * (n % 2), 64 * (n % 2) + 64)
                    pe.matmul(k.bank[update_bank(n)][:, update_cols(n)], kut[rows, n // 2, :], cv[rows, n // 2, :],
                              start=True, stop=True).then_inc(update_ready, 1)
                for h in range(4):
                    rows = slice(32 * h, 32 * h + 32)
                    for t in range(4):
                        c = slice(128 * t, 128 * t + 128)
                        last = pe.matmul(k.bank[4 + h][:, c], ki[rows, c], qd[rows, c], start=True, stop=True)
                    last.then_inc(att_ready, 1)
                pe.wait_ge(states_ready, 1)
                pe.wait_ge(att_masked, 4)
                for p in range(2):
                    out = k.bank[p]
                    for n in range(8):
                        pe.matmul(out[:, 64 * n:64 * n + 64], st[:, n, 128 * p:128 * p + 128],
                                  qd[:, 64 * n:64 * n + 64], start=n == 0, stop=False, skip_group_check=True)
                    for h in (2 * p, 2 * p + 1):
                        rows = slice(64 * (h % 2), 64 * (h % 2) + 64)
                        for t in range(4):
                            last = pe.matmul(out[rows, 128 * t:128 * t + 128], cv[:, t, 64 * h:64 * h + 64],
                                             att[:, h, t, :], start=False, stop=(h % 2 == 1 and t == 3),
                                             skip_group_check=True)
                    last.then_inc(out_ready, 1)

            @block.vector
            def _(dve):
                step = Order(dve, order)
                heads = const(k, "gla_heads")
                for n in range(8):
                    dve.wait_ge(update_ready, 8)
                    upd = k.bank[update_bank(n)][:, update_cols(n)]
                    if n < 7:
                        step(dve.tensor_tensor(st[:, n + 1, :], upd, heads, ALU.mult))
                        step(dve.scalar_tensor_tensor(st[:, n + 1, :], st[:, n, :], dec[:, n:n + 1], st[:, n + 1, :],
                                                      ALU.mult, ALU.add))
                dve.tensor_copy(tmp[:, 0:8], dec[:, :]).then_inc(states_ready, 1)
                mask = const(k, "gla_mask").rearrange("p (a t) -> p a t", a=1).to_broadcast([128, 4, 128])
                for h in range(4):
                    dve.wait_ge(att_ready, h + 1)
                    dve.tensor_tensor(att[:, h, :, :], k.bank[4 + h][:, :].rearrange("p (a t) -> p a t", a=4), mask,
                                      ALU.mult).then_inc(att_masked, 1)
                for p in range(2):
                    dve.wait_ge(out_ready, p + 1)
                    dve.tensor_copy(k.yb[:, 4 + p, :], k.bank[p][:, :]).then_inc(out_copied, 1)

    def finish(p):
        y = k.yb[:, 4 + p, :]

        def run(dve, step, rstd):
            step(dve.tensor_tensor(y, y, rstd, ALU.mult))
            return dve.scalar_tensor_tensor(y, y, p1("c_norm", p), pj[:, T1["cg"] + p, :], ALU.mult, ALU.mult)
        return run

    head_norm(k, [dict(src=k.yb[:, 4 + p, :], scale=1.0 / 64, eps=k.eps[:, 1:2], finish=finish(p))
                  for p in range(2)])


def mixer_d(k, pj, av, cv):
    p1 = lambda n, j=0: k.par1[:, P1[n] + j:P1[n] + j + 1]
    low = pj[:, T1["low"], :]
    tiled = lambda ap: ap.rearrange("p (c t) -> p c t", t=128)
    R, K_, V = T1["dr"], T1["dk"], T1["dv"]
    wk = [pj[:, n, :] for n in range(T1["low"])]
    rs = [k.res[:, n, :] for n in range(KT)]
    lg, cw, ic, ga = wk[0:2], wk[2:4], wk[4:6], wk[6:8]
    kk, bonus = rs[0:2], rs[2:4]
    at, bt = rs[4:6], rs[6:8]
    tmp, tmp2 = wk[8], wk[9]
    rt, kt = pj[:, R:R + 2, :], pj[:, K_:K_ + 2, :]
    cg = [pj[:, n, :] for n in range(T1["cq"], T1["cq"] + 4)]
    sh = cg[0]
    e_dn, e_up, e_a = cg[1], cg[2], cg[3]
    with memory(k, tl=(SEQ,), zs=(2, 4)) as (tl, zs):
        with stage(k, "vector_order") as (block, order):
            @block.vector
            def _(dve):
                step = Order(dve, order)
                for j, t in enumerate([R, R + 1, K_, K_ + 1, V, V + 1, T1["low"]]):
                    z = pj[:, t, :]
                    step(dve.tensor_tensor(sh[:, 1:SEQ], z[:, 0:SEQ - 1], z[:, 1:SEQ], ALU.subtract))
                    step(dve.tensor_scalar(sh[:, 0:1], z[:, 0:1], -1.0, None, ALU.mult))
                    step(dve.scalar_tensor_tensor(z, sh, p1("mu", j), z, ALU.mult, ALU.add))
        with stage(k, "inner_ready", "low_ready", "sigmoids_ready", "gates_copied", "vector_order") as (
                block, inner_ready, low_ready, sigmoids_ready, gates_copied, order):
            @block.scalar
            def _(act):
                act.activation(tl[0:16, :], low[0:16, :], ACT.Tanh).then_inc(inner_ready, 1)
                act.activation(tl[32:48, :], low[32:48, :], ACT.Copy).then_inc(inner_ready, 1)
                act.activation(tl[64:96, :], low[64:96, :], ACT.Sigmoid).then_inc(inner_ready, 1)
                act.wait_ge(low_ready, 6)
                for p in range(2):
                    act.activation(lg[p], k.bank[p][:, :], ACT.Sigmoid, bias=p1("w0", p)).then_inc(sigmoids_ready, 1)
                    act.activation(ic[p], k.bank[2 + p][:, :], ACT.Sigmoid, bias=p1("a0", p)).then_inc(
                        sigmoids_ready, 1)

            @block.tensor
            def _(pe):
                pe.wait_ge(inner_ready, 3)
                for m, rows in enumerate((slice(0, 16), slice(32, 48), slice(64, 96))):
                    for p in range(2):
                        pe.matmul(k.bank[2 * m + p][:, :], k.mats1[rows, 128 * p:128 * p + 128], tl[rows, :],
                                  start=True, stop=True).then_inc(low_ready, 1)

            @block.vector
            def _(dve):
                step = Order(dve, order)
                dve.wait_ge(low_ready, 6)
                for p in range(2):
                    step(dve.tensor_copy(ga[p], k.bank[4 + p][:, :]))
                dve.wait_ge(sigmoids_ready, 4)
                for p in range(2):
                    step(dve.tensor_scalar(lg[p], lg[p], -math.exp(-0.5), None, ALU.mult))
                    step(dve.tensor_tensor_scan(cw[p], const(k, "reset128"), lg[p], 0.0, ALU.mult, ALU.add))
                    step(dve.tensor_scalar(kk[p], pj[:, K_ + p, :], p1("k_k", p), None, ALU.mult))
                    step(dve.tensor_scalar(tmp, ic[p], 1.0, p1("k_a", p), ALU.subtract, ALU.mult))
                    step(dve.scalar_tensor_tensor(pj[:, K_ + p, :], tmp, 1.0, pj[:, K_ + p, :], ALU.add, ALU.mult))
                    step(dve.scalar_tensor_tensor(bonus[p], pj[:, R + p, :], p1("r_k", p), pj[:, K_ + p, :],
                                                  ALU.mult, ALU.mult))
        with stage(k, "squared", "summed", "norm_ready", "exponent_ready", "exps_ready", "exps_used",
                   "scales_ready", "vector_order") as (block, squared, summed, norm_ready, exponent_ready,
                                                       exps_ready, exps_used, scales_ready, order):
            @block.tensor
            def _(pe):
                for p in range(2):
                    pe.matmul(k.bank[2 + p][:, :], const(k, "blk64"), bonus[p], start=True, stop=True)
                for p in range(2):
                    pe.wait_ge(squared, p + 1)
                    pe.matmul(k.bank[p][:, :], const(k, "blk64"), (tl[:, :], sh)[p], start=True, stop=True).then_inc(
                        summed, 1)

            @block.scalar
            def _(act):
                for p in range(2):
                    act.activation((tl[:, :], sh)[p], kk[p], ACT.Square).then_inc(squared, 1)
                for p in range(2):
                    act.wait_ge(summed, p + 1)
                    act.activation((tl[:, :], sh)[p], k.bank[p][:, :], ACT.Sqrt).then_inc(norm_ready, 1)
                for p in range(2):
                    act.wait_ge(exponent_ready, 3 * p + 3)
                    act.activation(e_dn, cw[p], ACT.Exp).then_inc(exps_ready, 1)
                    act.activation(e_up, cw[p], ACT.Exp, scale=-1.0).then_inc(exps_ready, 1)
                    act.activation(e_a, lg[p], ACT.Exp).then_inc(exps_ready, 1)
                    act.activation(zs[:, p, :], zs[:, p, :], ACT.Exp).then_inc(exps_ready, 1)
                    act.wait_ge(exps_used, p + 1)

            @block.vector
            def _(dve):
                step = Order(dve, order)
                dve.wait_ge(summed, 2)
                for p in range(2):
                    nrm = (tl[:, :], sh)[p]
                    step(dve.tensor_tensor(bonus[p], k.bank[2 + p][:, :], pj[:, V + p, :], ALU.mult))
                    dve.wait_ge(norm_ready, p + 1)
                    step(dve.tensor_scalar(nrm, nrm, 1e-12, None, ALU.max))
                    step(dve.reciprocal(nrm, nrm))
                    step(dve.tensor_tensor(kk[p], kk[p], nrm, ALU.mult))
                for p in range(2):
                    c = tiled(cw[p])
                    step(dve.tensor_tensor(zs[:, p, :], c[:, :, 127], c[:, :, 63], ALU.subtract))
                    dve.tensor_tensor(zs[:, p, 0:3], zs[:, p, 0:3], c[:, 1:4, 63], ALU.add).then_inc(
                        exponent_ready, 1)
                    step(dve.tensor_copy(tmp2[:, 0:4], c[:, :, 63]))
                    mid = tmp2[:, 0:4].rearrange("p (c t) -> p c t", t=1).to_broadcast([128, 4, 128])
                    dve.tensor_tensor(c, c, mid, ALU.subtract).then_inc(exponent_ready, 1)
                    dve.wait_ge(exponent_ready, 3 * p + 2)
                    dve.tensor_tensor(lg[p], cw[p], lg[p], ALU.subtract).then_inc(exponent_ready, 1)
                    dve.wait_ge(exps_ready, 4 * p + 4)
                    step(dve.scalar_tensor_tensor(at[p], kk[p], -1.0, e_a, ALU.mult, ALU.mult))
                    step(dve.tensor_tensor(bt[p], kk[p], ic[p], ALU.mult))
                    step(dve.tensor_tensor(bt[p], bt[p], e_up, ALU.mult))
                    step(dve.tensor_tensor(kt[:, p, :], kt[:, p, :], e_up, ALU.mult))
                    dve.tensor_tensor(rt[:, p, :], rt[:, p, :], e_dn, ALU.mult).then_inc(exps_used, 1)
                    dve.wait_ge(exps_used, p + 1)
        vt = pj[:, 0:2, :].rearrange("p a (c n) -> p (a c) n", c=2)
        btt = pj[:, 2:4, :].rearrange("p a (c n) -> p (a c) n", c=2)
        ktt = pj[:, 4:6, :].rearrange("p a (c n) -> p (a c) n", c=2)
        tiles = [slice(128 * t, 128 * t + 128) for t in range(4)]
        jobs = []
        for dst, src in ((vt, [pj[:, V + p, :] for p in range(2)]), (btt, bt), (ktt, [kt[:, 0, :], kt[:, 1, :]])):
            for c in range(0, 4, 2):
                jobs.append((dst[:, c:c + 2, :].rearrange("p c n -> p (c n)"),
                             [src[p][:, tiles[c + e]] for e in range(2) for p in range(2)]))
        turn(k, jobs)
        pairs = lambda rows: [rows[:, t:t + 2, :].rearrange("p a n -> p (a n)") for t in (0, 2)]
        free = cg + [wk[8], wk[9], rs[0], rs[1], low, pj[:, V, :], pj[:, V + 1, :]] + pairs(av) + pairs(cv)
        delta_chunks(k, at, bt, kt, rt, vt, btt, ktt, zs, free)
        y = [k.yb[:, 6, :], k.yb[:, 7, :]]
        with stage(k, "mean_ready", "vector_order") as (block, mean_ready, order):
            @block.tensor
            def _(pe):
                for p in range(2):
                    pe.matmul(k.bank[p][:, :], const(k, "blk64"), y[p], start=True, stop=True).then_inc(
                        mean_ready, 1)

            @block.vector
            def _(dve):
                step = Order(dve, order)
                for p in range(2):
                    dve.wait_ge(mean_ready, p + 1)
                    step(dve.scalar_tensor_tensor(y[p], k.bank[p][:, :], -1.0 / 64, y[p], ALU.mult, ALU.add))

        def finish(p):
            def run(dve, step, rstd):
                step(dve.tensor_tensor(y[p], y[p], rstd, ALU.mult))
                step(dve.tensor_scalar(y[p], y[p], p1("gn_w", p), p1("gn_b", p), ALU.mult, ALU.add))
                step(dve.tensor_tensor(y[p], y[p], bonus[p], ALU.add))
                return dve.tensor_tensor(y[p], y[p], ga[p], ALU.mult)
            return run

        head_norm(k, [dict(src=y[p], scale=1.0 / 64, eps=k.eps[:, 2:3], finish=finish(p)) for p in range(2)])


def delta_chunks(k, at, bt, kt, rt, vt, btt, ktt, zs, free):
    SETS, LAG = 15, 3
    four = lambda ap: ap.rearrange("p (h t) -> p h t", h=4)
    wide = lambda name, n: const(k, name).rearrange("p (a t) -> p a t", a=1).to_broadcast([128, n, 128])
    rows = [slice(64 * (h % 2), 64 * (h % 2) + 64) for h in range(4)]
    quarter = [slice(128 * h, 128 * h + 128) for h in range(4)]
    order_of_sets = []
    for n in range(2 * SETS + LAG):
        if n < 2 * SETS:
            order_of_sets.append((2 * (n // SETS), n % SETS))
        if n >= LAG:
            order_of_sets.append((2 * ((n - LAG) // SETS) + 1, (n - LAG) % SETS))
    before = lambda c, n: SETS * (c // 2) + n
    with memory(k, d_own=(9, SEQ), d_r=(2, 256), d_u=(2, 256), d_z=(2, 64)) as (own, rr_all, uu_all, z), \
            stage(k, "even_products", "odd_products", "even_evacuated", "odd_evacuated", "vector_order") as (
                block, even_products, odd_products, even_evacuated, odd_evacuated, order):
        tiles = free + [own[:, 0, :]]
        lanes = []
        for lane in range(2):
            ed, el, md, nt, bi, ki, s1, s2 = (four(x) for x in tiles[8 * lane:8 * lane + 8])
            pq, pq2 = (own[:, 1 + 4 * lane + 2 * j:3 + 4 * lane + 2 * j, :].rearrange(
                "p a n -> p (a n)").rearrange("p (h t) -> p h t", h=4) for j in range(2))
            lanes.append(dict(ed=ed, el=el, md=md, nt=nt, bi=bi, ki=ki, s1=s1, s2=s2, s3=el, s4=md, s5=ed, pq=pq,
                              pq2=pq2, x=pq2[:, :, 0:128], q=pq2[:, :, 128:256], rr=rr_all[:, lane, :],
                              uu=uu_all[:, lane, :], bank=k.bank[4 * lane:4 * lane + 4]))
        products_done = (even_products, odd_products)
        evacuated = (even_evacuated, odd_evacuated)

        @block.tensor
        def _(pe):
            def by_head(out, left, right):
                for h in range(4):
                    last = pe.matmul(out[:, quarter[h]], left[:, h, :], right[:, h, :], start=True, stop=True)
                return last

            def by_head_wide(outs, left, right):
                for h in range(4):
                    last = pe.matmul(outs[h // 2][:, 256 * (h % 2):256 * (h % 2) + 256], left[:, h, :],
                                     right[:, h, :], start=True, stop=True)
                return last

            for c, n in order_of_sets:
                ln = lanes[c % 2]
                bank, cols = ln["bank"], quarter[c]
                if before(c, n):
                    pe.wait_ge(evacuated[c % 2], before(c, n))
                if n == 0:
                    for h in range(4):
                        p, r = h // 2, rows[h]
                        for m, left in enumerate((bt[p], kt[:, p, :])):
                            b = bank[2 * m + h % 2]
                            pe.matmul(b[:, 256 * p:256 * p + 128], left[r, cols], at[p][r, cols], start=True,
                                      stop=True)
                            last = pe.matmul(b[:, 256 * p + 128:256 * p + 256], left[r, cols], rt[r, p, cols],
                                             start=True, stop=True)
                elif n == 1:
                    for h in range(4):
                        p, r = h // 2, rows[h]
                        last = pe.matmul(bank[h % 2][:, 128 * p:128 * p + 128], at[p][r, cols], bt[p][r, cols],
                                         start=True, stop=True)
                elif n == 2:
                    by_head(bank[0], ln["md"], ln["el"])
                    by_head(bank[1], ln["md"], ln["ed"])
                    last = by_head(bank[2], ln["ed"], ln["md"])
                elif n == 3:
                    by_head(bank[0], ln["s2"], ln["s1"])
                    by_head(bank[1], ln["s1"], ln["s2"])
                    last = by_head_wide(bank[2:4], ln["s2"], ln["pq"])
                elif n == 4:
                    by_head(bank[1], ln["s3"], ln["s4"])
                    last = by_head_wide(bank[2:4], ln["s4"], ln["pq2"])
                elif n == 5:
                    last = by_head_wide(bank[2:4], ln["s2"], ln["pq"])
                elif n == 6:
                    for h in range(4):
                        last = pe.transpose(bank[0][:, quarter[h]], ln["pq2"][:, h, 128:256], const(k, "ident"))
                elif n == 7:
                    by_head(bank[1], ln["s5"], ln["q"])
                    last = by_head(bank[2], ln["q"], ln["s5"])
                elif n == 8:
                    last = by_head(bank[1], ln["s1"], ln["s2"])
                elif n <= 11:
                    last = by_head(bank[0], ln[("s3", "s2", "s5")[n - 9]], ln["x"])
                elif n == 12:
                    if c:
                        pe.wait_ge(evacuated[(c - 1) % 2], before(c - 1, SETS))
                    for h in range(4):
                        p, r = h // 2, rows[h]
                        o = bank[1 + h % 2][:, 64 * p:64 * p + 64]
                        if c:
                            pe.matmul(o, at[p][r, cols], z[r, p, :], start=True, stop=False)
                        last = pe.matmul(o, ln["nt"][:, h, :], vt[:, c, 64 * h:64 * h + 64], start=not c, stop=True)
                elif n == 13:
                    for h in range(4):
                        hs = slice(64 * h, 64 * h + 64)
                        last = pe.matmul(bank[3][:, hs], ln["x"][:, h, :], ln["rr"][:, hs], start=True, stop=True)
                else:
                    for h in range(4):
                        p, r = h // 2, rows[h]
                        us, vs = ln["uu"][:, 64 * h:64 * h + 64], vt[:, c, 64 * h:64 * h + 64]
                        if c < 3:
                            o = bank[2][r, 64 * p:64 * p + 64]
                            pe.matmul(o, btt[:, c, 64 * h:64 * h + 64], us, start=True, stop=False)
                            pe.matmul(o, ktt[:, c, 64 * h:64 * h + 64], vs, start=False, stop=True)
                        o = bank[h % 2][r, 128 * p:128 * p + 128]
                        if c:
                            pe.matmul(o, z[r, p, :], rt[r, p, cols], start=True, stop=False)
                        pe.matmul(o, us, ln["bi"][:, h, :], start=not c, stop=False)
                        last = pe.matmul(o, vs, ln["ki"][:, h, :], start=False, stop=True)
                last.then_inc(products_done[c % 2], 1)

        @block.vector
        def _(dve):
            step = Order(dve, order)

            def grow(dst, src, banks):
                for p in range(2):
                    a = slice(2 * p, 2 * p + 2)
                    last = dve.tensor_tensor(dst[:, a, :], src[:, a, :],
                                             banks[p][:, :].rearrange("p (h t) -> p h t", h=2), ALU.add)
                    if p == 0:
                        step(last)
                return last

            for c, n in order_of_sets:
                ln = lanes[c % 2]
                bank = ln["bank"]
                dve.wait_ge(products_done[c % 2], before(c, n) + 1)
                if n == 0:
                    for p in range(2):
                        b = bank[p][:, :].rearrange("p (h g t) -> p h g t", h=2, g=2)
                        m = bank[2 + p][:, :].rearrange("p (h g t) -> p h g t", h=2, g=2)
                        hs = slice(p, 4, 2)
                        step(dve.tensor_tensor(ln["ed"][:, hs, :], b[:, :, 0, :], wide("up_same", 2), ALU.mult))
                        step(dve.tensor_tensor(ln["el"][:, hs, :], b[:, :, 0, :], wide("up_other", 2), ALU.mult))
                        step(dve.tensor_tensor(ln["bi"][:, hs, :], b[:, :, 1, :], wide("up_diag", 2), ALU.mult))
                        step(dve.tensor_tensor(ln["nt"][:, hs, :], m[:, :, 0, :], wide("up", 2), ALU.mult))
                        step(dve.tensor_tensor(ln["ki"][:, hs, :], m[:, :, 1, :], wide("up_diag", 2), ALU.mult))
                    last = dve.tensor_tensor(ln["pq"][:, :, 0:128], ln["ed"][:, :, :], wide("ident", 4), ALU.add)
                elif n == 1:
                    for p in range(2):
                        last = dve.tensor_tensor(ln["md"][:, p:4:2, :],
                                                 bank[p][:, 0:256].rearrange("p (h t) -> p h t", h=2),
                                                 wide("low_same", 2), ALU.mult)
                        if p == 0:
                            step(last)
                elif n == 2:
                    step(dve.tensor_tensor(ln["pq"][:, :, 128:256], ln["el"][:, :, :], four(bank[0][:, :]), ALU.add))
                    step(dve.tensor_copy(ln["s1"][:, :, :], four(bank[1][:, :])))
                    last = dve.tensor_copy(ln["s2"][:, :, :], four(bank[2][:, :]))
                elif n == 3:
                    step(dve.tensor_copy(ln["s3"][:, :, :], four(bank[0][:, :])))
                    step(dve.tensor_copy(ln["s4"][:, :, :], four(bank[1][:, :])))
                    last = grow(ln["pq2"], ln["pq"], bank[2:4])
                elif n == 4:
                    step(dve.tensor_copy(ln["s2"][:, :, :], four(bank[1][:, :])))
                    last = grow(ln["pq"], ln["pq2"], bank[2:4])
                elif n == 5:
                    last = grow(ln["pq2"], ln["pq"], bank[2:4])
                elif n == 6:
                    last = dve.tensor_copy(ln["s5"][:, :, :], four(bank[0][:, :]))
                elif n == 7:
                    step(dve.tensor_copy(ln["s1"][:, :, :], four(bank[1][:, :])))
                    last = dve.tensor_copy(ln["s2"][:, :, :], four(bank[2][:, :]))
                elif n == 8:
                    last = dve.tensor_copy(ln["s3"][:, :, :], four(bank[1][:, :]))
                elif n <= 11:
                    last = dve.tensor_tensor(ln["x"], ln["x"], four(bank[0][:, :]), ALU.add)
                elif n == 12:
                    for p in range(2):
                        last = dve.tensor_copy(ln["rr"].rearrange("p (h v) -> p h v", h=4)[:, p:4:2, :],
                                               bank[1 + p][:, 0:128].rearrange("p (h v) -> p h v", h=2))
                        if p == 0:
                            step(last)
                elif n == 13:
                    last = dve.tensor_copy(ln["uu"], bank[3][:, 0:256])
                else:
                    for p in range(2):
                        r = rows[p]
                        last = dve.tensor_copy(k.yb[r, 6:8, quarter[c]],
                                               bank[p][r, 0:256].rearrange("p (a t) -> p a t", a=2))
                        if p == 0:
                            step(last)
                    if c < 3:
                        step(last)
                        b = bank[2][:, 0:128].rearrange("p (a t) -> p a t", a=2)
                        if c:
                            step(dve.tensor_tensor(z[:, :, :], z[:, :, :], b, ALU.add))
                        else:
                            step(dve.tensor_copy(z[:, :, :], b))
                        step(dve.tensor_scalar(z[:, 0, :], z[:, 0, :], zs[:, 0, c:c + 1], None, ALU.mult))
                        last = dve.tensor_scalar(z[:, 1, :], z[:, 1, :], zs[:, 1, c:c + 1], None, ALU.mult)
                last.then_inc(evacuated[c % 2], 1)




def route(k, hot, hot2, gates, norm):
    ws = k.ws
    ws.plan(8)
    bias = k.mats1[:, 512:548]
    four = lambda name: const(k, name).rearrange("p (q e) -> p q e", q=4)
    with memory(k, lg=(4, 128), pick=(4, 4), m=(4, 8), le=(4, 32), wide=(4, 32)) as (lg, pick, m, le, wide), \
            stage(k, "logits_ready", "exp_ready", "best_ready", "gates_ready", "vector_order", *norm[0]) as (
                block, logits_ready, exp_ready, best_ready, gates_ready, order, *norm_sems):
        norm = norm[1]
        bc = lambda ap, n: ap.to_broadcast([128, 4, n])

        @block.sync
        def _(sp):
            ws.load(sp)

        @block.gpsimd
        def _(pool):
            ws.divide(pool)

        @block.tensor
        def _(pe):
            norm["tensor_start"](pe, *norm_sems)
            for t in range(KT):
                norm["tensor"](pe, t, *norm_sems)
                still = [(k.xh[:, t, 128 * q:128 * q + 128], k.xl[:, t, 128 * q:128 * q + 128]) for q in range(4)]
                last = ws.product_tm(pe, [k.bank[q][:, 0:128] for q in range(4)], still, 1, t == 0, t == KT - 1)
            last.then_inc(logits_ready, 1)

        @block.scalar
        def _(act):
            norm["scalar"](act, *norm_sems)
            act.wait_ge(best_ready, 1)
            act.activation(m[:, :, 4:8], lg[:, :, 0:4], ACT.Exp).then_inc(exp_ready, 1)
            act.wait_ge(best_ready, 2)
            act.activation(m[:, :, 3:4], m[:, :, 3:4], ACT.Exp).then_inc(exp_ready, 1)

        @block.vector
        def _(dve):
            norm["vector"](dve, *norm_sems)
            step = Order(dve, order)
            dve.wait_ge(logits_ready, 1)
            for q in range(4):
                step(dve.tensor_tensor(lg[:, q, 0:36], k.bank[q][:, 0:36], bias, ALU.add))
            step(dve.tensor_reduce(m[:, :, 0:1], lg[:, :, 0:4], AX.X, ALU.max))
            step(dve.tensor_tensor(pick[:, :, :], lg[:, :, 0:4], bc(m[:, :, 0:1], 4), ALU.is_equal))
            dve.tensor_tensor(lg[:, :, 0:4], lg[:, :, 0:4], bc(m[:, :, 0:1], 4), ALU.subtract).then_inc(best_ready, 1)
            step(dve.tensor_tensor(pick[:, :, :], pick[:, :, :], four("rank8")[:, :, 0:4], ALU.mult))
            step(dve.tensor_reduce(m[:, :, 1:2], pick[:, :, :], AX.X, ALU.max))
            step(dve.tensor_tensor(pick[:, :, :], pick[:, :, :], bc(m[:, :, 1:2], 4), ALU.is_equal))
            dve.wait_ge(exp_ready, 1)
            step(dve.tensor_reduce(m[:, :, 2:3], m[:, :, 4:8], AX.X, ALU.add))
            step(dve.reciprocal(m[:, :, 2:3], m[:, :, 2:3]))
            spread = pick[:, :, :].rearrange("p q (g a) -> p (q g) a", a=1).to_broadcast([128, 16, 8])
            groups = lambda ap: ap.rearrange("p q (g e) -> p (q g) e", e=8)
            step(dve.tensor_copy(groups(wide[:, :, :]), spread))
            step(dve.tensor_tensor(le[:, :, :], lg[:, :, 4:36], wide[:, :, :], ALU.mult))
            step(dve.tensor_scalar(wide[:, :, :], wide[:, :, :], 1.0, -MASKED, ALU.subtract, ALU.mult))
            step(dve.tensor_tensor(le[:, :, :], le[:, :, :], wide[:, :, :], ALU.add))
            for hots, at in ((hot, 0), (hot2, 1)):
                step(dve.tensor_reduce(m[:, :, at:at + 1], le[:, :, :], AX.X, ALU.max))
                step(dve.tensor_tensor(hots[:, :, :], le[:, :, :], bc(m[:, :, at:at + 1], 32), ALU.is_equal))
                step(dve.tensor_tensor(hots[:, :, :], hots[:, :, :],
                                       const(k, "rank8").rearrange("p (a e) -> p a e", a=1).to_broadcast([128, 4, 32]),
                                       ALU.mult))
                step(dve.tensor_reduce(m[:, :, 4:5], hots[:, :, :], AX.X, ALU.max))
                step(dve.tensor_tensor(hots[:, :, :], hots[:, :, :], bc(m[:, :, 4:5], 32), ALU.is_equal))
                if at == 0:
                    step(dve.scalar_tensor_tensor(le[:, :, :], hots[:, :, :], 2 * MASKED, le[:, :, :], ALU.mult,
                                                  ALU.add))
            dve.tensor_tensor(m[:, :, 3:4], m[:, :, 1:2], m[:, :, 0:1], ALU.subtract).then_inc(best_ready, 1)
            dve.wait_ge(exp_ready, 2)
            step(dve.tensor_scalar(m[:, :, 5:6], m[:, :, 3:4], 1.0, None, ALU.add))
            step(dve.reciprocal(m[:, :, 5:6], m[:, :, 5:6]))
            step(dve.tensor_tensor(gates[:, 0, :], m[:, :, 5], m[:, :, 2], ALU.mult))
            dve.tensor_tensor(gates[:, 1, :], gates[:, 0, :], m[:, :, 3], ALU.mult).then_inc(gates_ready, 1)


def dispatch(k, hots, gates, block_expert, pos, pos_rows, gate_rows):
    ones, up = const(k, "ones"), const(k, "up")
    n_blocks = block_expert.shape[-1]
    with memory(k, mask=(4, 32), rank=(4, 32), per=(4, 32), cmp=(n_blocks, 32), ended=(2, n_blocks),
                diag=(2, 128)) as (mask, rank, per, cmp, ended, diag), \
            stage(k, "mask_ready", "ranks_ready", "diag_ready", "spread_ready", "spread_copied", "vector_order") as (
                block, mask_ready, ranks_ready, diag_ready, spread_ready, spread_copied, order):
        @block.tensor
        def _(pe):
            pe.wait_ge(mask_ready, 1)
            for q in range(4):
                for r in range(q):
                    pe.matmul(k.bank[0][:, 32 * q:32 * q + 32], ones, mask[:, r, :], start=r == 0, stop=False)
                pe.matmul(k.bank[0][:, 32 * q:32 * q + 32], up, mask[:, q, :], start=q == 0, stop=True)
            for q in range(4):
                last = pe.matmul(k.bank[1][:, 0:32], ones, mask[:, q, :], start=q == 0, stop=q == 3)
            last.then_inc(ranks_ready, 1)
            for n in range(16):
                pe.wait_ge(diag_ready, n + 1)
                pe.matmul(k.bank[2 + n // 4][:, 128 * (n % 4):128 * (n % 4) + 128], ones, diag[:, n % 2, :],
                          start=True, stop=True).then_inc(spread_ready, 1)

        @block.vector
        def _(dve):
            step = Order(dve, order)
            dve.tensor_tensor(mask[:, :, :], hots[0], hots[1], ALU.add).then_inc(mask_ready, 1)
            dve.wait_ge(ranks_ready, 1)
            count, blocks, upto, start = (per[:, j, :] for j in range(4))
            step(dve.tensor_copy(rank[:, :, :], k.bank[0][:, 0:128].rearrange("p (q e) -> p q e", q=4)))
            step(dve.tensor_copy(count, k.bank[1][:, 0:32]))
            step(dve.tensor_scalar(blocks, count, 0.0, None, ALU.is_gt))
            for j in range(1, SEQ // ROWS):
                step(dve.scalar_tensor_tensor(blocks, count, float(ROWS * j), blocks, ALU.is_gt, ALU.add))
            step(dve.tensor_tensor_scan(upto, ones[:, 0:32], blocks, 0.0, ALU.mult, ALU.add))
            step(dve.tensor_tensor(start, upto, blocks, ALU.subtract))
            ends = upto.rearrange("p (b e) -> p b e", b=1).to_broadcast([128, n_blocks, 32])
            numbers = const(k, "count")[:, 0:n_blocks].rearrange("p (b e) -> p b e", e=1).to_broadcast(
                [128, n_blocks, 32])
            step(dve.tensor_tensor(cmp[:, :, :], ends, numbers, ALU.is_le))
            step(dve.tensor_reduce(ended[:, 0, :], cmp[:, :, :], AX.X, ALU.add))
            step(dve.tensor_scalar(ended[:, 1, :], ended[:, 0, :], EXPERTS - 1.0, None, ALU.min))
            step(dve.tensor_copy(block_expert, ended[:, 1, :]))
            first = start.rearrange("p (q e) -> p q e", q=1).to_broadcast([128, 4, 32])
            step(dve.scalar_tensor_tensor(rank[:, :, :], first, float(ROWS), rank[:, :, :], ALU.mult, ALU.add))
            for pick in range(2):
                step(dve.tensor_tensor(hots[pick], hots[pick], rank[:, :, :], ALU.mult))
                step(dve.tensor_reduce(pos[:, pick, :], hots[pick], AX.X, ALU.add))
            columns = [pos[:, 0, :], pos[:, 1, :], gates[:, 0, :], gates[:, 1, :]]
            rows = [pos_rows[:, 0, :], pos_rows[:, 1, :], gate_rows[:, 0, :], gate_rows[:, 1, :]]
            for n in range(16):
                if n >= 2:
                    dve.wait_ge(spread_ready, n - 1)
                dve.tensor_scalar(diag[:, n % 2, :], const(k, "ident"), columns[n // 4][:, n % 4:n % 4 + 1], None,
                                  ALU.mult).then_inc(diag_ready, 1)
            for j in range(4):
                dve.wait_ge(spread_ready, 4 * j + 4)
                dve.tensor_copy(rows[j], k.bank[2 + j][:, :]).then_inc(spread_copied, 1)
    xh, xl = token_major(k)
    with stage(k, "turned", "rounded", "split") as (block, turned, rounded, split):
        @block.tensor
        def _(pe):
            for n in range(8):
                if n >= 4:
                    pe.wait_ge(split, n - 3)
                for t in range(4):
                    last = pe.transpose(k.bank[n % 4][:, 128 * t:128 * t + 128],
                                        k.res[:, 4 * (n % 2) + t, 128 * (n // 2):128 * (n // 2) + 128],
                                        const(k, "ident"))
                last.then_inc(turned, 1)

        @block.scalar
        def _(act):
            for n in range(8):
                act.wait_ge(turned, n + 1)
                act.activation(xh[:, n // 2, 512 * (n % 2):512 * (n % 2) + 512], k.bank[n % 4][:, :],
                               ACT.Copy).then_inc(rounded, 1)

        @block.vector
        def _(dve):
            for n in range(8):
                c = slice(512 * (n % 2), 512 * (n % 2) + 512)
                dve.wait_ge(rounded, n + 1)
                dve.tensor_tensor(xl[:, n // 2, c], k.bank[n % 4][:, :], xh[:, n // 2, c].bitcast(F32),
                                  ALU.subtract).then_inc(split, 1)


def token_major(k):
    return [x[:, :, :].rearrange("p (q a) n -> p q (a n)", a=2) for x in (k.xh, k.xl)]


SHARED = (3,)


def experts(k, block_expert, pos, pos_rows, gate_rows):
    ws = k.ws
    c0 = ws.blocks // 16
    assert ws.blocks % 16 == 0 and ws.n_loaded == c0 and ws.n_split == c0
    xh, xl = token_major(k)
    with memory(k, raw2=(CHUNK,), hi2=("r", CHUNK), lo2=("r", CHUNK), pick=("r", 4, 256), spread=("r", 2, SEQ),
                gh=("r", KT, 256), gl=("r", KT, 256), silu=(2, 256), mid=(2, 256), hh=("r", 2, 256),
                hl=("r", 2, 256), yh=("r", 2, D), yl=("r", 2, D), junk=(SEQ,), gate_row=(2, 4), row=(2,), both_done=(1,)) as (
            raw2, hi2, lo2, pick, spread, gh, gl, silu, mid, hh, hl, yh, yl, junk, gate_row, row,
            both_done), \
            stage(k, "m_loaded0", "m_loaded1", "m_loaded2", "m_rounded", "m_split", "m_half", "m_shared", "m_used", "picks_ready",
                  "spread_ready", "gathered", "rows_rounded", "rows_split", "hidden_ready", "silu_ready", "mixed",
                  "turned", "turned_rounded", "turned_split", "y_ready", "y_rounded", "y_split", "scattered", "added",
                  "vector_order") as (
                block, m_loaded0, m_loaded1, m_loaded2, m_rounded, m_split, m_half, m_shared, m_used, picks_ready, spread_ready,
                gathered, rows_rounded, rows_split, hidden_ready, silu_ready, mixed, turned, turned_rounded,
                turned_split, y_ready, y_rounded, y_split, scattered, added, order):
        raw = [ws.raw[:, 0, :], ws.raw[:, 1, :], raw2[:, :]]
        hi = [ws.hi[:, 0, :], ws.hi[:, 1, :], hi2[:, :]]
        lo = [ws.lo[:, 0, :], ws.lo[:, 1, :], lo2[:, :]]
        loaded = [m_loaded0, m_loaded1, m_loaded2]
        parts = [(0, 0), (0, 1), (1, 0), (1, 1), (0, 2), (1, 2)]
        halves = [slice(0, 512), slice(512, 1024)]

        @block.sync
        def _(sp):
            def load(c, expert):
                sp.dma_start(raw[c % 3], ws.dram[expert * MOE_CHUNKS + (c0 + parts[c % 6][1]), :, :]).then_inc(
                    loaded[c % 3], 16)

            first = [sp.value_load(block_expert[0:1, b:b + 1], min_val=0, max_val=EXPERTS - 1) for b in range(2)]
            for c in range(3):
                load(c, first[parts[c][0]])
            with sp.Fori(0, TURNS) as i:
                here, ahead = ([sp.value_load(block_expert[0:1, bass.ds(2 * i + n + b, 1)], min_val=0,
                                              max_val=EXPERTS - 1) for b in range(2)] for n in (0, 2))
                for c in range(3, 9):
                    sp.wait_ge(m_split, 6 * i + (c - 2))
                    load(c, (here if c < 6 else ahead)[parts[c % 6][0]])
            sp.wait_ge(m_split, 6 * TURNS + 3)

        def rounds(act, c, turn=0):
            act.wait_ge(loaded[c % 3], 32 * turn + 16 * (c // 3 + 1))
            if c >= 3:
                act.wait_ge(m_used, 6 * turn + (c - 2))
            act.activation(hi[c % 3], raw[c % 3], ACT.Copy).then_inc(m_rounded, 1)

        @block.gpsimd
        def _(pool):
            def rest(c, turn=0):
                pool.wait_ge(m_rounded, 6 * turn + (c + 1))
                if c not in SHARED:
                    pool.tensor_tensor(lo[c % 3], raw[c % 3], hi[c % 3].bitcast(F32), ALU.subtract).then_inc(
                        m_split, 1)
                    return
                s = slice(0, CHUNK // 2)
                shared = len(SHARED) * turn + (SHARED.index(c) + 1)
                pool.tensor_tensor(lo[c % 3][:, s], raw[c % 3][:, s], hi[c % 3][:, s].bitcast(F32),
                                   ALU.subtract).then_inc(m_half, 1)
                pool.wait_ge(m_half, shared)
                pool.wait_ge(m_shared, shared)
                pool.tensor_tensor(both_done[:, :], ws.zero[:, :], ws.zero[:, :], ALU.add).then_inc(m_split, 1)

            for c in range(3):
                rest(c)
            with pool.Fori(0, TURNS) as i:
                for c in range(3, 9):
                    rest(c, i)

        @block.tensor
        def _(pe):
            with pe.Fori(0, TURNS) as i:
                def gate_up(b, first, last):
                    for t in range(first, last):
                        c = 2 * b + t // 4
                        if t % 4 == 0:
                            pe.wait_ge(m_split, 6 * i + (c + 1))
                        if b == 0 and t % 2 == 0:
                            pe.wait_ge(rows_split, 4 * i + (t // 2 + 1))
                        s, w = slice(128 * b, 128 * b + 128), slice(512 * (t % 4), 512 * (t % 4) + 512)
                        out = k.bank[4 + b][:, :]
                        mm = pe.matmul(out, gh[:, t, s], hi[c % 3][:, w], start=t == 0, stop=False)
                        if t % 4 == 0 and c:
                            mm.then_inc(m_used, 1)
                        pe.matmul(out, gh[:, t, s], lo[c % 3][:, w], start=False, stop=False)
                        mm = pe.matmul(out, gl[:, t, s], hi[c % 3][:, w], start=False, stop=t == KT - 1)
                    if last == KT:
                        mm.then_inc(hidden_ready, 1)

                def turn_hidden(b):
                    pe.wait_ge(mixed, 2 * i + (b + 1))
                    for u in range(2):
                        mm = pe.transpose(k.bank[6 + b][:, 128 * u:128 * u + 128], mid[:, b, 128 * u:128 * u + 128],
                                          const(k, "ident"))
                    mm.then_inc(turned, 1)

                def down(b, half):
                    c = 4 + b
                    if half == 0:
                        pe.wait_ge(m_split, 6 * i + (c + 1))
                        pe.wait_ge(turned_split, 2 * i + (b + 1))
                    out = k.bank[2 * b + half][:, :]
                    for u in range(2):
                        s = slice(128 * u, 128 * u + 128)
                        w = slice(1024 * u + 512 * half, 1024 * u + 512 * half + 512)
                        mm = pe.matmul(out, hh[:, b, s], hi[c % 3][:, w], start=u == 0, stop=False)
                        if half == 0 and u == 0:
                            mm.then_inc(m_used, 1)
                        pe.matmul(out, hh[:, b, s], lo[c % 3][:, w], start=False, stop=False)
                        mm = pe.matmul(out, hl[:, b, s], hi[c % 3][:, w], start=False, stop=u == 1)
                    mm.then_inc(y_ready, 1)

                pe.wait_ge(picks_ready, i + 1)
                for t in range(KT):
                    out = k.bank[t // 2][:, 256 * (t % 2):256 * (t % 2) + 256]
                    for q in range(4):
                        for x in (xh, xl):
                            mm = pe.matmul(out, x[:, q, 128 * t:128 * t + 128], pick[:, q, :],
                                           start=q == 0 and x is xh, stop=q == 3 and x is xl)
                    if t % 2:
                        mm.then_inc(gathered, 1)
                pe.wait_ge(added, 8 * i + 1)
                gate_up(0, 0, KT)
                gate_up(1, 0, KT // 2)
                turn_hidden(0)
                gate_up(1, KT // 2, KT)
                down(0, 0)
                turn_hidden(1)
                down(0, 1)
                down(1, 0)
                down(1, 1)
                pe.wait_ge(spread_ready, 2 * i + 2)
                for g in range(2):
                    for b in range(2):
                        if g == 0:
                            pe.wait_ge(y_split, 4 * i + (2 * b + 2))
                        for t in range(4 * g, 4 * g + 4):
                            if g == 1 and b == 0:
                                pe.wait_ge(added, 8 * i + (t - 2))
                            for y in (yh, yl):
                                mm = pe.matmul(k.bank[4 + t % 4][:, :], y[:, b, 128 * t:128 * t + 128],
                                               spread[:, b, :], start=b == 0 and y is yh, stop=b == 1 and y is yl)
                                if t == 0 and b == 0 and y is yh:
                                    mm.then_inc(m_used, 1)
                            if b == 1:
                                mm.then_inc(scattered, 1)

        @block.scalar
        def _(act):
            for c in range(3):
                rounds(act, c)
            with act.Fori(0, TURNS) as i:
                def silus(b):
                    act.wait_ge(hidden_ready, 2 * i + (b + 1))
                    act.activation(silu[:, b, :], k.bank[4 + b][:, 0:256], ACT.Silu).then_inc(silu_ready, 1)

                def round_hidden(b):
                    act.wait_ge(turned, 2 * i + (b + 1))
                    act.activation(hh[:, b, :], k.bank[6 + b][:, 0:256], ACT.Copy).then_inc(turned_rounded, 1)

                def round_y(b, half):
                    act.wait_ge(y_ready, 4 * i + (2 * b + half + 1))
                    act.activation(yh[:, b, halves[half]], k.bank[2 * b + half][:, :], ACT.Copy).then_inc(
                        y_rounded, 1)

                for g in range(4):
                    act.wait_ge(gathered, 4 * i + (g + 1))
                    act.activation(gh[:, 2 * g:2 * g + 2, :].rearrange("p a n -> p (a n)"), k.bank[g][:, :],
                                   ACT.Copy).then_inc(rows_rounded, 1)
                rounds(act, 3, i)
                silus(0)
                rounds(act, 4, i)
                round_hidden(0)
                rounds(act, 5, i)
                silus(1)
                round_y(0, 0)
                round_hidden(1)
                round_y(0, 1)
                rounds(act, 6, i)
                round_y(1, 0)
                round_y(1, 1)
                rounds(act, 7, i)
                rounds(act, 8, i)

        @block.vector
        def _(dve):
            numbers = const(k, "count")

            def choose_first(q):
                return dve.tensor_scalar(pick[:, q, :], numbers, pos[:, 0, q:q + 1], None, ALU.is_equal)

            def choose_second(q):
                return dve.scalar_tensor_tensor(pick[:, q, :], numbers, pos[:, 1, q:q + 1],
                                                pick[:, q, :].bitcast(F32), ALU.is_equal, ALU.add)

            dve.memset(junk[:, 0:1], 0.0).then_inc(added, 1)
            dve.tensor_copy(row[:, :], const(k, "row")).then_inc(order, 1)
            dve.wait_ge(added, 1)
            for q in range(4):
                choose_first(q).then_inc(order, 1)
            dve.wait_ge(order, 5)
            for q in range(4):
                last = choose_second(q)
            last.then_inc(picks_ready, 1)
            STEPS = 18
            with dve.Fori(0, TURNS) as i:
                n = [5]

                def step(instruction):
                    instruction.then_inc(order, 1)
                    n[0] += 1
                    dve.wait_ge(order, STEPS * i + n[0])

                def mix(b):
                    dve.wait_ge(silu_ready, 2 * i + (b + 1))
                    dve.scalar_tensor_tensor(mid[:, b, :], k.bank[4 + b][:, 256:512], gate_row[:, b, 2:3],
                                             silu[:, b, :], ALU.mult, ALU.mult).then_inc(mixed, 1)

                def share(c):
                    s = slice(CHUNK // 2, CHUNK)
                    dve.wait_ge(m_rounded, 6 * i + (c + 1))
                    dve.tensor_tensor(lo[c % 3][:, s], raw[c % 3][:, s], hi[c % 3][:, s].bitcast(F32),
                                      ALU.subtract).then_inc(m_shared, 1)

                def split_hidden(b):
                    dve.wait_ge(turned_rounded, 2 * i + (b + 1))
                    dve.tensor_tensor(hl[:, b, :], k.bank[6 + b][:, 0:256], hh[:, b, :].bitcast(F32),
                                      ALU.subtract).then_inc(turned_split, 1)

                def split_y(b, half):
                    dve.wait_ge(y_rounded, 4 * i + (2 * b + half + 1))
                    dve.tensor_tensor(yl[:, b, halves[half]], k.bank[2 * b + half][:, :],
                                      yh[:, b, halves[half]].bitcast(F32), ALU.subtract).then_inc(y_split, 1)

                for g in range(4):
                    dve.wait_ge(rows_rounded, 4 * i + (g + 1))
                    rows = slice(2 * g, 2 * g + 2)
                    dve.tensor_tensor(gl[:, rows, :].rearrange("p a n -> p (a n)"), k.bank[g][:, :],
                                      gh[:, rows, :].rearrange("p a n -> p (a n)").bitcast(F32),
                                      ALU.subtract).then_inc(rows_split, 1)
                def spread_rows(b):
                    s = spread[:, b, :]
                    step(dve.tensor_scalar(s, pos_rows[:, 0, :], row[:, b:b + 1], None, ALU.is_equal))
                    step(dve.tensor_tensor(junk[:, :], s.bitcast(F32), gate_rows[:, 0, :], ALU.mult))
                    step(dve.tensor_reduce(gate_row[:, b, 0:1], junk[:, :], AX.X, ALU.add))
                    step(dve.scalar_tensor_tensor(junk[:, :], pos_rows[:, 1, :], row[:, b:b + 1], gate_rows[:, 1, :],
                                                  ALU.is_equal, ALU.mult))
                    step(dve.tensor_reduce(gate_row[:, b, 1:2], junk[:, :], AX.X, ALU.add))
                    step(dve.tensor_tensor(gate_row[:, b, 2:3], gate_row[:, b, 0:1], gate_row[:, b, 1:2], ALU.add))
                    dve.scalar_tensor_tensor(s, pos_rows[:, 1, :], row[:, b:b + 1], s.bitcast(F32), ALU.is_equal,
                                             ALU.add).then_inc(spread_ready, 1)

                spread_rows(0)
                share(3)
                mix(0)
                spread_rows(1)
                split_hidden(0)
                mix(1)
                step(dve.tensor_scalar(pos[:, :, :], pos[:, :, :], 2.0 * ROWS, None, ALU.subtract))
                split_y(0, 0)
                split_hidden(1)
                for q in range(4):
                    step(choose_first(q))
                split_y(0, 1)
                choose_second(0)
                choose_second(1)
                split_y(1, 0)
                choose_second(2)
                choose_second(3).then_inc(picks_ready, 1)
                split_y(1, 1)
                dve.wait_ge(spread_ready, 2 * i + 2)
                step(dve.tensor_scalar(row[:, :], row[:, :], 2.0 * ROWS, None, ALU.add))
                for t in range(KT):
                    dve.wait_ge(scattered, 8 * i + (t + 1))
                    dve.tensor_tensor(k.res[:, t, :], k.res[:, t, :], k.bank[4 + t % 4][:, :], ALU.add).then_inc(
                        added, 1)
                assert n[0] == 5 + STEPS




def retention(k, pj, rv):
    par = lambda n, j=0: k.par2[:, P2[n] + j:P2[n] + j + 1]
    rotate = const(k, "rotate")
    with memory(k, decays=(4, STRIP)) as decays:
        with memory(k, tabs=(2 * SEQ + 2 * STRIP,), rot_t=(SEQ,), lgam=(3, 8)) as (tabs, tmp, lgam):
            cos, sin = tabs[:, 0:SEQ], tabs[:, SEQ:2 * SEQ]
            ahead, behind = tabs[:, 2 * SEQ:2 * SEQ + STRIP], tabs[:, 2 * SEQ + STRIP:2 * SEQ + 2 * STRIP]
            with stage(k, "tables_in", "rotated", "rotated_read", "abs_ready", "exp_ready", "log_ready", "powers_ready",
                       "strips_ready", "vector_order") as (block, tables_in, rotated, rotated_read, abs_ready, exp_ready,
                                                           log_ready, powers_ready, strips_ready, order):
                @block.sync
                def _(sp):
                    sp.dma_start(tabs[:, :], k.dram["tables"][:, 0:2 * SEQ + 2 * STRIP]).then_inc(tables_in, 16)

                @block.tensor
                def _(pe):
                    for j in range(4):
                        if j >= 2:
                            pe.wait_ge(rotated_read, j - 1)
                        pe.matmul(k.bank[j % 2][:, :], rotate, pj[:, T2["rq"] + j, :], start=True, stop=True).then_inc(
                            rotated, 1)

                @block.scalar
                def _(act):
                    act.wait_ge(abs_ready, 1)
                    act.activation(lgam[:, 1, :], lgam[:, 1, :], ACT.Exp, scale=-1.0).then_inc(exp_ready, 1)
                    act.wait_ge(exp_ready, 1)
                    act.activation(lgam[:, 1, :], lgam[:, 1, :], ACT.Ln, bias=k.eps[:, 3:4]).then_inc(log_ready, 1)
                    for h in range(4):
                        act.wait_ge(powers_ready, h + 1)
                        act.activation(decays[:, h, :], decays[:, h, :], ACT.Exp).then_inc(strips_ready, 1)

                @block.vector
                def _(dve):
                    step = Order(dve, order)
                    g = k.par2[:, P2["decay"]:P2["decay"] + 8]
                    step(dve.tensor_scalar(lgam[:, 0, :], g, -1.0, None, ALU.mult))
                    dve.tensor_tensor(lgam[:, 1, :], lgam[:, 0, :], g, ALU.max).then_inc(abs_ready, 1)
                    step(dve.tensor_scalar(lgam[:, 2, :], g, 0.0, None, ALU.min))
                    dve.wait_ge(log_ready, 1)
                    step(dve.tensor_tensor(lgam[:, 2, :], lgam[:, 2, :], lgam[:, 1, :], ALU.subtract))
                    dve.wait_ge(tables_in, 16)
                    for h in range(4):
                        d = decays[:, h, :]
                        step(dve.tensor_scalar(d, behind, lgam[:, 2, 4 + h:5 + h], None, ALU.mult))
                        dve.scalar_tensor_tensor(d, ahead, lgam[:, 2, h:h + 1], d, ALU.mult, ALU.add).then_inc(
                            powers_ready, 1)
                    for j in range(4):
                        z = pj[:, T2["rq"] + j, :]
                        dve.wait_ge(rotated, j + 1)
                        dve.tensor_tensor(tmp[:, :], k.bank[j % 2][:, :], sin, ALU.mult).then_inc(rotated_read, 1)
                        dve.wait_ge(rotated_read, j + 1)
                        step(dve.tensor_tensor(z, z, cos, ALU.mult))
                        step(dve.tensor_tensor(z, z, tmp[:, :], ALU.add))
        with memory(k, wsc=(2, 4, SEQ)) as wsc:
            with stage(k, "scores_ready", "scores_used", "out_ready", "out_copied", "silu_done") as (
                    block, scores_ready, scores_used, out_ready, out_copied, silu_done):
                @block.scalar
                def _(act):
                    for p in range(2):
                        g = pj[:, T2["rg"] + p, :]
                        act.activation(g, g, ACT.Silu).then_inc(silu_done, 1)

                @block.tensor
                def _(pe):
                    for h in range(5):
                        if h < 4:
                            rows = slice(64 * (h % 2), 64 * (h % 2) + 64)
                            for j in range(4):
                                u = 4 * h + j
                                if u >= 4:
                                    pe.wait_ge(scores_used, u - 3)
                                pe.matmul(k.bank[u % 4][:, :], pj[rows, T2["rk"] + h // 2, 128 * j:128 * j + 128],
                                          pj[rows, T2["rq"] + h // 2, :], start=True, stop=True).then_inc(
                                    scores_ready, 1)
                        if h >= 1:
                            g = h - 1
                            rows = slice(64 * (g % 2), 64 * (g % 2) + 64)
                            pe.wait_ge(scores_used, 4 * g + 4)
                            for j in range(4):
                                last = pe.matmul(k.bank[4 + g // 2][rows, :], rv[:, j, 64 * g:64 * g + 64],
                                                 wsc[:, g % 2, j, :], start=j == 0, stop=j == 3)
                            last.then_inc(out_ready, 1)

                @block.vector
                def _(dve):
                    for u in range(16):
                        h, j = divmod(u, 4)
                        if j == 0 and h >= 2:
                            dve.wait_ge(out_ready, h - 1)
                        dve.wait_ge(scores_ready, u + 1)
                        dve.scalar_tensor_tensor(wsc[:, h % 2, j, :], k.bank[u % 4][:, :], 0.125,
                                                 decays[:, h, 384 - 128 * j:384 - 128 * j + SEQ], ALU.mult,
                                                 ALU.mult).then_inc(scores_used, 1)
                    for p in range(2):
                        dve.wait_ge(out_ready, 2 * p + 2)
                        dve.tensor_copy(k.yb[:, p, :], k.bank[4 + p][:, :]).then_inc(out_copied, 1)
    def finish(p):
        y = k.yb[:, p, :]

        def run(dve, step, rstd):
            step(dve.tensor_tensor(y, y, rstd, ALU.mult))
            return dve.scalar_tensor_tensor(y, y, par("ret", p), pj[:, T2["rg"] + p, :], ALU.mult, ALU.mult)
        return run

    head_norm(k, [dict(src=k.yb[:, p, :], scale=1.0 / 64, eps=k.eps[:, 1:2], finish=finish(p)) for p in range(2)])


def pooling(k, pj, loads):
    n = SEQ + 16
    with memory(k, padded=(2, n), sums=(2, n), share=(2, SEQ)) as (padded, sums, share):
        with stage(k, "counts_in", "loads_in", "vector_order") as (block, counts_in, loads_in, order):
            @block.sync
            def _(sp):
                at = 2 * SEQ + 2 * STRIP
                sp.dma_start(share[:, :, :], k.dram["tables"][:, at:at + 2 * SEQ].rearrange(
                    "p (a t) -> p a t", a=2)).then_inc(counts_in, 16)
                for dst, src in loads:
                    sp.dma_start(dst, src).then_inc(loads_in, 16)
                sp.wait_ge(loads_in, 16 * len(loads))

            @block.vector
            def _(dve):
                step = Order(dve, order)
                step(dve.memset(padded[:, :, :], 0.0))
                step(dve.memset(sums[:, :, :], 1.0))
                for p in range(2):
                    step(dve.tensor_copy(padded[:, p, 9:9 + SEQ], pj[:, T2["pv"] + p, :]))
                for p in range(2):
                    step(dve.tensor_tensor_scan(padded[:, p, :], sums[:, p, :], padded[:, p, :], 0.0, ALU.mult,
                                                ALU.add))
                for g in range(4):
                    h = POOL_WINDOWS[g] // 2
                    r, p = slice(64 * (g % 2), 64 * (g % 2) + 64), g // 2
                    step(dve.tensor_tensor(sums[r, p, 0:SEQ], padded[r, p, 8 + h:8 + h + SEQ],
                                           padded[r, p, 8 - h:8 - h + SEQ], ALU.subtract))
                dve.wait_ge(counts_in, 16)
                for p in range(2):
                    step(dve.tensor_tensor(sums[:, p, 0:SEQ], sums[:, p, 0:SEQ], share[:, p, :], ALU.mult))
                    step(dve.tensor_tensor(sums[:, p, 0:SEQ], sums[:, p, 0:SEQ], pj[:, T2["pv"] + p, :],
                                           ALU.subtract))
        small_products(k, [(k.yb[:, 2 + p, :], k.mats2[:, 128 * p:128 * p + 128], sums[:, p, 0:SEQ],
                            k.par2[:, P2["pool"] + p:P2["pool"] + p + 1]) for p in range(2)])


def grid_bias(k, layer, bias_dram, tab, made):
    names = ("rows_in", "bias_ready", "bias_copied", "bias_stored")

    def loads(sp, rows_in, *_):
        sp.dma_start(made[64:96, :], k.dram["na_rows"]).then_inc(rows_in, 16)
        sp.dma_start(tab[64:96, :], k.dram["na_rpb"][layer, :, :]).then_inc(rows_in, 16)

    def scalar(act, rows_in, bias_ready, bias_copied, bias_stored):
        act.wait_ge(bias_copied, 8)
        act.dma_start(bias_dram, made[0:60, :]).then_inc(bias_stored, 16)
        act.wait_ge(bias_stored, 16)

    def tensor(pe, rows_in, bias_ready, bias_copied, bias_stored):
        pe.wait_ge(rows_in, 32)
        for j in range(8):
            if j >= 2:
                pe.wait_ge(bias_copied, j - 1)
            pe.matmul(k.bank[2 + j % 2][0:60, :], tab[64:96, :], made[64:96, 512 * j:512 * j + 512], start=True,
                      stop=True).then_inc(bias_ready, 1)

    def vector(dve, rows_in, bias_ready, bias_copied, bias_stored):
        for j in range(8):
            dve.wait_ge(bias_ready, j + 1)
            dve.tensor_copy(made[0:60, 512 * j:512 * j + 512], k.bank[2 + j % 2][0:60, :]).then_inc(bias_copied, 1)
    return names, dict(loads=loads, scalar=scalar, tensor=tensor, vector=vector)


def grid_bias_loads(bias, bias_dram):
    out = []
    for half in range(2):
        for h in range(4):
            src = bass.AP(tensor=bias_dram.tensor, offset=15 * 4096 * h, ap=[[64, 64], [4096, 15], [1, 64]])
            out.append((bias[64 * half:64 * half + 64, h, half:half + 15, :], src))
    return out


def layer(k, i, bias_dram):
    par = lambda n, j=0: k.par2[:, P2[n] + j:P2[n] + j + 1]
    eps = k.eps[:, 1:2]
    with memory(k, yb=(KT, SEQ)) as k.yb:
        with memory(k, pj2=(T2_TILES, SEQ), rv=(4, 256), nv=(4, 256), mk=(2, 256), mv=(2, 256)) as (
                pj, rv, nv, mk, mv):
            with memory(k, memt=(KT, 256)) as memt:
                with memory(k, tab=(60,), made=(4096,)) as (tab, made), norm_buffers(k) as buffers:
                    norm = norm_programs(k, k.res, lambda t: par("mix", t), None, eps, False, buffers, k.xh, k.xl,
                                         loads=[(k.par2[:, :], k.dram["params2"][i, :, :]),
                                                (k.mats2[:, :], k.dram["mats2"][i, :, :]),
                                                (memt[:, :, :], k.dram["memT"])])
                    project(k, T2_TILES, pj, [(rv, 256), (nv, 256)], first=norm,
                            aside=grid_bias(k, i, bias_dram, tab, made))
                with memory(k, memh=("r", KT, 256), meml=("r", KT, 256)) as (memh, meml), \
                        norm_buffers(k, 256) as buffers:
                    project(k, 2, mk, [(mv, 256)], (memh, meml), 256, first=norm_programs(
                        k, memt, lambda t: par("mem", t), None, eps, False, buffers, memh, meml, n=256))
            jobs = []
            for name, gain in (("nq", "naq"), ("nk", "nak"), ("mq", "memq")):
                for p in range(2):
                    src = pj[:, T2[name] + p, :]
                    jobs.append(dict(src=src, scale=1.0 / 64, eps=eps, finish=gained(src, par(gain))))
            for p in range(2):
                jobs.append(dict(src=mk[:, p, :], scale=1.0 / 64, eps=eps, finish=gained(mk[:, p, :], par("memk"))))
            head_norm(k, jobs)
            retention(k, pj, rv)
            with memory(k, na_bias=(4, 16, 64)) as bias:
                pooling(k, pj, grid_bias_loads(bias, bias_dram))
                units = []
                for h in range(4):
                    rows = slice(64 * (h % 2), 64 * (h % 2) + 64)
                    for q in range(4):
                        cols = slice(128 * q, 128 * q + 128)
                        b = bias[:, h, 7 - 2 * q:15 - 2 * q, :].rearrange("p r c -> p (r c)")
                        units.append(dict(q=pj[rows, T2["nq"] + h // 2, cols], keys=pj[rows, T2["nk"] + h // 2, :],
                                          n=SEQ, scale=0.125, bias=b, select=None, strip=None, rows=rows, cols=cols,
                                          values=[nv[:, j, 64 * h:64 * h + 64] for j in range(4)], pair=h // 2))
                for h in range(4):
                    rows = slice(64 * (h % 2), 64 * (h % 2) + 64)
                    for q in range(4):
                        cols = slice(128 * q, 128 * q + 128)
                        units.append(dict(q=pj[rows, T2["mq"] + h // 2, cols], keys=mk[rows, h // 2, :], n=256,
                                          scale=0.125, bias=None, select=None, strip=None, rows=rows, cols=cols,
                                          values=[mv[:, j, 64 * h:64 * h + 64] for j in range(2)], pair=2 + h // 2))
                attention(k, units, [k.yb[:, 4 + p, :] for p in range(4)])
        merge(k, 1.0)
    feed_forward(k, lambda t: par("ffn", t), eps)


def feed_forward(k, gain, eps):
    ws = k.ws
    nf = FF // 128
    with memory(k, fh=("r", nf, SEQ), fl=("r", nf, SEQ), work=(3, SEQ)) as (fh, fl, work):
        silu, mid = work[:, 0:2, :], work[:, 2:3, :]
        ws.plan(nf * 16)
        buffers = (work[:, 0:2, :], work[:, :, :], k.mats1[:, 0:SEQ], None, None)
        norm_names, norm = norm_programs(k, k.res, gain, None, eps, False, buffers, k.xh, k.xl)
        with stage(k, "act_ready", "lin_ready", "silu_ready", "pair_read", "vector_order", *norm_names) as (
                block, act_ready, lin_ready, silu_ready, pair_read, order, *norm_sems):
            @block.sync
            def _(sp):
                ws.load(sp)

            @block.gpsimd
            def _(pool):
                ws.divide(pool)

            @block.tensor
            def _(pe):
                norm["tensor_start"](pe, *norm_sems)
                for j in range(nf):
                    if j >= 2:
                        pe.wait_ge(pair_read, j - 1)
                    for m, done in ((0, act_ready), (1, lin_ready)):
                        for t in range(KT):
                            if j == 0 and m == 0:
                                norm["tensor"](pe, t, *norm_sems)
                            last = ws.product(pe, k.bank[2 * (j % 2) + m][:, :], (k.xh[:, t, :], k.xl[:, t, :]),
                                              t == 0, t == KT - 1)
                        last.then_inc(done, 1)

            @block.scalar
            def _(act):
                norm["scalar"](act, *norm_sems)
                for j in range(nf):
                    act.wait_ge(act_ready, j + 1)
                    act.activation(silu[:, j % 2, :], k.bank[2 * (j % 2)][:, :], ACT.Silu).then_inc(silu_ready, 1)

            @block.vector
            def _(dve):
                norm["vector"](dve, *norm_sems)
                step = Order(dve, order)
                for j in range(nf):
                    dve.wait_ge(silu_ready, j + 1)
                    dve.wait_ge(lin_ready, j + 1)
                    dve.tensor_tensor(mid[:, 0, :], silu[:, j % 2, :], k.bank[2 * (j % 2) + 1][:, :],
                                      ALU.mult).then_inc(pair_read, 1)
                    dve.wait_ge(pair_read, j + 1)
                    step(dve.tensor_copy(fh[:, j, :], mid[:, 0, :]))
                    step(dve.tensor_tensor(fl[:, j, :], mid[:, 0, :], fh[:, j, :].bitcast(F32), ALU.subtract))
        add_product(k, nf, fh, fl, 1.0)




def scale_residual(k):
    with stage(k, "scaled") as (block, scaled):
        @block.vector
        def _(dve):
            for t in range(KT):
                dve.tensor_scalar(k.res[:, t, :], k.res[:, t, :], ALPHA, None, ALU.mult).then_inc(scaled, 1)


def store_out(k, c0):
    ws = k.ws
    end = c0 + LAYERS * LAYER_CHUNKS
    with stage(k, "stored") as (block, stored):
        @block.sync
        def _(sp):
            sp.dma_start(k.dram["outT"], k.res[:, :, :]).then_inc(stored, 16)
            sp.wait_ge(stored, 16)
            for c in (end + 1, end + 2):
                sp.wait_ge(ws.loaded[c % SLOTS], 16 * (c // SLOTS + 1))


def build(nc, dram):
    with ExitStack() as ctx:
        k = Kernel(nc, dram)
        k.bank = [ctx.enter_context(nc.psum_tensor(f"bank{b}", [128, 512], F32)) for b in range(8)]
        k.ws = Stream(nc, ctx, dram["weights"])
        k.ws.limit = FIRST_CHUNKS
        k.xh, k.xl, k.res, k.consts, k.par1, k.par2, k.mats1, k.mats2, k.eps = ctx.enter_context(memory(
            k, xh=("r", KT, SEQ), xl=("r", KT, SEQ), res=(KT, SEQ), consts=(CONSTS,), par1=(P1_COLS,),
            par2=(P2_COLS,), mats1=(548,), mats2=(256,), eps=(4,)))
        bias_dram = nc.dram_tensor("distance_bias", (8, 128, 1024), F32, kind="Internal").ap()
        grid_dram = nc.dram_tensor("grid_bias", (60, 4096), F32, kind="Internal").ap()
        with memory(k, yb=(KT, SEQ)) as k.yb:
            with memory(k, pj=(T1_TILES, SEQ), av=(4, 256), cv=(4, 256)) as (pj, av, cv):
                with memory(k, rows=(1024,), tab=(8,), bias_rows=(1024,)) as (rows, tab, bias_rows):
                    project(k, T1_TILES, pj, [(av, 256), (cv, 256)], first=split_start(k),
                            aside=distance_bias(k, bias_dram, rows, tab, bias_rows))
                mixers_ab(k, pj, av, bias_dram)
                mixer_c(k, pj, cv)
                mixer_d(k, pj, av, cv)
            merge(k, ALPHA, k.dram["xT"])
        par = lambda n, j: k.par1[:, P1[n] + j:P1[n] + j + 1]

        with memory(k, block_expert=("i", 2 * TURNS + 2), pos=(2, 4), pos_rows=(2, SEQ), gate_rows=(2, SEQ)) as (
                block_expert, pos, pos_rows, gate_rows):
            with memory(k, hot=(4, 32), hot2=(4, 32), gates=(2, 4)) as (hot, hot2, gates):
                with norm_buffers(k, mean=True) as buffers:
                    route(k, hot, hot2, gates, norm_programs(
                        k, k.res, lambda t: par("ln_g", t), lambda t: par("ln_b", t), k.eps[:, 0:1], True, buffers,
                        k.xh, k.xl, out=k.res))
                dispatch(k, (hot[:, :, :], hot2[:, :, :]), gates, block_expert[:, :], pos, pos_rows, gate_rows)
            scale_residual(k)
            experts(k, block_expert, pos, pos_rows, gate_rows)
        k.ws.skipped, k.ws.limit = EXPERTS * MOE_CHUNKS, None
        k.ws.plan(0)
        normalise(k, k.res, lambda t: par("ln_g", 8 + t), lambda t: par("ln_b", 8 + t), k.eps[:, 0:1], True,
                  out=k.res, stream=True)
        c0 = k.ws.blocks // 16
        with nc.Fori(0, LAYERS) as i:
            k.ws.turn = i * LAYER_CHUNKS
            layer(k, i, grid_dram)
            assert k.ws.blocks == 16 * (c0 + LAYER_CHUNKS)
        store_out(k, c0)




def fm_blocks(w):
    k, f = w.shape
    return w.reshape(k // 128, 128, f // 128, 128).transpose(2, 0, 1, 3).reshape(-1, 128, 128)


def tm_blocks(w):
    k, f = w.shape
    return w.reshape(k // 128, 128, f // 128, 128).transpose(0, 2, 1, 3).reshape(-1, 128, 128)


def merge_blocks(gate, branch):
    g = gate.reshape(8, 128, 4, 8, 128).transpose(3, 2, 0, 1, 4)
    b = branch.reshape(4, 2, 128, 8, 128).transpose(3, 0, 1, 2, 4)
    return np.concatenate([g, b], axis=2).reshape(-1, 128, 128)


def pair_blocks(a, b):
    x = fm_blocks(a).reshape(-1, 8, 128, 128)
    y = fm_blocks(b).reshape(-1, 8, 128, 128)
    return np.stack([x, y], axis=1).reshape(-1, 128, 128)


def weight_stream(v):
    w = v["w_in"][0]
    off = dict(aq=0, ak=256, av=512, bq=768, ckv=1024, iq=1088, ik=1344, iw=1376, cq=1384, ck=1512, cv=1640,
               ca=1896, cg=1912, dr=2168, dk=2424, dv=2680, dw=2936, da=2952, dg=2968, gate=3000)

    def cols(name, n):
        return w[:, off[name]:off[name] + n]

    low = np.zeros((D, 128), np.float32)
    low[:, 0:16] = cols("dw", 16)
    low[:, 32:48] = cols("da", 16)
    low[:, 64:96] = cols("dg", 32)
    low[:, 96:112] = cols("ca", 16)
    low[:, 112:120] = cols("iw", 8)
    router = np.zeros((D, 128), np.float32)
    router[:, 0:4] = v["router_g"][0]
    router[:, 4:36] = v["router_e"][0]
    fm = np.concatenate([cols("aq", 256), cols("ak", 256), cols("bq", 256), cols("iq", 256), cols("ckv", 64),
                         cols("ckv", 64)] + [cols("ik", 32)] * 4 + [low, cols("cq", 128), cols("ck", 128),
                         cols("cg", 256), cols("dr", 256), cols("dk", 256), cols("dv", 256)], axis=1)
    parts = [fm_blocks(fm), tm_blocks(cols("av", 256)), tm_blocks(cols("cv", 256)),
             merge_blocks(cols("gate", 4 * D), v["w_branch"][0]), fm_blocks(v["w_out"][0]), tm_blocks(router)]
    for e in range(EXPERTS):
        parts.append(tm_blocks(np.concatenate([v["moe_w_gate"][0, e], v["moe_w_up"][0, e]], axis=1)))
        parts.append(tm_blocks(v["moe_w_down"][0, e]))
    for l in range(LAYERS):
        w2 = v["w_in_2"][l]
        sec = [w2[:, 256 * n:256 * n + 256] for n in range(9)]
        rq, rk, rv, rg, pv, nq, nk, nv, mq = sec
        parts += [fm_blocks(np.concatenate([rq, rk, rg, pv, nq, nk, mq], axis=1)), tm_blocks(rv), tm_blocks(nv),
                  fm_blocks(v["w_mem_kv_2"][l][:, 0:256]), tm_blocks(v["w_mem_kv_2"][l][:, 256:512]),
                  merge_blocks(v["w_gate_2"][l], v["w_branch_2"][l]), fm_blocks(v["w_out_2"][l]),
                  pair_blocks(v["w_ffn_in_2"][l][:, 0:FF], v["w_ffn_in_2"][l][:, FF:2 * FF]),
                  fm_blocks(v["w_ffn_out_2"][l])]
    parts.append(np.zeros((16 * SPARE, 128, 128), np.float32))
    s = np.concatenate(parts, axis=0)
    assert s.shape[0] == 16 * (CHUNKS + SPARE)
    return np.ascontiguousarray(s.reshape(-1, 16, 128, 128).transpose(0, 2, 1, 3).reshape(-1, 128, CHUNK))


def t5_bucket(dist):
    exact = 16
    d = np.maximum(dist, 0)
    df = np.maximum(d, 1).astype(np.float32)
    large = exact + (np.log(df / np.float32(exact)) / np.float32(math.log(2048 / exact)) * np.float32(16)).astype(np.int32)
    return np.where(d < exact, d, np.minimum(large, 31))


def distance_rows():
    dist = 511 - np.arange(1024)
    r = np.zeros((34, 1024), np.float32)
    b = t5_bucket(dist)
    for y in range(1024):
        if dist[y] >= 0:
            r[b[y], y] = 1.0
    held = (dist <= 128).astype(int) + (dist % 4 == 0) + (dist % 16 == 0)
    held = np.where(dist >= 0, held, 0)
    r[32] = np.where(held > 0, np.log(np.maximum(held, 1)), MASKED)
    r[33] = np.where(dist >= 0, 0.0, MASKED)
    return r


def constants():
    c = np.zeros((128, CONSTS), np.float32)
    i, j = np.meshgrid(np.arange(128), np.arange(128), indexing="ij")

    def put(name, m):
        c[:, CONST[name]:CONST[name] + m.shape[1]] = m

    put("ident", (i == j))
    put("ones", np.ones((128, 128)))
    put("blk64", (i // 64 == j // 64))
    put("gla_mask", (i <= j) & (i // 64 == j // 64))
    put("up_same", (i < j) & (i // 16 == j // 16))
    put("up_other", (i < j) & (i // 16 != j // 16))
    put("low_same", (i > j) & (i // 16 == j // 16))
    put("up", (i < j))
    put("up_diag", (i <= j))
    put("future", np.where(j > i, MASKED, 0.0))
    a, b = np.meshgrid(np.arange(128), np.arange(256), indexing="ij")
    put("gla_heads", (a // 32 == b // 64))
    t = np.arange(512)[None, :] + np.zeros((128, 1))
    put("reset64", (t % 64 != 0))
    put("reset128", (t % 128 != 0))
    rot = np.where(j % 64 < 32, -1.0 * (i == j + 32), 1.0 * (i == j - 32))
    put("rotate", rot)
    put("rank8", np.tile(8.0 - np.arange(8), (128, 4)))
    put("count", np.tile(np.arange(256), (128, 1)))
    put("row", np.arange(128)[:, None] + np.array([[0, 128]]))
    return c


def layer_tables():
    half = 32
    inv = (np.float32(10000.0) ** (-np.arange(half, dtype=np.float32) / np.float32(half))).astype(np.float32)
    ang = (np.arange(SEQ, dtype=np.float32)[None, :] * inv[:, None]).astype(np.float32).astype(np.float64)
    cos, sin = (np.tile(f(ang), (4, 1)).astype(np.float32) for f in (np.cos, np.sin))
    p, x = np.meshgrid(np.arange(128), np.arange(STRIP), indexing="ij")
    ahead = np.maximum(x - 384 - p, 0).astype(np.float32)
    behind = np.maximum(384 + p - x, 0).astype(np.float32)
    t = np.arange(SEQ)
    counts = np.zeros((128, 2, SEQ), np.float32)
    for g in range(4):
        h = POOL_WINDOWS[g] // 2
        n = np.clip(t + h, 0, SEQ) - np.clip(t - h, 0, SEQ)
        counts[64 * (g % 2):64 * (g % 2) + 64, g // 2, :] = (1.0 / n)[None, :]
    return np.concatenate([cos, sin, ahead, behind, counts.reshape(128, -1)], axis=1)


def na_select():
    r = np.zeros((32, 64, 64), np.float32)
    for qc in range(64):
        lo = min(max(qc - 8, 0), 48)
        for kc in range(64):
            if lo <= kc < lo + 16:
                r[kc - qc + 15, qc, kc] = 1.0
            else:
                r[31, qc, kc] = MASKED
    return r.reshape(32, 4096)


def columns(*arrays):
    return np.concatenate([a.reshape(-1, 128).T for a in arrays], axis=1)


def device_arrays(v):
    f32 = np.float32
    a = {}
    a["xT"] = np.ascontiguousarray(v["x"][0].T.reshape(8, 128, SEQ).transpose(1, 0, 2))
    a["memT"] = np.ascontiguousarray(v["mem_2"][0].T.reshape(8, 128, 256).transpose(1, 0, 2))
    a["weights"] = weight_stream(v)
    a["consts"] = constants()
    a["tables"] = layer_tables()
    a["dist_rows"] = distance_rows()
    a["na_rows"] = na_select()
    tab = np.zeros((34, 8), f32)
    tab[0:32] = v["rpb_table"]
    tab[32, 0:4] = 1.0
    tab[33, 4:8] = 1.0
    a["rpb"] = tab
    mu = v["d_mu"][0]
    mu_low = np.zeros(128, f32)
    mu_low[0:16], mu_low[32:48], mu_low[64:96] = mu[768:784], mu[784:800], mu[800:832]
    dup = lambda z, n: np.tile(z, n)
    a["params1"] = np.ascontiguousarray(columns(
        v["ln_g"][0], v["ln_b"][0], dup(v["b_kv_gain"][0], 2), v["c_a_bias"][0], v["c_norm_gain"][0],
        mu[0:768], mu_low, v["d_w0"][0], v["d_a0"][0], v["d_k_k"][0], v["d_k_a"][0], v["d_r_k"][0],
        v["d_gn_w"][0], v["d_gn_b"][0]))
    low = np.zeros((128, 256), f32)
    low[0:16], low[32:48], low[64:96] = v["d_w2"][0], v["d_a2"][0], v["d_g2"][0]
    low[96:112, 0:128] = v["c_a_up"][0]
    uv = np.zeros((128, 256), f32)
    for h in range(4):
        r = 64 * (h % 2)
        uv[r:r + 64, 128 * (h // 2) + r:128 * (h // 2) + r + 64] = v["b_w_uv"][0, h]
    bias = np.concatenate([v["router_g_bias"][0], v["router_e_bias"][0]])
    a["mats1"] = np.concatenate([low, uv, np.tile(bias[None, :], (128, 1))], axis=1)
    p2, m2, rp = [], [], []
    for l in range(LAYERS):
        reps = np.concatenate([v["ret_decay_fwd_2"][l], v["ret_decay_bwd_2"][l]])
        p2.append(np.concatenate([columns(
            v["norm_mix_g_2"][l], v["norm_mem_g_2"][l], v["norm_ffn_g_2"][l], v["ret_norm_g_2"][l],
            v["pool_scale_2"][l], dup(v["na_q_norm_g_2"][l], 2), dup(v["na_k_norm_g_2"][l], 2),
            dup(v["mem_q_norm_g_2"][l], 2), dup(v["mem_k_norm_g_2"][l], 2)),
            np.tile(reps[None, :], (128, 1))], axis=1))
        pw = np.zeros((128, 256), f32)
        for g in range(4):
            r = 64 * (g % 2)
            pw[r:r + 64, 128 * (g // 2) + r:128 * (g // 2) + r + 64] = v["pool_w_2"][l, g]
        m2.append(pw)
        r = np.ones((32, 60), f32)
        r[0:31] = v["na_rpb_2"][l].reshape(60, 31).T
        rp.append(r)
    a["params2"] = np.stack(p2)
    a["mats2"] = np.stack(m2)
    a["na_rpb"] = np.stack(rp)
    return {k: np.ascontiguousarray(x) for k, x in a.items()}


def kernel(**inputs):
    import concourse.bacc as bacc
    from concourse.bass_utils import run_bass_kernel_spmd

    arrays = device_arrays({k: np.asarray(x) for k, x in inputs.items()})
    nc = bacc.Bacc("TRN2", target_bir_lowering=False, num_devices=1)
    dram = {k: nc.dram_tensor(k, x.shape, F32, kind="ExternalInput").ap() for k, x in arrays.items()}
    dram["outT"] = nc.dram_tensor("outT", (128, 8, SEQ), F32, kind="ExternalOutput").ap()
    build(nc, dram)
    r = run_bass_kernel_spmd(nc, [arrays], core_ids=[0])
    out = np.asarray(r.results[0]["outT"])
    return np.ascontiguousarray(out.transpose(2, 1, 0).reshape(1, SEQ, D))
```
